# Optimizing a Trainium2 kernel written in Bass

```python
import math
import jax, jax.numpy as jnp
from jax import lax
import numpy as np

D_MODEL = 1024
BATCH = 1
SEQ = 512
DEPTH = 1
DEC_BATCH = 1
DEC_SEQ = 1024
PAST_LEN = 128

GRID_W = 64
N_Q_HEADS = 16
N_KV_HEADS = 4
HEAD_DIM = 64
Q_BLOCK = 128
ROPE_THETA = 10000.0
AXIS_DIM = HEAD_DIM // 2
Q_WIDTH = N_Q_HEADS * HEAD_DIM
KV_WIDTH = N_KV_HEADS * HEAD_DIM
SSM_WIDTH = 512
SSM_GROUP = 16
N_SSM_GROUPS = SSM_WIDTH // SSM_GROUP
SSM_STATE = 64
N_DIRECTIONS = 2
STEP_MIN = 1e-3
STEP_MAX = 1e-1
D_FF = 4 * D_MODEL
EPS = 1e-6
IN_WIDTH = Q_WIDTH + 2 * KV_WIDTH + SSM_WIDTH + 2 * D_MODEL
SPLIT_POINTS = (
    Q_WIDTH,
    Q_WIDTH + KV_WIDTH,
    Q_WIDTH + 2 * KV_WIDTH,
    Q_WIDTH + 2 * KV_WIDTH + SSM_WIDTH,
    Q_WIDTH + 2 * KV_WIDTH + SSM_WIDTH + D_MODEL,
)

kernel_name = "hybrid_gated_s5_axial_gqa_encoder"

def rms_norm(x, gain):
    xf = x.astype(jnp.float32)
    xf = xf * lax.rsqrt(jnp.mean(xf * xf, axis=-1, keepdims=True) + EPS)
    return (xf * gain.astype(jnp.float32)).astype(x.dtype)

def axial_rope_tables(seq_len):
    rows = seq_len // GRID_W
    row_idx = jnp.broadcast_to(jnp.arange(rows)[:, None], (rows, GRID_W)).reshape(seq_len)
    col_idx = jnp.broadcast_to(jnp.arange(GRID_W)[None, :], (rows, GRID_W)).reshape(seq_len)
    inv_freq = ROPE_THETA ** (-jnp.arange(0, AXIS_DIM, 2, dtype=jnp.float32) / AXIS_DIM)
    ang_r = row_idx.astype(jnp.float32)[:, None] * inv_freq[None, :]
    ang_c = col_idx.astype(jnp.float32)[:, None] * inv_freq[None, :]
    ang = jnp.concatenate([ang_r, ang_c], axis=-1)
    return jnp.cos(ang), jnp.sin(ang)

def apply_axial_rope(x, cos, sin):
    xf = x.astype(jnp.float32).reshape(*x.shape[:-1], HEAD_DIM // 2, 2)
    x1, x2 = xf[..., 0], xf[..., 1]
    c = cos[:, None, :]
    s = sin[:, None, :]
    out = jnp.stack([x1 * c - x2 * s, x1 * s + x2 * c], axis=-1).reshape(x.shape)
    return out.astype(x.dtype)

def gqa_attention(q, k, v):
    b, l = q.shape[0], q.shape[1]
    rep = N_Q_HEADS // N_KV_HEADS
    n_blocks = l // Q_BLOCK
    qb = q.reshape(b, n_blocks, Q_BLOCK, N_KV_HEADS, rep, HEAD_DIM).transpose(1, 0, 2, 3, 4, 5)
    scale = HEAD_DIM ** -0.5

    def block(q_blk):
        s = jnp.einsum("bqgrd,bkgd->bgrqk", q_blk, k,
                       preferred_element_type=jnp.float32) * scale
        p = jax.nn.softmax(s, axis=-1)
        return jnp.einsum("bgrqk,bkgd->bqgrd", p.astype(v.dtype), v)

    o = lax.map(block, qb)
    return o.transpose(1, 0, 2, 3, 4, 5).reshape(b, l, Q_WIDTH)

def _linear_recurrence(e1, e2):
    a1, x1 = e1
    a2, x2 = e2
    return a1 * a2, a2 * x1 + x2

def s5_bidirectional(u, lam_re, lam_im, log_step, b_re, b_im, c_re, c_im, d_skip):
    bsz, l, _ = u.shape
    uf = u.astype(jnp.float32).reshape(bsz, l, N_SSM_GROUPS, SSM_GROUP)
    lam = lax.complex(lam_re.astype(jnp.float32), lam_im.astype(jnp.float32))
    step = jnp.exp(log_step.astype(jnp.float32))
    lam_bar = jnp.exp(lam * step[..., None])
    b = lax.complex(b_re.astype(jnp.float32), b_im.astype(jnp.float32))
    b_bar = ((lam_bar - 1.0) / lam)[..., None] * b
    c = lax.complex(c_re.astype(jnp.float32), c_im.astype(jnp.float32))

    def one_sequence(useq):
        ucx = useq.astype(jnp.complex64)
        outs = []
        for direction, rev in ((0, False), (1, True)):
            bu = jnp.einsum("gpc,lgc->lgp", b_bar[direction], ucx)
            a = jnp.broadcast_to(lam_bar[direction], bu.shape)
            _, h = lax.associative_scan(_linear_recurrence, (a, bu), reverse=rev, axis=0)
            outs.append(jnp.einsum("gcp,lgp->lgc", c[direction], h).real)
        return outs[0] + outs[1]

    y = lax.map(one_sequence, uf)
    y = y + d_skip.astype(jnp.float32).reshape(N_SSM_GROUPS, SSM_GROUP) * uf
    return y.reshape(bsz, l, SSM_WIDTH).astype(u.dtype)

def encoder_layer(x, cos, sin, norm_mix, w_in, q_norm, k_norm, w_attn_proj,
                  lam_re, lam_im, log_step, b_re, b_im, c_re, c_im, d_skip,
                  w_glu_a, w_glu_b, w_out, norm_mlp, w_ff1, w_ff2):
    bsz, l, _ = x.shape
    xn = rms_norm(x, norm_mix)
    proj = xn @ w_in
    q, k, v, u, g_attn, g_ssm = jnp.split(proj, SPLIT_POINTS, axis=-1)

    q = rms_norm(q.reshape(bsz, l, N_Q_HEADS, HEAD_DIM), q_norm)
    k = rms_norm(k.reshape(bsz, l, N_KV_HEADS, HEAD_DIM), k_norm)
    q = apply_axial_rope(q, cos, sin)
    k = apply_axial_rope(k, cos, sin)
    v = v.reshape(bsz, l, N_KV_HEADS, HEAD_DIM)
    attn_out = gqa_attention(q, k, v) @ w_attn_proj

    y = jax.nn.gelu(s5_bidirectional(u, lam_re, lam_im, log_step, b_re, b_im, c_re, c_im, d_skip))
    ssm_out = (y @ w_glu_a) * jax.nn.sigmoid(y @ w_glu_b)

    merged = jax.nn.sigmoid(g_attn) * attn_out + jax.nn.sigmoid(g_ssm) * ssm_out
    x = x + merged @ w_out

    h = rms_norm(x, norm_mlp)
    x = x + jnp.square(jax.nn.relu(h @ w_ff1)) @ w_ff2
    return x

def setup_inputs(seed: int = 0) -> dict:
    key = jax.random.key(seed)
    ks = jax.random.split(key, 24)
    f32 = jnp.float32

    def normal(k, shape, scale):
        return jax.random.normal(k, shape, f32) * scale

    n_idx = jnp.arange(SSM_STATE, dtype=f32)
    lam_shape = (DEPTH, N_DIRECTIONS, N_SSM_GROUPS, SSM_STATE)
    return {
        "x_prompt": jax.random.normal(ks[0], (BATCH, SEQ, D_MODEL), f32),
        "x_sample": jax.random.normal(ks[1], (DEC_BATCH, DEC_SEQ, D_MODEL), f32),
        "norm_mix": 1.0 + normal(ks[2], (DEPTH, D_MODEL), 0.02),
        "w_in": normal(ks[3], (DEPTH, D_MODEL, IN_WIDTH), D_MODEL ** -0.5),
        "q_norm": 1.0 + normal(ks[4], (DEPTH, HEAD_DIM), 0.02),
        "k_norm": 1.0 + normal(ks[5], (DEPTH, HEAD_DIM), 0.02),
        "w_attn_proj": normal(ks[6], (DEPTH, Q_WIDTH, D_MODEL), Q_WIDTH ** -0.5),
        "ssm_lambda_re": -0.5 + normal(ks[7], lam_shape, 0.01),
        "ssm_lambda_im": math.pi * n_idx + normal(ks[8], lam_shape, 0.01),
        "ssm_log_step": jax.random.uniform(ks[9], (DEPTH, N_DIRECTIONS, N_SSM_GROUPS), f32,
                                           math.log(STEP_MIN), math.log(STEP_MAX)),
        "ssm_b_re": normal(ks[10], (DEPTH, N_DIRECTIONS, N_SSM_GROUPS, SSM_STATE, SSM_GROUP), SSM_GROUP ** -0.5),
        "ssm_b_im": normal(ks[11], (DEPTH, N_DIRECTIONS, N_SSM_GROUPS, SSM_STATE, SSM_GROUP), SSM_GROUP ** -0.5),
        "ssm_c_re": normal(ks[12], (DEPTH, N_DIRECTIONS, N_SSM_GROUPS, SSM_GROUP, SSM_STATE), SSM_STATE ** -0.5),
        "ssm_c_im": normal(ks[13], (DEPTH, N_DIRECTIONS, N_SSM_GROUPS, SSM_GROUP, SSM_STATE), SSM_STATE ** -0.5),
        "ssm_d": normal(ks[14], (DEPTH, SSM_WIDTH), 1.0),
        "w_glu_a": normal(ks[15], (DEPTH, SSM_WIDTH, D_MODEL), SSM_WIDTH ** -0.5),
        "w_glu_b": normal(ks[16], (DEPTH, SSM_WIDTH, D_MODEL), SSM_WIDTH ** -0.5),
        "w_out": normal(ks[17], (DEPTH, D_MODEL, D_MODEL), D_MODEL ** -0.5),
        "norm_mlp": 1.0 + normal(ks[18], (DEPTH, D_MODEL), 0.02),
        "w_ff1": normal(ks[19], (DEPTH, D_MODEL, D_FF), D_MODEL ** -0.5),
        "w_ff2": normal(ks[20], (DEPTH, D_FF, D_MODEL), D_FF ** -0.5),
    }

def reference(x_prompt, x_sample, norm_mix, w_in, q_norm, k_norm, w_attn_proj,
              ssm_lambda_re, ssm_lambda_im, ssm_log_step, ssm_b_re, ssm_b_im,
              ssm_c_re, ssm_c_im, ssm_d, w_glu_a, w_glu_b, w_out, norm_mlp, w_ff1, w_ff2):
    def trunk(x):
        cos, sin = axial_rope_tables(x.shape[1])
        for i in range(DEPTH):
            x = encoder_layer(
                x, cos, sin, norm_mix[i], w_in[i], q_norm[i], k_norm[i], w_attn_proj[i],
                ssm_lambda_re[i], ssm_lambda_im[i], ssm_log_step[i], ssm_b_re[i], ssm_b_im[i],
                ssm_c_re[i], ssm_c_im[i], ssm_d[i], w_glu_a[i], w_glu_b[i], w_out[i],
                norm_mlp[i], w_ff1[i], w_ff2[i])
        return x

    y_prompt = trunk(x_prompt)
    y_sample = trunk(x_sample)
    return (y_prompt, y_sample)


_drawn_inputs = setup_inputs


def setup_inputs(seed=0):
    import zlib

    import numpy as np

    out = dict(_drawn_inputs(seed))
    spreads = {}
    factors = {'norm_mix': 8.0, 'q_norm': 8.0, 'k_norm': 8.0, 'ssm_lambda_re': 8.0, 'norm_mlp': 3.251}
    for name, (base, spread) in spreads.items():
        noise = np.random.default_rng([zlib.crc32(name.encode()), seed]).standard_normal(out[name].shape)
        drawn = base * np.exp(spread * noise) if base else spread * noise
        out[name] = __import__('jax').numpy.asarray(drawn.astype(out[name].dtype))
    for name, factor in factors.items():
        out[name] = (out[name] * factor).astype(out[name].dtype)
    return out
```

```python
import math
from contextlib import ExitStack

import numpy as np

import concourse.bass as bass
from concourse import mybir

ALU = mybir.AluOpType
ACT = mybir.ActivationFunctionType
AX = mybir.AxisListType
F32 = mybir.dt.float32
F32R = mybir.dt.float32r

P = 128
D_MODEL = 1024
D_FF = 4096
HEAD = 64
NQ, NKV = 16, 4
LEN_A, LEN_B = 512, 1024
TOK = LEN_A + LEN_B
BLK = 512
NBLK = TOK // BLK
KD = D_MODEL // P
EPS = 1e-6
GRID_W = 64
ROPE_THETA = 10000.0
CHUNK = 8
GROUPS, GC, STATE = 32, 16, 64
LN_EXP = "natural_log_exp_and_others"

Q_T, K_T, V_T, U_T, GA_T, GS_T = 0, 8, 10, 12, 16, 24
PROJ_T = 32


def f32(ap):
    return ap.bitcast(F32)


def alone(eng, turn):
    eng.sem_inc(turn, 1)


def three_products(pe, out, whi, wlo, xhi, xlo, start, stop):
    pe.matmul(out, whi, xhi, start=start, stop=False)
    pe.matmul(out, whi, xlo, start=False, stop=False)
    return pe.matmul(out, wlo, xhi, start=False, stop=stop)


def project(nc, x_t, w_in, gain, ones_d, proj):
    with ExitStack() as ctx:
        sb = lambda name, shape, dt=F32: ctx.enter_context(nc.sbuf_tensor(name, shape, dt))
        sem = lambda name: ctx.enter_context(nc.semaphore(name))
        x = sb("p1_x", [P, NBLK, KD, BLK])
        x_hi = sb("p1_xhi", [P, NBLK, KD, BLK], F32R)
        x_lo = sb("p1_xlo", [P, NBLK, KD, BLK], F32R)
        sq = sb("p1_sq", [P, 2, BLK])
        rs = sb("p1_rs", [P, TOK])
        g = sb("p1_gain", [P, KD])
        eps = sb("p1_eps", [P, 1])
        ones = sb("p1_ones", [P, P])
        w_raw = [sb(f"p1_wraw{s}", [P, KD, P]) for s in range(2)]
        w_hi = [sb(f"p1_whi{s}", [P, KD, P], F32R) for s in range(2)]
        w_lo = [sb(f"p1_wlo{s}", [P, KD, P], F32R) for s in range(2)]
        stage = [sb(f"p1_stage{s}", [P, TOK]) for s in range(2)]
        acc = ctx.enter_context(nc.psum_tensor("p1_acc", [P, 6, BLK], F32))
        mean = ctx.enter_context(nc.psum_tensor("p1_mean", [P, 2, BLK], F32))

        const_in = sem("p1_const_in")
        x_in = [sem(f"p1_x_in{b}") for b in range(NBLK)]
        w_in_s = [sem(f"p1_w_in{s}") for s in range(2)]
        eps_set = sem("p1_eps_set")
        sq_ready = sem("p1_sq_ready")
        sq_used = sem("p1_sq_used")
        ln_done = sem("p1_ln_done")
        rs_ready = sem("p1_rs_ready")
        xhi_ready = sem("p1_xhi_ready")
        xlo_ready = sem("p1_xlo_ready")
        whi_ready = sem("p1_whi_ready")
        wlo_ready = sem("p1_wlo_ready")
        summed = sem("p1_summed")
        evicted = sem("p1_evicted")
        stored = [sem(f"p1_stored{s}") for s in range(2)]

        with nc.Block() as block:

            @block.sync
            def _(sp):
                def load_w(m, s):
                    sp.dma_start(w_raw[s][:], w_in[m]).then_inc(w_in_s[s], 16)

                for s in range(2):
                    sp.sem_inc(stored[s], 16)
                sp.dma_start(g[:], gain).then_inc(const_in, 16)
                sp.dma_start(ones[:], ones_d).then_inc(const_in, 16)
                sp.dma_start(x[:, 0], x_t[0]).then_inc(x_in[0], 16)
                load_w(0, 0)
                load_w(1, 1)
                for b in range(1, NBLK):
                    sp.dma_start(x[:, b], x_t[b]).then_inc(x_in[b], 16)

                def pair(i, more):
                    for s in range(2):
                        if more:
                            sp.wait_ge(wlo_ready, 2 * i + s + 3)
                            load_w(2 * i + s + 2, s)
                        sp.wait_ge(evicted, 6 + 3 * (2 * i + s + 1))
                        sp.dma_start(proj[2 * i + s], stage[s][:]).then_inc(stored[s], 16)

                with sp.Fori(0, PROJ_T // 2 - 1) as i:
                    pair(i, True)
                pair(PROJ_T // 2 - 1, False)
                for s in range(2):
                    sp.wait_ge(stored[s], 16 * (PROJ_T // 2) + 16)

            @block.scalar
            def _(act):
                act.preload_act_table_set(LN_EXP)
                act.wait_ge(const_in, 32)
                act.wait_ge(eps_set, 1)
                for b in range(NBLK):
                    act.wait_ge(x_in[b], 16)
                    for k in range(KD):
                        act.activation(x_hi[:, b, k], x[:, b, k], ACT.Identity,
                                       scale=g[:, k:k + 1]).then_inc(xhi_ready, 1)
                        act.wait_ge(sq_used, b * KD + k + 1)
                        act.activation(sq[:, k % 2], x[:, b, k], ACT.Square).then_inc(sq_ready, 1)
                    if b < 2:
                        act.wait_ge(w_in_s[b], 16)
                        act.activation(w_hi[b][:], w_raw[b][:], ACT.Copy).then_inc(whi_ready, 1)
                    act.wait_ge(sq_used, 2 + (b + 1) * KD)
                    act.activation(rs[:, b * BLK:(b + 1) * BLK], mean[:, b % 2], ACT.Ln,
                                   bias=eps[:, 0:1]).then_inc(ln_done, 1)
                    act.wait_ge(ln_done, b + 1)
                    act.activation(rs[:, b * BLK:(b + 1) * BLK], rs[:, b * BLK:(b + 1) * BLK],
                                   ACT.Exp, scale=-0.5).then_inc(rs_ready, 1)
                with act.Fori(1, PROJ_T // 2) as i:
                    for s in range(2):
                        act.wait_ge(w_in_s[s], 16 * i + 16)
                        act.wait_ge(summed, 6 + 3 * (2 * i + s - 1))
                        act.activation(w_hi[s][:], w_raw[s][:], ACT.Copy).then_inc(whi_ready, 1)

            @block.vector
            def _(dve):
                dve.memset(eps[:], EPS).then_inc(eps_set, 1)
                dve.sem_inc(wlo_ready, 2)
                dve.sem_inc(evicted, 6)

                def low(m, s):
                    dve.wait_ge(whi_ready, m + 1)
                    dve.tensor_tensor(w_lo[s][:], w_raw[s][:], f32(w_hi[s][:]),
                                      ALU.subtract).then_inc(wlo_ready, 1)

                def evict(m, i, s, b):
                    dve.wait_ge(summed, 6 + 3 * m + b + 1)
                    if b == 0:
                        dve.wait_ge(stored[s], 16 * i + 16)
                    dve.tensor_tensor(stage[s][:, b * BLK:(b + 1) * BLK], acc[:, 3 * s + b],
                                      rs[:, b * BLK:(b + 1) * BLK], ALU.mult).then_inc(evicted, 1)

                dve.wait_ge(const_in, 32)
                for b in range(NBLK):
                    for k in range(KD):
                        dve.wait_ge(xhi_ready, b * KD + k + 1)
                        dve.scalar_tensor_tensor(x_lo[:, b, k], x[:, b, k], g[:, k:k + 1],
                                                 f32(x_hi[:, b, k]), ALU.mult,
                                                 ALU.subtract).then_inc(xlo_ready, 1)
                    if b == 0:
                        low(0, 0)
                dve.wait_ge(rs_ready, NBLK)

                def pair(i, more):
                    for s in range(2):
                        m = 2 * i + s
                        if s == 0 or more:
                            if s == 1:
                                dve.wait_ge(w_in_s[0], 16 * i + 32)
                            else:
                                dve.wait_ge(w_in_s[1], 16 * i + 16)
                            dve.wait_ge(summed, 3 * m + 6)
                            low(m + 1, 1 - s)
                        for b in range(NBLK):
                            evict(m, i, s, b)

                with dve.Fori(0, PROJ_T // 2 - 1) as i:
                    pair(i, True)
                pair(PROJ_T // 2 - 1, False)

            @block.tensor
            def _(pe):
                pe.sem_inc(sq_used, 2)
                pe.sem_inc(summed, 6)
                pe.wait_ge(const_in, 32)
                for b in range(NBLK):
                    if b == 2:
                        pe.wait_ge(ln_done, 1)
                    for k in range(KD):
                        pe.wait_ge(sq_ready, b * KD + k + 1)
                        pe.matmul(mean[:, b % 2], ones[:], sq[:, k % 2], start=(k == 0),
                                  stop=(k == KD - 1)).then_inc(sq_used, 1)
                with pe.Fori(0, PROJ_T // 2) as i:
                    for s in range(2):
                        m = 2 * i + s
                        pe.wait_ge(whi_ready, m + 1)
                        pe.wait_ge(wlo_ready, m + 3)
                        for b in range(NBLK):
                            pe.wait_ge(xlo_ready, KD * (b + 1))
                            pe.wait_ge(evicted, 3 * m + b + 1)
                            for k in range(KD):
                                mm = three_products(pe, acc[:, 3 * s + b], w_hi[s][:, k], w_lo[s][:, k],
                                                    x_hi[:, b, k], x_lo[:, b, k], k == 0, k == KD - 1)
                            mm.then_inc(summed, 1)


SWAP = [i ^ 1 for i in range(32)]


def rope_prep(nc, proj, gains_d, head_mean_d, tables_d, roped):
    with ExitStack() as ctx:
        sb = lambda name, shape, dt=F32: ctx.enter_context(nc.sbuf_tensor(name, shape, dt))
        sem = lambda name: ctx.enter_context(nc.semaphore(name))
        two = lambda name, dt=F32: [sb(f"r_{name}{s}", [P, TOK], dt) for s in range(2)]
        raw, sq, rs, qn, sw = (two(n) for n in ("raw", "sq", "rs", "qn", "sw"))
        hi, lo = two("hi", F32R), two("lo", F32R)
        table = sb("r_table", [P, 2, TOK])
        gains = sb("r_gains", [P, 2])
        hmean = sb("r_hmean", [P, P])
        eps = sb("r_eps", [P, 1])
        ps = ctx.enter_context(nc.psum_tensor("r_ps", [P, 2, 4, BLK], F32))
        NT = V_T

        const_in = sem("r_const_in")
        eps_set = sem("r_eps_set")
        dve_turn = sem("r_dve_turn")
        raw_in = [sem(f"r_raw_in{s}") for s in range(2)]
        out_done = [sem(f"r_out_done{s}") for s in range(2)]
        sq_ready = sem("r_sq_ready")
        mean_ready = sem("r_mean_ready")
        ln_done = sem("r_ln_done")
        rs_ready = sem("r_rs_ready")
        qn_ready = sem("r_qn_ready")
        sw_ready = sem("r_sw_ready")
        cos_ready = sem("r_cos_ready")
        sin_ready = sem("r_sin_ready")
        sum_ready = sem("r_sum_ready")
        hi_ready = sem("r_hi_ready")
        lo_ready = sem("r_lo_ready")

        with nc.Block() as block:

            @block.sync
            def _(sp):
                for s in range(2):
                    sp.sem_inc(out_done[s], 16)
                sp.dma_start(gains[:], gains_d).then_inc(const_in, 16)
                sp.dma_start(hmean[:], head_mean_d).then_inc(const_in, 16)
                sp.dma_start(table[:], tables_d).then_inc(const_in, 16)
                for s in range(2):
                    sp.dma_start(raw[s][:], proj[s]).then_inc(raw_in[s], 16)

                def pair(i, more):
                    for s in range(2):
                        t = 2 * i + s
                        if more:
                            sp.wait_ge(qn_ready, t + 2)
                            sp.dma_start(raw[s][:], proj[t + 2]).then_inc(raw_in[s], 16)
                        sp.wait_ge(lo_ready, t + 2)
                        for l, part in enumerate((hi, lo)):
                            sp.dma_start(roped[l].rearrange("(t h) d n -> t (h d) n", h=2)[t],
                                         f32(part[s][:])).then_inc(out_done[s], 16)

                with sp.Fori(0, NT // 2 - 1) as i:
                    pair(i, True)
                pair(NT // 2 - 1, False)
                for s in range(2):
                    sp.wait_ge(out_done[s], NT * 16 + 16)

            @block.scalar
            def _(act):
                act.preload_act_table_set(LN_EXP)
                act.sem_inc(rs_ready, 1)
                act.wait_ge(eps_set, 1)
                with act.Fori(0, NT // 2) as i:
                    for s in range(2):
                        t = 2 * i + s
                        act.wait_ge(raw_in[s], 16 * i + 16)
                        act.wait_ge(mean_ready, 2 * i + (s + 1))
                        act.activation(sq[s][:], raw[s][:], ACT.Square).then_inc(sq_ready, 1)
                        act.wait_ge(mean_ready, t + 2)
                        act.wait_ge(qn_ready, 2 * i + (s + 1))
                        act.activation(rs[s][:].rearrange("p (b n) -> p b n", b=NBLK), ps[:, s, 0:NBLK],
                                       ACT.Ln, bias=eps[:, 0:1]).then_inc(ln_done, 1)
                        act.wait_ge(ln_done, t + 1)
                        act.activation(rs[s][:], rs[s][:], ACT.Exp, scale=-0.5).then_inc(rs_ready, 1)
                        act.wait_ge(sum_ready, t + 1)
                        act.wait_ge(out_done[s], 32 * i + 16)
                        act.activation(hi[s][:], qn[s][:], ACT.Copy).then_inc(hi_ready, 1)

            @block.gpsimd
            def _(pool):
                pool.wait_ge(const_in, 48)
                with pool.Fori(0, NT // 2) as i:
                    for s in range(2):
                        t = 2 * i + s
                        pool.wait_ge(sw_ready, t + 1)
                        pool.tensor_tensor(sw[s][:], sw[s][:], table[:, 1], ALU.mult).then_inc(sin_ready, 1)

            @block.vector
            def _(dve):
                dve.memset(eps[:], EPS).then_inc(eps_set, 1)
                for sem_ in (qn_ready, lo_ready):
                    dve.sem_inc(sem_, 1)
                dve.wait_ge(const_in, 48)

                def pair(i, kind):
                    for s in range(2):
                        t = 2 * i + s
                        dve.wait_ge(rs_ready, t + 2)
                        dve.wait_ge(lo_ready, 2 * i + (s + 1))
                        dve.scalar_tensor_tensor(qn[s][:], raw[s][:], gains[:, kind:kind + 1], rs[s][:],
                                                 ALU.mult, ALU.mult).then_inc(qn_ready, 1)
                        dve.wait_ge(qn_ready, t + 2)
                        alone(dve, dve_turn)
                        dve.stream_shuffle(sw[s][:], qn[s][:], SWAP).then_inc(sw_ready, 1)
                        dve.wait_ge(sw_ready, t + 1)
                        dve.tensor_tensor(qn[s][:], qn[s][:], table[:, 0], ALU.mult).then_inc(cos_ready, 1)
                        dve.wait_ge(cos_ready, t + 1)
                        dve.wait_ge(sin_ready, t + 1)
                        dve.tensor_tensor(qn[s][:], qn[s][:], sw[s][:], ALU.add).then_inc(sum_ready, 1)
                        dve.wait_ge(hi_ready, t + 1)
                        dve.tensor_tensor(lo[s][:], qn[s][:], f32(hi[s][:]), ALU.subtract).then_inc(lo_ready, 1)

                with dve.Fori(0, K_T // 2) as i:
                    pair(i, 0)
                pair(K_T // 2, 1)

            @block.tensor
            def _(pe):
                pe.sem_inc(mean_ready, 1)
                pe.wait_ge(const_in, 48)
                with pe.Fori(0, NT // 2) as i:
                    for s in range(2):
                        pe.wait_ge(sq_ready, 2 * i + (s + 1))
                        pe.wait_ge(rs_ready, 2 * i + (s + 1))
                        for b in range(NBLK):
                            mm = pe.matmul(ps[:, s, b], hmean[:], sq[s][:, b * BLK:(b + 1) * BLK],
                                           start=True, stop=True)
                        mm.then_inc(mean_ready, 1)


CH_A, CH_B = LEN_A // CHUNK, LEN_B // CHUNK
NCH = CH_A + CH_B
HALF = GROUPS // 2
BATCH = 4
TWO_PI = 2 * math.pi
C1 = 6.28125
C2 = float(np.float32(TWO_PI - C1).view(np.uint32) & np.uint32(0xfffff000)) * 0 + float(
    (np.float32(TWO_PI - C1).view(np.uint32) & np.uint32(0xfffff000)).view(np.float32))
C3 = TWO_PI - C1 - C2
ROUND = 1.5 * 2.0 ** 23


def state_space(nc, proj, lam_d, step_d, b_d, c_d, d_d, sign_d, ident_d, mix):
    with ExitStack() as ctx:
        sb = lambda name, shape, dt=F32: ctx.enter_context(nc.sbuf_tensor(name, shape, dt))
        sem = lambda name: ctx.enter_context(nc.semaphore(name))
        G = GROUPS
        lam = sb("s_lam", [P, 2, G])
        lstep = sb("s_lstep", [P, G])
        bb_in = sb("s_b", [P, 2, G, GC])
        cc = sb("s_c", [P, 2, G, GC])
        dd = sb("s_d", [GC, G])
        sign = sb("s_sign", [P, 1])
        ident = sb("s_ident", [P, P])
        half_pi = sb("s_half_pi", [P, 1])
        z = sb("s_z", [P, 2, G])
        tmp = sb("s_tmp", [P, 4, G])
        ang = sb("s_ang", [P, 2, G])
        mag = sb("s_mag", [P, G])
        ratio = sb("s_ratio", [P, G])
        unit = sb("s_unit", [P, 4, 2, G])
        pw = sb("s_pw", [P, 9, 2, G])
        turn = sb("s_turn", [P, 7, 2, G])
        fac = sb("s_fac", [P, 2, G])
        wf = sb("s_wf", [P, 2, G])
        p_lag = sb("s_plag", [P, 8, 2, G])
        p_in = sb("s_pin", [P, 8, 2, G])
        bbar = sb("s_bbar", [P, 2, G, GC])
        bw = sb("s_bw", [P, 2, G, GC])
        diag = sb("s_diag", [GC, G, GC])
        cneg = sb("s_cneg", [P, G, GC])
        out_w = sb("s_outw", [P, 2, HALF, 8, GC])
        in_t = sb("s_int", [P, 2, HALF, 8, GC])
        scratch = [sb(f"s_scratch{i}", [P, HALF * 8 * GC]) for i in range(2)]
        wide = [t[:].rearrange("p (g l c) -> p g l c", g=HALF, l=8) for t in scratch]
        tb = [t[:, 0:G * GC].rearrange("p (g c) -> p g c", g=G) for t in scratch]
        gin = [t[:, 0:BATCH * NCH] for t in scratch]
        gt = [t[:, 1024:1024 + BATCH * NCH] for t in scratch]
        in_w = sb("s_inw", [P, 2, HALF, P])
        resp = sb("s_resp", [GC, HALF, 15, GC])
        local = sb("s_local", [P, HALF, P])
        rot = sb("s_rot", [P, 2, HALF, NCH])
        rt = [sb(f"s_rt{i}", [P, HALF, CH_B // 2]) for i in range(2)]
        decay = sb("s_decay", [P, HALF, NCH])
        u = sb("s_u", [P, HALF, NCH])
        y = sb("s_y", [P, HALF, NCH])
        gs = [sb(f"s_gs{i}", [P, BATCH * NCH + 2]) for i in range(2)]
        hs = [[sb(f"s_h{i}{s}", [P, BATCH, NCH]) for i in range(2)] for s in range(2)]
        ps = ctx.enter_context(nc.psum_tensor("s_ps", [P, 8, BLK], F32))
        S_BANK, Y_BANK, W_BANK = 0, 4, 6

        par_in = sem("s_par_in")
        u_in = [sem(f"s_u_in{h}") for h in range(2)]
        local_in = [sem(f"s_local_in{h}") for h in range(2)]
        y_out = [sem(f"s_y_out{h}") for h in range(2)]
        a_done = sem("s_a_done")
        d_done = sem("s_d_done")
        g_done = sem("s_g_done")
        t_done = sem("s_t_done")
        r_done = sem("s_r_done")
        s_done = sem("s_s_done")
        y_done = sem("s_y_done")
        t_read = sem("s_t_read")
        r_read = sem("s_r_read")
        s_read = sem("s_s_read")
        h_ready = sem("s_h_ready")
        y_ready = sem("s_y_ready")
        angle_ready = sem("s_angle_ready")
        polar_ready = sem("s_polar_ready")
        turn_ready = sem("s_turn_ready")
        in_ready = sem("s_in_ready")
        rot_ready = sem("s_rot_ready")
        half_done = sem("s_half_done")
        resp_ready = sem("s_resp_ready")
        NB = HALF // BATCH

        with nc.Block() as block:

            @block.sync
            def _(sp):
                for dst, src in ((lam, lam_d), (lstep, step_d), (bb_in, b_d), (cc, c_d), (dd, d_d),
                                 (sign, sign_d), (ident, ident_d)):
                    sp.dma_start(dst[:], src).then_inc(par_in, 16)
                seqs = ((0, 0, CH_A), (LEN_A, CH_A, CH_B))
                u_src = proj[U_T:U_T + 4].rearrange("t p n -> (t p) n").rearrange("(g c) n -> c g n", c=GC)
                y_dst = mix[8:12].rearrange("t p n -> (t p) n").rearrange("(g c) n -> c g n", c=GC)
                for h in range(2):
                    gsl = slice(h * HALF, (h + 1) * HALF)
                    if h:
                        sp.wait_ge(y_done, NB)
                    for t in range(CHUNK):
                        for pos, k0, n in seqs:
                            sp.dma_start(u[t * GC:(t + 1) * GC, :, k0:k0 + n],
                                         u_src[:, gsl, pos + t * n:pos + (t + 1) * n]).then_inc(u_in[h], 16)
                    sp.wait_ge(resp_ready, h + 1)
                    for s in range(CHUNK):
                        sp.dma_start(local[s * GC:(s + 1) * GC],
                                     resp[:, :, 7 - s:15 - s].rearrange("p g l c -> p g (l c)")
                                     ).then_inc(local_in[h], 16)
                    sp.wait_ge(y_ready, NB * (h + 1))
                    for t in range(CHUNK):
                        for pos, k0, n in seqs:
                            sp.dma_start(y_dst[:, gsl, pos + t * n:pos + (t + 1) * n],
                                         y[t * GC:(t + 1) * GC, :, k0:k0 + n]).then_inc(y_out[h], 16)
                for h in range(2):
                    sp.wait_ge(y_out[h], 16 * 2 * CHUNK)

            @block.scalar
            def _(act):
                act.wait_ge(par_in, 16 * 7)
                act.activation(lstep[:], lstep[:], ACT.Exp).then_inc(a_done, 1)
                act.wait_ge(angle_ready, 1)
                act.activation(mag[:], z[:, 0], ACT.Exp).then_inc(polar_ready, 1)
                act.activation(ratio[:], z[:, 0], ACT.Exp, scale=float(CHUNK)).then_inc(polar_ready, 1)
                act.activation(unit[:, 0, 1], ang[:, 0], ACT.Sin).then_inc(polar_ready, 1)
                act.activation(unit[:, 0, 0], ang[:, 1], ACT.Sin, scale=-1.0,
                               bias=half_pi[:, 0:1]).then_inc(polar_ready, 1)
                for h in range(2):
                    if h:
                        act.wait_ge(s_done, NB)
                    for i in range(2 * HALF // 4):
                        act.wait_ge(t_done, h * (2 * HALF // 4) + i + 1)
                        j, g0 = divmod(4 * i, HALF)
                        act.activation(in_w[:, j, g0:g0 + 4],
                                       ps[:, W_BANK + i % 2].rearrange("p (g c) -> p g c", g=4),
                                       ACT.Copy).then_inc(t_read, 1)
                    if h:
                        act.wait_ge(y_out[0], 16 * 2 * CHUNK)
                    for b in range(NB):
                        act.wait_ge(y_done, h * NB + b + 1)
                        act.activation(y[:, b * BATCH:(b + 1) * BATCH].rearrange("p (b g) k -> p b g k", b=2),
                                       ps[:, Y_BANK:Y_BANK + 2, 0:2 * NCH].rearrange("p b (g k) -> p b g k", g=2),
                                       ACT.Gelu_apprx_tanh).then_inc(y_ready, 1)

            @block.gpsimd
            def _(pool):
                n_link = [0]

                def link(ins):
                    n_link[0] += 1
                    ins.then_inc(g_done, 1)
                    pool.wait_ge(g_done, n_link[0])

                for h in range(2):
                    gsl = slice(h * HALF, (h + 1) * HALF)
                    if h:
                        pool.wait_ge(half_done, 1)
                    pool.wait_ge(turn_ready, 1)
                    re, im = rot[:, 0, :, CH_A:], rot[:, 1, :, CH_A:]
                    link(pool.memset(re[:, :, 0:1], 1.0))
                    link(pool.memset(im[:, :, 0:1], 0.0))
                    for j in range(7):
                        n = 1 << j
                        t_re, t_im = (turn[:, j, x, gsl].unsqueeze(2).broadcast_to([P, HALF, n]) for x in range(2))
                        a, b = rt[0][:, :, 0:n], rt[1][:, :, 0:n]
                        link(pool.tensor_tensor(a, re[:, :, 0:n], t_re, ALU.mult))
                        link(pool.tensor_tensor(b, im[:, :, 0:n], t_im, ALU.mult))
                        link(pool.tensor_tensor(re[:, :, n:2 * n], a, b, ALU.subtract))
                        link(pool.tensor_tensor(a, re[:, :, 0:n], t_im, ALU.mult))
                        link(pool.tensor_tensor(b, im[:, :, 0:n], t_re, ALU.mult))
                        link(pool.tensor_tensor(im[:, :, n:2 * n], a, b, ALU.add))
                    link(pool.tensor_copy(rot[:, :, :, 0:CH_A], rot[:, :, :, CH_A:2 * CH_A]))
                    link(pool.tensor_copy(decay[:], ratio[:, gsl].unsqueeze(2).broadcast_to([P, HALF, NCH])))
                    link(pool.memset(decay[0:64, :, 0:1], 0.0))
                    link(pool.memset(decay[0:64, :, CH_A:CH_A + 1], 0.0))
                    link(pool.memset(decay[64:128, :, CH_A - 1:CH_A], 0.0))
                    pool.memset(decay[64:128, :, NCH - 1:NCH], 0.0).then_inc(rot_ready, 1)

            @block.vector
            def _(dve):
                n_link = [0]

                def link(ins):
                    n_link[0] += 1
                    ins.then_inc(d_done, 1)
                    dve.wait_ge(d_done, n_link[0])

                def tt(out, a, b, op):
                    link(dve.tensor_tensor(out, a, b, op))

                def cmul(out, a, b, t):
                    tt(t[0], a[0], b[0], ALU.mult)
                    tt(t[1], a[1], b[1], ALU.mult)
                    tt(t[2], a[0], b[1], ALU.mult)
                    tt(t[3], a[1], b[0], ALU.mult)
                    tt(out[0], t[0], t[1], ALU.subtract)
                    tt(out[1], t[2], t[3], ALU.add)

                T4 = [tmp[:, i] for i in range(4)]
                pair = lambda t: (t[:, 0], t[:, 1])
                link(dve.memset(half_pi[:], math.pi / 2))
                dve.wait_ge(par_in, 16 * 7)
                dve.wait_ge(a_done, 1)
                for i in range(2):
                    tt(z[:, i], lam[:, i], lstep[:], ALU.mult)
                link(dve.tensor_scalar(T4[0], z[:, 1], 1 / TWO_PI, ROUND, ALU.mult, ALU.add))
                link(dve.tensor_scalar(T4[0], T4[0], -ROUND, None, ALU.add))
                link(dve.scalar_tensor_tensor(ang[:, 0], T4[0], -C1, z[:, 1], ALU.mult, ALU.add))
                link(dve.scalar_tensor_tensor(ang[:, 0], T4[0], -C2, ang[:, 0], ALU.mult, ALU.add))
                link(dve.scalar_tensor_tensor(ang[:, 0], T4[0], -C3, ang[:, 0], ALU.mult, ALU.add))
                link(dve.tensor_scalar(ang[:, 0], ang[:, 0], 3.1415925, -3.1415925, ALU.min, ALU.max))
                dve.scalar_tensor_tensor(ang[:, 1], ang[:, 0], -1.0, ang[:, 0], ALU.mult,
                                         ALU.max).then_inc(angle_ready, 1)
                dve.wait_ge(polar_ready, 4)
                one, lb = (pw[:, 0, 0], pw[:, 0, 1]), (pw[:, 1, 0], pw[:, 1, 1])
                link(dve.memset(one[0], 1.0))
                link(dve.memset(one[1], 0.0))
                for i in range(2):
                    tt(lb[i], unit[:, 0, i], mag[:], ALU.mult)
                for lo, n in ((1, 1), (1, 2), (1, 4)):
                    for j in range(n):
                        cmul(pair(pw[:, n + 1 + j]), pair(pw[:, lo + j]), pair(pw[:, n]), T4)
                for i in range(3):
                    cmul(pair(unit[:, i + 1]), pair(unit[:, i]), pair(unit[:, i]), T4)
                link(dve.tensor_copy(turn[:, 0, 0], unit[:, 3, 0]))
                link(dve.tensor_scalar(turn[:, 0, 1], unit[:, 3, 1], sign[:, 0:1], None, ALU.mult))
                for j in range(6):
                    cmul(pair(turn[:, j + 1]), pair(turn[:, j]), pair(turn[:, j]), T4)
                link(dve.tensor_scalar(T4[0], unit[:, 3, 1], -1.0, None, ALU.mult))
                dve.tensor_copy(wf[:, 0], unit[:, 3, 0]).then_inc(turn_ready, 1)
                dve.wait_ge(turn_ready, 1)
                link(dve.tensor_copy(wf[:, 1], T4[0]))
                link(dve.tensor_scalar(T4[0], lb[0], -1.0, None, ALU.add))
                tt(T4[1], T4[0], lam[:, 0], ALU.mult)
                tt(T4[2], lb[1], lam[:, 1], ALU.mult)
                tt(fac[:, 0], T4[1], T4[2], ALU.add)
                tt(T4[1], lb[1], lam[:, 0], ALU.mult)
                tt(T4[2], T4[0], lam[:, 1], ALU.mult)
                tt(fac[:, 1], T4[1], T4[2], ALU.subtract)
                tt(T4[1], lam[:, 0], lam[:, 0], ALU.mult)
                tt(T4[2], lam[:, 1], lam[:, 1], ALU.mult)
                tt(T4[3], T4[1], T4[2], ALU.add)
                link(dve.reciprocal(T4[3], T4[3]))
                for i in range(2):
                    tt(fac[:, i], fac[:, i], T4[3], ALU.mult)
                cmul(pair(turn_w := tb[0][:, 0:4, :].rearrange("p (x a) c -> p x (a c)", x=2)),
                     lb, pair(wf), T4)
                link(dve.tensor_copy(wf[:], turn_w))
                wide_of = lambda t: tuple(t[:, i].unsqueeze(2).broadcast_to([P, G, GC]) for i in range(2))
                f2, w2 = wide_of(fac), wide_of(wf)
                for out, a, f in ((bbar, bb_in, f2), (bw, bbar, w2)):
                    for i, (x, yy, op) in enumerate(((0, 1, ALU.subtract), (1, 0, ALU.add))):
                        tt(tb[0][:], a[:, 0], f[x], ALU.mult)
                        tt(tb[1][:], a[:, 1], f[yy], ALU.mult)
                        tt(out[:, i], tb[0][:], tb[1][:], op)
                link(dve.tensor_scalar(cneg[:], cc[:, 1], -1.0, None, ALU.mult))
                tt(diag[:], ident[0:GC, 0:GC].unsqueeze(1).broadcast_to([GC, G, GC]),
                   dd[:].unsqueeze(2).broadcast_to([GC, G, GC]), ALU.mult)
                for l in range(8):
                    link(dve.tensor_copy(p_lag[0:64, l], pw[0:64, l]))
                    link(dve.tensor_copy(p_lag[64:128, l], pw[64:128, 7 - l]))
                    link(dve.tensor_copy(p_in[0:64, l], pw[0:64, 7 - l]))
                    link(dve.tensor_copy(p_in[64:128, l], pw[64:128, l]))

                for h in range(2):
                    gsl = slice(h * HALF, (h + 1) * HALF)
                    if h:
                        dve.wait_ge(y_done, NB)
                    full = [P, HALF, 8, GC]
                    power = lambda t, i: t[:, :, i, gsl].rearrange("p l g -> p g l").unsqueeze(3).broadcast_to(full)
                    chan = lambda t: t.unsqueeze(2).broadcast_to(full)
                    for out, pt, c_re, c_im, x_im, op in (
                            (out_w, p_lag, cc[:, 0, gsl], cc[:, 1, gsl], cneg[:, gsl], ALU.subtract),
                            (in_t, p_in, bw[:, 0, gsl], bw[:, 1, gsl], bw[:, 1, gsl], ALU.add)):
                        tt(wide[0][:], power(pt, 0), chan(c_re), ALU.mult)
                        tt(wide[1][:], power(pt, 1), chan(c_im), ALU.mult)
                        tt(out[:, 0], wide[0][:], wide[1][:], ALU.subtract)
                        tt(wide[0][:], power(pt, 0), chan(x_im), ALU.mult)
                        tt(wide[1][:], power(pt, 1), chan(c_re), ALU.mult)
                        ins = dve.tensor_tensor(out[:, 1], wide[0][:], wide[1][:], op)
                        ins.then_inc(in_ready, 1)
                        dve.wait_ge(in_ready, 2 * h + (1 if out is out_w else 2))
                    if h:
                        dve.wait_ge(local_in[0], 16 * CHUNK)
                    for i in range(HALF // 4):
                        g4 = slice(4 * i, 4 * i + 4)
                        view = lambda b: ps[0:GC, b].rearrange("p (g l c) -> p g l c", g=4, l=8)
                        fwd, bwd = view(S_BANK + 2 * (i % 2)), view(S_BANK + 2 * (i % 2) + 1)
                        dve.wait_ge(r_done, h * (HALF // 4) + i + 1)
                        link(dve.tensor_copy(resp[:, g4, 7:15], fwd))
                        link(dve.tensor_copy(resp[:, g4, 0:7], bwd[:, :, 0:7]))
                        tt(resp[:, g4, 7], bwd[:, :, 7], resp[:, g4, 7], ALU.add)
                        dve.tensor_tensor(resp[:, g4, 7], resp[:, g4, 7],
                                          diag[:, h * HALF + 4 * i:h * HALF + 4 * i + 4],
                                          ALU.add).then_inc(r_read, 1)
                    dve.wait_ge(r_read, (h + 1) * (HALF // 4))
                    dve.sem_inc(resp_ready, 1)

                    dve.wait_ge(rot_ready, h + 1)
                    for b in range(NB):
                        bsl = slice(b * BATCH, (b + 1) * BATCH)
                        v4 = lambda t: t.rearrange("p (g k) -> p g k", g=BATCH)
                        s_re = ps[:, S_BANK:S_BANK + BATCH, 0:NCH]
                        s_im = ps[:, S_BANK:S_BANK + BATCH, NCH:2 * NCH]
                        e_re, e_im = rot[:, 0, bsl], rot[:, 1, bsl]
                        dve.wait_ge(s_done, h * NB + b + 1)
                        tt(v4(gin[0][:]), s_re, e_re, ALU.mult)
                        tt(v4(gt[0][:]), s_im, e_im, ALU.mult)
                        tt(gin[0][:], gin[0][:], gt[0][:], ALU.add)
                        tt(v4(gin[1][:]), s_im, e_re, ALU.mult)
                        link(dve.tensor_tensor(v4(gt[1][:]), s_re, e_im, ALU.mult))
                        dve.tensor_tensor(gin[1][:], gin[1][:], gt[1][:], ALU.subtract).then_inc(s_read, 1)
                        dve.wait_ge(s_read, h * NB + b + 1)
                        dec = decay[:, bsl].rearrange("p g k -> p (g k)")
                        n = BATCH * NCH
                        for i in range(2):
                            link(dve.tensor_tensor_scan(gs[i][0:64, 2:n + 2], dec[0:64], gin[i][0:64],
                                                        0.0, ALU.mult, ALU.add))
                            link(dve.tensor_tensor_scan(gs[i][64:128, 0:n][:, ::-1], dec[64:128][:, ::-1],
                                                        gin[i][64:128][:, ::-1], 0.0, ALU.mult, ALU.add))
                            ent = gs[i][:, 1:n + 1].rearrange("p (g k) -> p g k", g=BATCH)
                            for rows, k0 in ((slice(0, 64), 0), (slice(0, 64), CH_A),
                                             (slice(64, 128), CH_A - 1), (slice(64, 128), NCH - 1)):
                                link(dve.memset(ent[rows, :, k0:k0 + 1], 0.0))
                        e0, e1 = v4(gs[0][:, 1:n + 1]), v4(gs[1][:, 1:n + 1])
                        hr, hi = hs[b % 2]
                        if h * NB + b >= 2:
                            dve.wait_ge(y_done, h * NB + b - 1)
                        tt(v4(gt[0][:]), e0, e_re, ALU.mult)
                        tt(v4(gt[1][:]), e1, e_im, ALU.mult)
                        tt(hr[:], v4(gt[0][:]), v4(gt[1][:]), ALU.subtract)
                        tt(v4(gt[0][:]), e0, e_im, ALU.mult)
                        tt(v4(gt[1][:]), e1, e_re, ALU.mult)
                        dve.tensor_tensor(hi[:], v4(gt[0][:]), v4(gt[1][:]), ALU.add).then_inc(h_ready, 1)
                        dve.wait_ge(h_ready, h * NB + b + 1)
                    dve.wait_ge(h_ready, (h + 1) * NB)
                    dve.sem_inc(half_done, 1)

            @block.tensor
            def _(pe):
                pe.wait_ge(par_in, 16 * 7)
                flat = lambda t: t.rearrange("p l c -> p (l c)")
                for h in range(2):
                    pe.wait_ge(in_ready, 2 * h + 1)
                    for i in range(HALF // 4):
                        n = h * (HALF // 4) + i
                        if n >= 2:
                            pe.wait_ge(r_read, n - 1)
                        if h and i == 0:
                            pe.wait_ge(s_read, NB)
                        for d, rows in enumerate((slice(0, 64), slice(64, 128))):
                            for j in range(4):
                                g = 4 * i + j
                                out = ps[0:GC, S_BANK + 2 * (i % 2) + d, j * P:(j + 1) * P]
                                for x in range(2):
                                    mm = pe.matmul(out, bbar[rows, x, h * HALF + g], flat(out_w[rows, x, g]),
                                                   start=(x == 0), stop=(x == 1))
                        mm.then_inc(r_done, 1)
                    pe.wait_ge(in_ready, 2 * h + 2)
                    for i in range(2 * HALF // 4):
                        n = h * (2 * HALF // 4) + i
                        if n >= 2:
                            pe.wait_ge(t_read, n - 1)
                        for j in range(4):
                            x, g = divmod(4 * i + j, HALF)
                            mm = pe.transpose(ps[:, W_BANK + i % 2, j * P:(j + 1) * P], flat(in_t[:, x, g]), ident[:])
                        mm.then_inc(t_done, 1)
                    pe.wait_ge(t_read, (h + 1) * (2 * HALF // 4))
                    pe.wait_ge(r_read, (h + 1) * (HALF // 4))
                    pe.wait_ge(u_in[h], 16 * 2 * CHUNK)
                    pe.wait_ge(local_in[h], 16 * CHUNK)

                    def outputs(b):
                        n = h * NB + b
                        pe.wait_ge(h_ready, n + 1)
                        if n >= 1:
                            pe.wait_ge(y_ready, n)
                        for j in range(BATCH):
                            g = b * BATCH + j
                            out = ps[:, Y_BANK + j // 2, (j % 2) * NCH:(j % 2 + 1) * NCH]
                            pe.matmul(out, local[:, g], u[:, g], start=True, stop=False)
                            pe.matmul(out, flat(out_w[:, 0, g]), hs[b % 2][0][:, j], start=False, stop=False)
                            mm = pe.matmul(out, flat(out_w[:, 1, g]), hs[b % 2][1][:, j], start=False, stop=True)
                        mm.then_inc(y_done, 1)

                    for b in range(NB):
                        n = h * NB + b
                        if n >= 1:
                            pe.wait_ge(s_read, n)
                        for j in range(BATCH):
                            g = b * BATCH + j
                            for x in range(2):
                                mm = pe.matmul(ps[:, S_BANK + j, x * NCH:(x + 1) * NCH], in_w[:, x, g], u[:, g],
                                               start=True, stop=True)
                        mm.then_inc(s_done, 1)
                        if b >= 1:
                            outputs(b - 1)
                    outputs(NB - 1)


QKP = 4
LAG = 3


def attention(nc, roped, proj, ident_d, mix):
    with ExitStack() as ctx:
        sb = lambda name, shape, dt=F32: ctx.enter_context(nc.sbuf_tensor(name, shape, dt))
        sem = lambda name: ctx.enter_context(nc.semaphore(name))
        k1 = sb("a_k1", [P, NKV, TOK], F32R)
        k2 = sb("a_k2", [P, NKV, TOK], F32R)
        KT = TOK // P
        v1 = sb("a_v1", [P, KT, NKV, P], F32R)
        v2 = sb("a_v2", [P, KT, NKV, P], F32R)
        v_raw = sb("a_vraw", [P, 2, TOK])
        ident = sb("a_ident", [P, P])
        q1 = [sb(f"a_q1{s}", [P, BLK], F32R) for s in range(NKV)]
        q2 = [sb(f"a_q2{s}", [P, BLK], F32R) for s in range(NKV)]
        nmax = [sb(f"a_nmax{s}", [P, BLK // P], F32R) for s in range(NKV)]
        p32 = [sb(f"a_p32{s}", [P, BLK]) for s in range(QKP)]
        p_hi = [sb(f"a_phi{s}", [P, BLK], F32R) for s in range(QKP)]
        p_lo = [sb(f"a_plo{s}", [P, BLK], F32R) for s in range(QKP)]
        den = [sb(f"a_den{s}", [HEAD, BLK]) for s in range(2)]
        o = [sb(f"a_o{s}", [HEAD, BLK]) for s in range(2)]
        ps = ctx.enter_context(nc.psum_tensor("a_ps", [P, 8, BLK], F32))
        ST_BANK, O_BANK, MX_BANK = 0, 2, 4

        k_in = sem("a_k_in")
        v_in = sem("a_v_in")
        ones_set = sem("a_ones_set")
        q_in = [sem(f"a_q_in{s}") for s in range(NKV)]
        nmax_in = [sem(f"a_nmax_in{s}") for s in range(NKV)]
        stored = [sem(f"a_stored{s}") for s in range(2)]
        v_turned = sem("a_v_turned")
        v1_ready = sem("a_v1_ready")
        v2_ready = sem("a_v2_ready")
        max_mm = sem("a_max_mm")
        max_found = sem("a_max_found")
        scored = sem("a_scored")
        exp_done = sem("a_exp_done")
        phi_done = sem("a_phi_done")
        plo_done = sem("a_plo_done")
        pv_done = sem("a_pv_done")
        ln_done = sem("a_ln_done")
        rden_done = sem("a_rden_done")
        normed = sem("a_normed")

        class Seq:
            def __init__(self, u0, s0, n, iters, kt0, blk0):
                self.u0, self.s0, self.n, self.iters, self.kt0, self.blk0 = u0, s0, n, iters, kt0, blk0
        A = Seq(0, 0, LEN_A // P, 4, 0, 0)
        B = Seq(16, 16 * A.n, LEN_B // P, 8, LEN_A // P, 1)
        SEQS = (A, B)
        STEPS = B.s0 + 32 * B.n

        def for_iterations(eng, sq, body):
            body(0, False)
            with eng.Fori(1, sq.iters - 1) as it:
                body(it, False)
            body(sq.iters - 1, True)

        def looks_ahead(last, kv):
            return not (last and kv >= 2)

        with nc.Block() as block:

            @block.sync
            def _(sp):
                for l, dst, rows in ((0, k1, 0), (0, k1, HEAD), (1, k2, 0)):
                    sp.dma_start(f32(dst[rows:rows + HEAD]),
                                 roped[l, NQ:NQ + NKV].rearrange("h d n -> d h n")).then_inc(k_in, 16)
                sp.dma_start(ident[:], ident_d).then_inc(v_in, 16)
                sp.dma_start(v_raw[:], proj[V_T:V_T + 2].rearrange("t p n -> p t n")).then_inc(v_in, 16)

                def load_q(kv, head, blk):
                    for l, dst, rows in ((0, q1, 0), (1, q1, HEAD), (0, q2, 0)):
                        sp.dma_start(f32(dst[kv][rows:rows + HEAD]),
                                     roped[l, head][:, bass.ds(blk * BLK, BLK)]).then_inc(q_in[kv], 16)

                def place_max(sq, it, kv):
                    u = sq.u0 + it * 4 + kv
                    s = kv
                    sp.wait_ge(max_found, 4 * u + 6)
                    for j in range(BLK // P):
                        sp.dma_start(f32(q2[s][HEAD:HEAD + 1, j * P:(j + 1) * P]),
                                     f32(nmax[s][:, j:j + 1])).then_inc(nmax_in[s], 16)

                def store(it, kv, head, blk, u):
                    sp.wait_ge(normed, u + 3)
                    sp.dma_start(mix[head][:, bass.ds(blk * BLK, BLK)], o[kv % 2][:]).then_inc(stored[kv % 2], 16)

                for kv in range(NKV):
                    load_q(kv, 4 * kv, 0)
                for sq in SEQS:
                    for kv in range(2):
                        place_max(sq, 0, kv)
                    n_blk = sq.iters // 4
                    for bi in range(n_blk):
                        blk = sq.blk0 + bi
                        def iteration(g, last_g):
                            it = g + 4 * bi
                            last = last_g and bi == n_blk - 1
                            for kv in range(NKV):
                                u = sq.u0 + it * 4 + kv
                                if looks_ahead(last, kv):
                                    place_max(sq, it if kv < 2 else it + 1, (kv + 2) % 4)
                                sp.wait_ge(scored, sq.s0 + sq.n * (it * 4 + kv + 1))
                                if not last_g:
                                    load_q(kv, g + (4 * kv + 1), blk)
                                elif blk + 1 < NBLK:
                                    load_q(kv, 4 * kv, blk + 1)
                                store(it, kv, g + 4 * kv, blk, u)
                        with sp.Fori(0, 3) as g:
                            iteration(g, False)
                        iteration(3, True)
                for s in range(2):
                    sp.wait_ge(stored[s], 16 * 24)

            @block.gpsimd
            def _(pool):
                pool.sem_inc(plo_done, QKP)
                with pool.Fori(0, STEPS // QKP) as i:
                    for s in range(QKP):
                        pool.wait_ge(phi_done, QKP * i + (s + 1))
                        pool.wait_ge(pv_done, QKP * i + (s + 1))
                        pool.tensor_tensor(p_lo[s][:], p32[s][:], f32(p_hi[s][:]),
                                           ALU.subtract).then_inc(plo_done, 1)

            @block.scalar
            def _(act):
                act.preload_act_table_set(LN_EXP)
                act.sem_inc(exp_done, 2)
                act.wait_ge(ones_set, 1)
                for i in range(6):
                    t, c = divmod(i, 3)
                    act.wait_ge(v_turned, i + 1)
                    act.activation(v1[:, 4 * c:4 * c + 4, 2 * t:2 * t + 2, 0:HEAD],
                                   ps[:, i].rearrange("p (c h d) -> p c h d", c=4, h=2),
                                   ACT.Copy).then_inc(v1_ready, 1)

                def normalise(u, s):
                    act.wait_ge(normed, u + 1)
                    act.activation(den[s][:], ps[HEAD:P, O_BANK + s], ACT.Ln).then_inc(ln_done, 1)
                    act.wait_ge(ln_done, u + 1)
                    act.activation(den[s][:], den[s][:], ACT.Exp, scale=-1.0).then_inc(rden_done, 1)

                for sq in SEQS:
                    def iteration(it, last):
                        for kv in range(NKV):
                            for kt in range(sq.n):
                                step = it * (4 * sq.n) + (sq.s0 + kv * sq.n + kt)
                                act.wait_ge(scored, step + 1)
                                act.wait_ge(plo_done, step + 1)
                                act.activation(p32[kt % QKP][:], ps[:, ST_BANK + kt % 2], ACT.Exp,
                                               scale=HEAD ** -0.5).then_inc(exp_done, 1)
                                if kt == LAG and not (isinstance(it, int) and it == 0 and kv == 0):
                                    act.wait_ge(pv_done, step + (1 + QKP - LAG))
                                    normalise(it * 4 + (sq.u0 + kv - 1), (kv + 1) % 2)
                    for_iterations(act, sq, iteration)
                    act.wait_ge(pv_done, sq.s0 + 4 * sq.iters * sq.n + QKP)
                    normalise(sq.u0 + 4 * sq.iters - 1, 1)

            @block.vector
            def _(dve):
                dve.sem_inc(max_found, 2)
                dve.sem_inc(normed, 2)
                dve.memset(f32(v1[:, :, :, HEAD:P]), 1.0).then_inc(ones_set, 1)
                dve.memset(f32(v2[:, :, :, HEAD:P]), 0.0)
                dve.memset(f32(k2[HEAD:HEAD + 1]), 1.0).then_inc(ones_set, 1)
                for i in range(6):
                    t, c = divmod(i, 3)
                    dve.wait_ge(v1_ready, i + 1)
                    dve.tensor_tensor(v2[:, 4 * c:4 * c + 4, 2 * t:2 * t + 2, 0:HEAD],
                                      ps[:, i].rearrange("p (c h d) -> p c h d", c=4, h=2),
                                      f32(v1[:, 4 * c:4 * c + 4, 2 * t:2 * t + 2, 0:HEAD]),
                                      ALU.subtract).then_inc(v2_ready, 1)

                def find_max(sq, u, s, j):
                    dve.wait_ge(max_mm, 4 * u + (j + 1))
                    if sq is A:
                        src = ps[:, MX_BANK + j]
                    else:
                        src = ps[:, MX_BANK + 2 * (j % 2):MX_BANK + 2 * (j % 2) + 2]
                    dve.tensor_reduce(nmax[s][:, j:j + 1], src, AX.X if sq is A else AX.XY, ALU.max,
                                      negate=True).then_inc(max_found, 1)

                def scale_out(u, s):
                    dve.wait_ge(rden_done, u + 1)
                    half = (u - s) * 8
                    dve.wait_ge(stored[s], half)
                    dve.tensor_tensor(o[s][:], ps[0:HEAD, O_BANK + s], den[s][:],
                                      ALU.mult).then_inc(normed, 1)

                for sq in SEQS:
                    for kv in range(2):
                        for j in range(4):
                            find_max(sq, sq.u0 + kv, kv, j)

                    def iteration(it, last):
                        for kv in range(NKV):
                            for kt in range(sq.n):
                                step = it * (4 * sq.n) + (sq.s0 + kv * sq.n + kt)
                                dve.wait_ge(exp_done, step + 3)
                                dve.wait_ge(pv_done, step + 1)
                                dve.tensor_copy(p_hi[kt % QKP][:], p32[kt % QKP][:]).then_inc(phi_done, 1)
                                if kt == LAG and not (isinstance(it, int) and it == 0 and kv == 0):
                                    scale_out(it * 4 + (sq.u0 + kv - 1), (kv + 1) % 2)
                                if looks_ahead(last, kv):
                                    per = sq.n // 4
                                    if kt % per == per - 1:
                                        find_max(sq, it * 4 + (sq.u0 + kv + 2), (kv + 2) % 4, kt // per)
                    for_iterations(dve, sq, iteration)
                    scale_out(sq.u0 + 4 * sq.iters - 1, 1)

            @block.tensor
            def _(pe):
                pe.sem_inc(pv_done, QKP)
                pe.wait_ge(v_in, 32)
                for i in range(6):
                    t, c = divmod(i, 3)
                    for j in range(4):
                        kt = 4 * c + j
                        mm = pe.transpose(ps[:, i, j * P:(j + 1) * P], v_raw[:, t, kt * P:(kt + 1) * P],
                                          ident[:])
                    mm.then_inc(v_turned, 1)
                pe.wait_ge(ones_set, 2)
                pe.wait_ge(v2_ready, 6)
                pe.wait_ge(k_in, 48)

                def max_part(sq, u, s, kt):
                    per = sq.n // 4
                    j, half = divmod(kt, per)
                    if half == 0:
                        pe.wait_ge(max_found, 4 * u + (j + 1))
                    bank = MX_BANK + (j if sq is A else 2 * (j % 2) + half)
                    key0 = (sq.kt0 + 4 * half) * P
                    mm = pe.matmul(ps[:, bank], q1[s][0:HEAD, j * P:(j + 1) * P],
                                   k1[0:HEAD, s, key0:key0 + BLK], start=True, stop=True)
                    if half == per - 1:
                        mm.then_inc(max_mm, 1)

                def output(sq, unit, s, kt, step):
                    pe.wait_ge(plo_done, step + 1 + QKP)
                    if kt == 0:
                        pe.wait_ge(normed, unit + 1)
                    out, tile = ps[:, O_BANK + s % 2], sq.kt0 + kt
                    first, last = kt == 0, kt == sq.n - 1
                    pe.matmul(out, v1[:, tile, s], p_hi[kt % QKP][:], start=first, stop=False)
                    pe.matmul(out, v2[:, tile, s], p_hi[kt % QKP][:], start=False, stop=False)
                    pe.matmul(out, v1[:, tile, s], p_lo[kt % QKP][:], start=False,
                              stop=last).then_inc(pv_done, 1)

                for sq in SEQS:
                    for kv in range(2):
                        pe.wait_ge(q_in[kv], 48 * (sq.u0 // 4 + 1))
                        for kt in range(sq.n):
                            max_part(sq, sq.u0 + kv, kv, kt)

                    def iteration(it, last):
                        for kv in range(NKV):
                            unit = it * 4 + (sq.u0 + kv)
                            ahead, s_ahead = unit + 2, (kv + 2) % 4
                            n_of = lambda k: it + (sq.u0 // 4 + 1 + (1 if k >= NKV else 0))
                            pe.wait_ge(nmax_in[kv], n_of(kv) * 64)
                            pe.wait_ge(q_in[kv], n_of(kv) * 48)
                            if looks_ahead(last, kv):
                                pe.wait_ge(q_in[s_ahead], n_of(kv + 2) * 48)
                            for kt in range(sq.n):
                                step = it * (4 * sq.n) + (sq.s0 + kv * sq.n + kt)
                                tile = sq.kt0 + kt
                                pe.wait_ge(exp_done, step + 1)
                                out = ps[:, ST_BANK + kt % 2]
                                keys = slice(tile * P, (tile + 1) * P)
                                pe.matmul(out, k1[:, kv, keys], q1[kv][:], start=True, stop=False)
                                pe.matmul(out, k2[0:HEAD + 1, kv, keys], q2[kv][0:HEAD + 1], start=False,
                                          stop=True).then_inc(scored, 1)
                                if looks_ahead(last, kv):
                                    max_part(sq, ahead, s_ahead, kt)
                                if kt >= LAG:
                                    output(sq, unit, kv, kt - LAG, step - LAG)
                                elif not (isinstance(it, int) and it == 0 and kv == 0):
                                    output(sq, unit - 1, (kv + 3) % 4, kt - LAG + sq.n, step - LAG)
                    for_iterations(pe, sq, iteration)
                    for kt in range(sq.n - LAG, sq.n):
                        output(sq, sq.u0 + 4 * sq.iters - 1, 3, kt, sq.s0 + (4 * sq.iters - 1) * sq.n + kt)


TAIL_T = 2 * KD + KD + 2 * (D_FF // P)
QUART = 8
MLP_ORDER = [("f1", 0), ("f1", 1), ("f2", 0), ("f1", 2), ("f2", 1), ("f1", 3), ("f2", 2), ("f2", 3)]


def tail(nc, mix, proj, x_t, w_tail, gain, ones_d, y_t):
    with ExitStack() as ctx:
        sb = lambda name, shape, dt=F32: ctx.enter_context(nc.sbuf_tensor(name, shape, dt))
        sem = lambda name: ctx.enter_context(nc.semaphore(name))
        h_hi = sb("t_hhi", [P, KD, BLK], F32R)
        h_lo = sb("t_hlo", [P, KD, BLK], F32R)
        y_hi = sb("t_yhi", [P, 4, BLK], F32R)
        y_lo = sb("t_ylo", [P, 4, BLK], F32R)
        a_hi = [sb(f"t_ahi{s}", [P, QUART, BLK], F32R) for s in range(2)]
        a_lo = [sb(f"t_alo{s}", [P, QUART, BLK], F32R) for s in range(2)]
        x1 = sb("t_x1", [P, KD, BLK])
        w_raw = [sb(f"t_wraw{s}", [P, KD, P]) for s in range(2)]
        w_hi = [sb(f"t_whi{s}", [P, KD, P], F32R) for s in range(2)]
        w_lo = [sb(f"t_wlo{s}", [P, KD, P], F32R) for s in range(2)]
        g_raw = [sb(f"t_graw{s}", [P, 2, BLK]) for s in range(2)]
        sg = [sb(f"t_sg{s}", [P, 2, BLK]) for s in range(2)]
        sgb = [sb(f"t_sgb{s}", [P, BLK]) for s in range(2)]
        ta = [sb(f"t_ta{s}", [P, BLK]) for s in range(2)]
        tb = [sb(f"t_tb{s}", [P, BLK]) for s in range(2)]
        tc = [sb(f"t_tc{s}", [P, BLK]) for s in range(2)]
        rs = sb("t_rs", [P, BLK])
        gn = sb("t_gain", [P, KD])
        eps = sb("t_eps", [P, 1])
        ones = sb("t_ones", [P, P])
        ps = ctx.enter_context(nc.psum_tensor("t_ps", [P, 8, BLK], F32))
        A_BANK, G_BANK, O_BANK, F1_BANK, F2_BANK, MEAN = 0, 2, 6, 0, 2, 4

        const_in = sem("t_const_in")
        eps_set = sem("t_eps_set")
        act_turn = sem("t_act_turn")
        w_in_s = [sem(f"t_w_in{s}") for s in range(2)]
        mix_in = [sem(f"t_mix_in{s}") for s in range(2)]
        g_in = [sem(f"t_g_in{s}") for s in range(2)]
        x1_in = sem("t_x1_in")
        y_out = sem("t_y_out")
        mixhi_ready = sem("t_mixhi_ready")
        mixlo_ready = sem("t_mixlo_ready")
        whi_ready = sem("t_whi_ready")
        wlo_ready = sem("t_wlo_ready")
        summed = sem("t_summed")
        sg_ready = sem("t_sg_ready")
        sgb_ready = sem("t_sgb_ready")
        merge_step = sem("t_merge_step")
        merged32 = sem("t_merged32")
        mhi_ready = sem("t_mhi_ready")
        mlo_ready = sem("t_mlo_ready")
        x1_ready = sem("t_x1_ready")
        hhi_ready = sem("t_hhi_ready")
        hlo_ready = sem("t_hlo_ready")
        sq_ready = sem("t_sq_ready")
        sq_used = sem("t_sq_used")
        ln_done = sem("t_ln_done")
        rs_ready = sem("t_rs_ready")
        relu_ready = sem("t_relu_ready")
        t_ready = sem("t_t_ready")
        tsq_ready = sem("t_tsq_ready")
        ahi_ready = sem("t_ahi_ready")
        alo_ready = sem("t_alo_ready")
        f2_added = sem("t_f2_added")

        S1, S2 = 0, 2 * KD
        MLP = S2 + KD
        SECT = [(kind, q, MLP + QUART * n) for n, (kind, q) in enumerate(MLP_ORDER)]
        PAIRS = QUART // 2
        gates = proj[GA_T:GS_T + KD].rearrange("(t m) p n -> m p t n", t=2)

        with nc.Block() as block:

            @block.sync
            def _(sp):
                def load_w(j, s):
                    sp.dma_start(w_raw[s][:], w_tail[j]).then_inc(w_in_s[s], 16)

                def next_w(b, j, s):
                    sp.wait_ge(wlo_ready, b * TAIL_T + j + 3)
                    load_w(j + 2, s)

                sp.sem_inc(y_out, 16)
                sp.dma_start(gn[:], gain).then_inc(const_in, 16)
                sp.dma_start(ones[:], ones_d).then_inc(const_in, 16)
                load_w(0, 0)
                load_w(1, 1)
                with sp.Fori(0, NBLK) as b:
                    blk = bass.ds(b * BLK, BLK)

                    def mix_pair(c, s):
                        sp.dma_start(g_raw[s][:], mix[2 * c:2 * c + 2, :, blk].rearrange(
                            "k p n -> p k n")).then_inc(mix_in[s], 16)

                    for c in range(6):
                        if c < 2:
                            sp.wait_ge(sg_ready, b * KD + 1)
                        else:
                            sp.wait_ge(mixlo_ready, b * 6 + c - 1)
                        mix_pair(c, c % 2)
                    for m in range(2):
                        sp.wait_ge(mixlo_ready, b * 6 + 5 + m)
                        sp.dma_start(g_raw[m][:], gates[m][:, :, blk]).then_inc(g_in[m], 16)
                    sp.wait_ge(y_out, b * KD * 16 + 16)
                    sp.dma_start(x1[:], x_t[b]).then_inc(x1_in, 16)

                    def merge_pair(i, more):
                        for s in range(2):
                            m = 2 * i + s
                            next_w(b, S1 + 2 * m, 0)
                            next_w(b, S1 + 2 * m + 1, 1)
                            if more:
                                sp.wait_ge(sg_ready, b * KD + m + 2)
                                sp.dma_start(g_raw[s][:], gates[m + 2][:, :, blk]).then_inc(g_in[s], 16)

                    with sp.Fori(0, KD // 2 - 1) as i:
                        merge_pair(i, True)
                    merge_pair(KD // 2 - 1, False)
                    with sp.Fori(0, (TAIL_T - S2 - QUART) // 2) as i:
                        for s in range(2):
                            next_w(b, 2 * i + (S2 + s), s)
                    with sp.Fori(0, PAIRS) as i:
                        for s in range(2):
                            next_w(b, 2 * i + (TAIL_T - QUART + s), s)
                            sp.wait_ge(f2_added, b * (4 * KD) + 2 * i + (3 * KD + s + 3))
                            sp.dma_start(y_t[b][:, 2 * i + s], x1[:, 2 * i + s]).then_inc(y_out, 16)
                sp.wait_ge(y_out, NBLK * KD * 16 + 16)
                for s in range(2):
                    sp.wait_ge(w_in_s[s], 16 * (NBLK * TAIL_T // 2 + 1))

            @block.gpsimd
            def _(pool):
                pool.sem_inc(wlo_ready, 2)
                with pool.Fori(0, NBLK * TAIL_T // 2 + 1) as i:
                    for s in range(2):
                        pool.wait_ge(whi_ready, 2 * i + (s + 1))
                        pool.wait_ge(w_in_s[s], 16 * i + 16)
                        pool.tensor_tensor(w_lo[s][:], w_raw[s][:], f32(w_hi[s][:]),
                                           ALU.subtract).then_inc(wlo_ready, 1)

            @block.scalar
            def _(act):
                act.preload_act_table(ACT.Sigmoid)
                act.sem_inc(relu_ready, 2)
                for sem_ in (sg_ready, mhi_ready, ahi_ready):
                    act.sem_inc(sem_, 1)

                def w_high(b, j, s):
                    act.wait_ge(w_in_s[s], b * (8 * TAIL_T) + (j - s) * 8 + 16)
                    act.wait_ge(summed, b * TAIL_T + j + 1)
                    act.activation(w_hi[s][:], w_raw[s][:], ACT.Copy).then_inc(whi_ready, 1)

                w_high(0, 0, 0)
                w_high(0, 1, 1)
                act.wait_ge(const_in, 32)
                act.wait_ge(eps_set, 1)
                with act.Fori(0, NBLK) as b:
                    act.preload_act_table(ACT.Sigmoid)
                    act.wait_ge(summed, b * TAIL_T + 2)
                    for c in range(6):
                        s = c % 2
                        act.wait_ge(mix_in[s], b * 48 + (c // 2 + 1) * 16)
                        dst = h_hi[:, 2 * c:2 * c + 2] if c < 4 else y_hi[:, 2 * c - 8:2 * c - 6]
                        act.activation(dst, g_raw[s][:], ACT.Copy).then_inc(mixhi_ready, 1)
                    with act.Fori(0, KD // 2) as i:
                        for s in range(2):
                            m = 2 * i + s
                            act.wait_ge(g_in[s], b * (8 * KD) + 16 * i + 16)
                            act.wait_ge(merged32, m + (b * KD + 1))
                            act.activation(sg[s][:], g_raw[s][:], ACT.Sigmoid).then_inc(sg_ready, 1)
                            w_high(b, 4 * i + (2 * s + 2), 0)
                            act.wait_ge(summed, b * TAIL_T + 4 * i + (2 * s + 4))
                            act.activation(sgb[s][:], ps[:, G_BANK + 2 * s + 1],
                                           ACT.Sigmoid).then_inc(sgb_ready, 1)
                            w_high(b, 4 * i + (2 * s + 3), 1)
                            act.wait_ge(merged32, b * KD + m + 2)
                            alone(act, act_turn)
                            act.activation(a_hi[0][:, m], tc[s][:], ACT.Copy).then_inc(mhi_ready, 1)
                    act.preload_act_table_set(LN_EXP)
                    with act.Fori(0, KD // 2) as i:
                        for s in range(2):
                            m = 2 * i + s
                            w_high(b, 2 * i + (S2 + 2 + s), s)
                            act.wait_ge(x1_ready, b * KD + m + 3)
                            alone(act, act_turn)
                            act.activation(h_hi[:, m], x1[:, m], ACT.Identity,
                                           scale=gn[:, bass.ds(m, 1)]).then_inc(hhi_ready, 1)
                            act.wait_ge(sq_used, b * KD + m + 1)
                            alone(act, act_turn)
                            act.activation(sgb[s][:], x1[:, m], ACT.Square).then_inc(sq_ready, 1)

                    for kind, q, j0 in SECT:
                        def pair(i, first=False):
                            for s in range(2):
                                j = 2 * i + (j0 + s)
                                f = 2 * i + (QUART * q + s)
                                if kind == "f1":
                                    act.wait_ge(summed, b * TAIL_T + j + 3)
                                    act.wait_ge(tsq_ready, b * (4 * QUART) + f + 1)
                                    act.activation(ta[s][:], ps[:, F1_BANK + s],
                                                   ACT.Relu).then_inc(relu_ready, 1)
                                w_high(b, j + 2, s)
                                if kind == "f1":
                                    if first and s == 0:
                                        act.wait_ge(sq_used, b * KD + KD + 2)
                                        act.activation(rs[:], ps[:, MEAN], ACT.Ln,
                                                       bias=eps[:, 0:1]).then_inc(ln_done, 1)
                                        act.wait_ge(ln_done, b + 1)
                                        act.activation(rs[:], rs[:], ACT.Exp,
                                                       scale=-0.5).then_inc(rs_ready, 1)
                                    act.wait_ge(t_ready, b * (4 * QUART) + f + 1)
                                    alone(act, act_turn)
                                    act.activation(a_hi[q % 2][:, 2 * i + s], tb[s][:],
                                                   ACT.Square).then_inc(ahi_ready, 1)
                        if (kind, q) == ("f1", 0):
                            pair(0, True)
                            with act.Fori(1, PAIRS) as i:
                                pair(i)
                        else:
                            with act.Fori(0, PAIRS) as i:
                                pair(i)

            @block.vector
            def _(dve):
                dve.memset(eps[:], EPS).then_inc(eps_set, 1)
                for s_ in (x1_ready, alo_ready, f2_added):
                    dve.sem_inc(s_, 2)
                dve.sem_inc(merge_step, 6)
                for s_ in (merged32, mlo_ready, tsq_ready):
                    dve.sem_inc(s_, 1)
                dve.wait_ge(const_in, 32)
                with dve.Fori(0, NBLK) as b:
                    for c in range(6):
                        dst, hi = ((h_lo[:, 2 * c:2 * c + 2], h_hi[:, 2 * c:2 * c + 2]) if c < 4 else
                                   (y_lo[:, 2 * c - 8:2 * c - 6], y_hi[:, 2 * c - 8:2 * c - 6]))
                        dve.wait_ge(mixhi_ready, b * 6 + c + 1)
                        dve.tensor_tensor(dst, g_raw[c % 2][:], f32(hi), ALU.subtract).then_inc(mixlo_ready, 1)
                    with dve.Fori(0, KD // 2) as i:
                        for s in range(2):
                            mm = b * KD + 2 * i + s
                            dve.wait_ge(sg_ready, mm + 2)
                            dve.wait_ge(summed, b * TAIL_T + 4 * i + (2 * s + 3))
                            dve.wait_ge(mhi_ready, mm + 1)
                            dve.wait_ge(mlo_ready, mm + 1)
                            dve.tensor_tensor(ta[s][:], ps[:, A_BANK + s], sg[s][:, 0],
                                              ALU.mult).then_inc(merge_step, 1)
                            dve.wait_ge(sgb_ready, mm + 1)
                            dve.tensor_tensor(tb[s][:], ps[:, G_BANK + 2 * s], sgb[s][:],
                                              ALU.mult).then_inc(merge_step, 1)
                            dve.wait_ge(merge_step, mm * 3 + 8)
                            dve.tensor_tensor(tb[s][:], tb[s][:], sg[s][:, 1], ALU.mult).then_inc(merge_step, 1)
                            dve.wait_ge(merge_step, mm * 3 + 9)
                            dve.tensor_tensor(tc[s][:], ta[s][:], tb[s][:], ALU.add).then_inc(merged32, 1)
                            dve.wait_ge(mhi_ready, mm + 2)
                            dve.tensor_tensor(a_lo[0][:, 2 * i + s], tc[s][:], f32(a_hi[0][:, 2 * i + s]),
                                              ALU.subtract).then_inc(mlo_ready, 1)
                    with dve.Fori(0, KD // 2) as i:
                        for s in range(2):
                            m = 2 * i + s
                            dve.wait_ge(x1_in, b * 16 + 16)
                            dve.wait_ge(summed, b * TAIL_T + 2 * i + (S2 + s + 3))
                            dve.tensor_tensor(x1[:, m], ps[:, O_BANK + s], x1[:, m],
                                              ALU.add).then_inc(x1_ready, 1)
                            dve.wait_ge(hhi_ready, b * KD + m + 1)
                            dve.scalar_tensor_tensor(h_lo[:, m], x1[:, m], gn[:, bass.ds(m, 1)],
                                                     f32(h_hi[:, m]), ALU.mult,
                                                     ALU.subtract).then_inc(hlo_ready, 1)
                    for kind, q, j0 in SECT:
                        with dve.Fori(0, PAIRS) as i:
                            for s in range(2):
                                n = 2 * i + s
                                f = b * (4 * QUART) + 2 * i + (QUART * q + s)
                                if kind == "f1":
                                    if (q, s) == (0, 0):
                                        dve.wait_ge(rs_ready, b + 1)
                                    dve.wait_ge(relu_ready, f + 3)
                                    dve.wait_ge(ahi_ready, f + 1)
                                    dve.tensor_tensor(tb[s][:], ta[s][:], rs[:], ALU.mult).then_inc(t_ready, 1)
                                    dve.wait_ge(t_ready, f + 1)
                                    dve.wait_ge(alo_ready, f + 2)
                                    dve.tensor_tensor(tc[s][:], tb[s][:], tb[s][:],
                                                      ALU.mult).then_inc(tsq_ready, 1)
                                    dve.wait_ge(tsq_ready, f + 2)
                                    dve.wait_ge(ahi_ready, f + 2)
                                    dve.tensor_tensor(a_lo[q % 2][:, n], tc[s][:], f32(a_hi[q % 2][:, n]),
                                                      ALU.subtract).then_inc(alo_ready, 1)
                                else:
                                    dve.wait_ge(summed, b * TAIL_T + 2 * i + (j0 + s + 3))
                                    if q:
                                        dve.wait_ge(f2_added, f - 5)
                                    dve.tensor_tensor(x1[:, n], ps[:, F2_BANK + s], x1[:, n],
                                                      ALU.add).then_inc(f2_added, 1)

            @block.tensor
            def _(pe):
                pe.sem_inc(summed, 2)
                pe.sem_inc(sq_used, 2)
                pe.wait_ge(const_in, 32)

                def weights(b, j):
                    pe.wait_ge(whi_ready, b * TAIL_T + j + 1)
                    pe.wait_ge(wlo_ready, b * TAIL_T + j + 3)

                def product(bank, s, x_hi, x_lo, k0=0, n=KD, each=None, done=True):
                    for k in range(n):
                        if each:
                            each(k)
                        mm = three_products(pe, ps[:, bank], w_hi[s][:, k0 + k], w_lo[s][:, k0 + k],
                                            x_hi[:, k], x_lo[:, k], k == 0, k == n - 1)
                    if done:
                        mm.then_inc(summed, 1)

                def add_square(b, k, s):
                    pe.wait_ge(sq_ready, b * KD + k + 1)
                    pe.matmul(ps[:, MEAN], ones[:], sgb[s][:], start=isinstance(k, int) and k == 0,
                              stop=isinstance(k, int) and k == KD - 1, skip_group_check=True).then_inc(sq_used, 1)

                with pe.Fori(0, NBLK) as b:
                    with pe.Fori(0, KD // 2) as i:
                        for s in range(2):
                            pe.wait_ge(mixlo_ready, b * 6 + 6)
                            pe.wait_ge(f2_added, b * (4 * KD) + 2)
                            m = b * KD + 2 * i + s
                            pe.wait_ge(merge_step, m * 3 + 2)
                            weights(b, 4 * i + 2 * s)
                            product(A_BANK + s, 0, h_hi, h_lo)
                            weights(b, 4 * i + (2 * s + 1))
                            product(G_BANK + 2 * s, 1, y_hi, y_lo, 0, 4, done=False)
                            product(G_BANK + 2 * s + 1, 1, y_hi, y_lo, 4, 4)

                    def out_pair(i):
                        for s in range(2):
                            weights(b, 2 * i + (S2 + s))
                            pe.wait_ge(x1_ready, b * KD + 2 * i + (s + 1))
                            product(O_BANK + s, s, a_hi[0], a_lo[0], each=(
                                lambda k: pe.wait_ge(mlo_ready, b * KD + k + 2))
                                if (i, s) == (0, 0) else None)
                            if i and s == 0:
                                add_square(b, 2 * i - 2, 0)
                                add_square(b, 2 * i - 1, 1)

                    for i in range(KD // 2):
                        out_pair(i)

                    for kind, q, j0 in SECT:
                        def pair(i, first=False):
                            for s in range(2):
                                n = b * (4 * QUART) + 2 * i + (QUART * q + s)
                                weights(b, 2 * i + (j0 + s))
                                if kind == "f1":
                                    pe.wait_ge(relu_ready, n + 1)
                                    product(F1_BANK + s, s, h_hi, h_lo, each=(
                                        lambda k: pe.wait_ge(hlo_ready, b * KD + k + 1))
                                        if first and s == 0 else None)
                                    if first and s == 0 and q == 0:
                                        add_square(b, KD - 2, 0)
                                        add_square(b, KD - 1, 1)
                                else:
                                    pe.wait_ge(f2_added, n + 1)
                                    product(F2_BANK + s, s, a_hi[q % 2], a_lo[q % 2], each=(
                                        lambda k: pe.wait_ge(alo_ready, b * (4 * QUART) + QUART * q + k + 3))
                                        if first and s == 0 else None)
                        pair(0, True)
                        with pe.Fori(1, PAIRS) as i:
                            pair(i)


def encoder_layer(nc, ap, y_t):
    scratch = lambda name, shape: nc.dram_tensor(name, shape, F32).ap()
    proj = scratch("proj_scratch", [PROJ_T, P, TOK])
    roped = scratch("roped_scratch", [2, NQ + NKV, HEAD, TOK])
    mix = scratch("mix_scratch", [12, P, TOK])
    project(nc, ap["x_t"], ap["w_in_t"], ap["norm_mix_t"], ap["model_mean"], proj)
    rope_prep(nc, proj, ap["qk_gain"], ap["head_mean"], ap["rope"], roped)
    state_space(nc, proj, ap["lam"], ap["log_step"], ap["ssm_b"], ap["ssm_c"], ap["ssm_d_t"],
                ap["direction"], ap["identity"], mix)
    attention(nc, roped, proj, ap["identity"],
              mix[0:8].rearrange("t p n -> (t p) n").rearrange("(h d) n -> h d n", d=HEAD))
    tail(nc, mix, proj, ap["x_t"], ap["w_tail_t"], ap["norm_mlp_t"], ap["model_mean"], y_t)



def tiles(w):
    k, m = w.shape
    return w.reshape(k // P, P, m // P, P).transpose(2, 1, 0, 3)


def tail_stream(w_attn, w_glu_a, w_glu_b, w_out, w_ff1, w_ff2):
    attn, f1 = tiles(w_attn), tiles(w_ff1)
    glu = np.concatenate([tiles(w_glu_a), tiles(w_glu_b)], 2)
    f2 = tiles(w_ff2).reshape(KD, P, D_FF // P // QUART, QUART, P).transpose(2, 0, 1, 3, 4)
    parts = [np.stack([attn, glu], 1).reshape(2 * KD, P, KD, P), tiles(w_out)]
    parts += [f1[QUART * q:QUART * (q + 1)] if kind == "f1" else f2[q] for kind, q in MLP_ORDER]
    return np.ascontiguousarray(np.concatenate(parts + [attn[:1], glu[:1]], 0))


def token_order(length):
    return np.arange(length).reshape(length // CHUNK, CHUNK).T.reshape(-1)


def rope_tables():
    axis = HEAD // 2
    inv = (ROPE_THETA ** (-np.arange(0, axis, 2, dtype=np.float32) / np.float32(axis))).astype(np.float32)
    out = []
    for length in (LEN_A, LEN_B):
        t = token_order(length)
        ang = np.concatenate([(t // GRID_W)[None, :].astype(np.float32) * inv[:, None],
                              (t % GRID_W)[None, :].astype(np.float32) * inv[:, None]], 0)
        cos, sin = np.repeat(np.cos(ang), 2, 0), np.repeat(np.sin(ang), 2, 0)
        sin[0::2] *= -1
        out.append(np.tile(np.stack([cos, sin], 1), (2, 1, 1)))
    return np.ascontiguousarray(np.concatenate(out, 2).astype(np.float32))


def layouts(v):
    lay = np.ascontiguousarray
    g = lambda name: np.asarray(v[name])[0]
    x = np.concatenate([g("x_prompt")[token_order(LEN_A)], g("x_sample")[token_order(LEN_B)]], 0)
    eye = np.eye(P, dtype=np.float32)
    two = lambda a, b: np.stack([g(a), g(b)])
    return {
        "x_t": lay(x.reshape(NBLK, BLK, KD, P).transpose(0, 3, 2, 1)),
        "w_in_t": lay(tiles(g("w_in"))),
        "norm_mix_t": lay(g("norm_mix").reshape(KD, P).T),
        "norm_mlp_t": lay(g("norm_mlp").reshape(KD, P).T),
        "qk_gain": lay(np.tile(np.stack([g("q_norm"), g("k_norm")], 1), (2, 1))),
        "w_tail_t": tail_stream(g("w_attn_proj"), g("w_glu_a"), g("w_glu_b"), g("w_out"),
                                g("w_ff1"), g("w_ff2")),
        "lam": lay(two("ssm_lambda_re", "ssm_lambda_im").transpose(1, 3, 0, 2).reshape(P, 2, GROUPS)),
        "log_step": lay(np.repeat(g("ssm_log_step"), STATE, axis=0)),
        "ssm_b": lay(two("ssm_b_re", "ssm_b_im").transpose(1, 3, 0, 2, 4).reshape(P, 2, GROUPS, GC)),
        "ssm_c": lay(two("ssm_c_re", "ssm_c_im").transpose(1, 4, 0, 2, 3).reshape(P, 2, GROUPS, GC)),
        "ssm_d_t": lay(g("ssm_d").reshape(GROUPS, GC).T),
        "model_mean": np.full((P, P), 1.0 / D_MODEL, np.float32),
        "head_mean": lay(np.kron(np.eye(2), np.full((HEAD, HEAD), 1.0 / HEAD)).astype(np.float32)),
        "rope": rope_tables(),
        "direction": lay(np.repeat(np.array([1.0, -1.0], np.float32), STATE)[:, None]),
        "identity": eye,
    }


def kernel(**inputs):
    import concourse.bacc as bacc
    from concourse.bass_utils import run_bass_kernel_spmd

    arrays = layouts(inputs)
    nc = bacc.Bacc("TRN2", target_bir_lowering=False, num_devices=1)
    ap = {n: nc.dram_tensor(n, a.shape, F32, kind="ExternalInput").ap() for n, a in arrays.items()}
    y_t = nc.dram_tensor("y_t", (NBLK, P, KD, BLK), F32, kind="ExternalOutput").ap()
    encoder_layer(nc, ap, y_t)
    result = run_bass_kernel_spmd(nc, [arrays], core_ids=[0])
    y = np.asarray(result.results[0]["y_t"]).transpose(0, 3, 2, 1).reshape(TOK, D_MODEL)
    out = []
    for start, length in ((0, LEN_A), (LEN_A, LEN_B)):
        part = y[start:start + length].reshape(CHUNK, length // CHUNK, D_MODEL).transpose(1, 0, 2)
        out.append(np.ascontiguousarray(part.reshape(1, length, D_MODEL)))
    return tuple(out)
```

```python
import math
from contextlib import ExitStack

import numpy as np

import concourse.bass as bass
from concourse import mybir

ALU = mybir.AluOpType
ACT = mybir.ActivationFunctionType
AX = mybir.AxisListType
F32 = mybir.dt.float32
F32R = mybir.dt.float32r

P = 128
D_MODEL = 1024
D_FF = 4096
HEAD = 64
NQ, NKV = 16, 4
LEN_A, LEN_B = 512, 1024
TOK = LEN_A + LEN_B
BLK = 512
NBLK = TOK // BLK
KD = D_MODEL // P
EPS = 1e-6
GRID_W = 64
ROPE_THETA = 10000.0
CHUNK = 8
GROUPS, GC, STATE = 32, 16, 64
LN_EXP = "natural_log_exp_and_others"

Q_T, K_T, V_T, U_T, GA_T, GS_T = 0, 8, 10, 12, 16, 24
PROJ_T = 32


def f32(ap):
    return ap.bitcast(F32)


def alone(eng, turn):
    eng.sem_inc(turn, 1)


def three_products(pe, out, whi, wlo, xhi, xlo, start, stop):
    pe.matmul(out, whi, xhi, start=start, stop=False)
    pe.matmul(out, whi, xlo, start=False, stop=False)
    return pe.matmul(out, wlo, xhi, start=False, stop=stop)


SWAP = [i ^ 1 for i in range(32)]
QK_T = V_T


CH_A, CH_B = LEN_A // CHUNK, LEN_B // CHUNK
NCH = CH_A + CH_B
BATCH = 4
TWO_PI = 2 * math.pi
C1 = 6.28125
C2 = float((np.float32(TWO_PI - C1).view(np.uint32) & np.uint32(0xfffff000)).view(np.float32))
C3 = TWO_PI - C1 - C2
ROUND = 1.5 * 2.0 ** 23


class Shared:

    def __init__(self, nc, ctx):
        sb = lambda name, shape, dt=F32: ctx.enter_context(nc.sbuf_tensor(name, shape, dt))
        self.x_hi = sb("x_hi", [P, NBLK, KD, BLK], F32R)
        self.x_lo = sb("x_lo", [P, NBLK, KD, BLK], F32R)
        self.rs = sb("x_rs", [P, TOK])
        self.w_raw = [sb(f"w_raw{s}", [P, KD, P]) for s in range(2)]
        self.w_hi = [sb(f"w_hi{s}", [P, KD, P], F32R) for s in range(2)]
        self.w_lo = [sb(f"w_lo{s}", [P, KD, P], F32R) for s in range(2)]
        self.stage = [sb(f"stage{s}", [P, TOK]) for s in range(2)]
        self.slot = [sb(f"slot{s}", [P, KD * BLK]) for s in range(2)]
        self.ident = sb("s_ident", [P, P])
        self.dd = sb("s_d", [GC, GROUPS])
        self.ratio = sb("s_ratio", [P, GROUPS])
        G, at = GROUPS, 0
        parts = {}
        for name, size in (("cc", 2 * G * GC), ("bbar", 2 * G * GC), ("bw", 2 * G * GC), ("turn", 14 * G),
                           ("p_lag", 16 * G)):
            parts[name] = self.slot[0][:, at:at + size]
            at += size
        assert at <= KD * BLK
        self.cc, self.bbar, self.bw = (parts[n].rearrange("p (x g c) -> p x g c", x=2, g=G)
                                       for n in ("cc", "bbar", "bw"))
        self.turn = parts["turn"].rearrange("p (j x g) -> p j x g", j=7, x=2)
        self.p_lag = parts["p_lag"].rearrange("p (l x g) -> p l x g", l=8, x=2)


def project(nc, sh, x_t, w_in, gain, ones_d, qk_gain, head_mean_d, tables_d, lam_d, step_d, b_d, c_d, d_d,
            sign_d, ident_d, proj, roped):
    with ExitStack() as ctx:
        sb = lambda name, shape, dt=F32: ctx.enter_context(nc.sbuf_tensor(name, shape, dt))
        sem = lambda name: ctx.enter_context(nc.semaphore(name))
        x_hi, x_lo, rs, w_raw, w_hi, w_lo, stage = sh.x_hi, sh.x_lo, sh.rs, sh.w_raw, sh.w_hi, sh.w_lo, sh.stage
        x = [sh.slot[b % 2][:].rearrange("p (k n) -> p k n", k=KD) for b in range(NBLK)]
        sq = sb("p1_sq", [P, 2, BLK])
        g = sb("p1_gain", [P, KD])
        eps = sb("p1_eps", [P, 1])
        ones = sb("p1_ones", [P, P])
        table = sh.slot[1][:, 0:2 * TOK].rearrange("p (x n) -> p x n", x=2)
        head_gain = sb("p1_head_gain", [P, 2])
        hmean = sb("p1_hmean", [P, P])
        head_rs, qn, sw = (sb(f"p1_{n}", [P, 2, BLK]) for n in ("head_rs", "qn", "sw"))
        r_hi, r_lo = (sb(f"p1_{n}", [P, 2, BLK], F32R) for n in ("r_hi", "r_lo"))
        G = GROUPS
        lam = sb("s_lam", [P, 2, G])
        lstep = sb("s_lstep", [P, G])
        sign = sb("s_sign", [P, 1])
        half_pi = sb("s_half_pi", [P, 1])
        z = sb("s_z", [P, 2, G])
        lam_sq = sb("s_lam_sq", [P, G])
        tmp = sb("s_tmp", [P, 4, G])
        ang = sb("s_ang", [P, 2, G])
        mag = sb("s_mag", [P, G])
        unit = sb("s_unit", [P, 4, 2, G])
        pw = sb("s_pw", [P, 9, 2, G])
        fac = sb("s_fac", [P, 2, G])
        wf = sb("s_wf", [P, 2, G])
        bb_in = qn[:].rearrange("p s (g c) -> p s g c", g=G)
        tb = [sw[:, i].rearrange("p (g c) -> p g c", g=G) for i in range(2)]
        acc = ctx.enter_context(nc.psum_tensor("p1_acc", [P, 6, BLK], F32))
        mean = ctx.enter_context(nc.psum_tensor("p1_mean", [P, 2, BLK], F32))
        MEAN_BANK = (0, 1, 1)

        const_in = sem("p1_const_in")
        rope_in = sem("p1_rope_in")
        x_in = [sem(f"p1_x_in{b}") for b in range(4 + NBLK)]
        w_in_s = [sem(f"p1_w_in{s}") for s in range(2)]
        eps_set = sem("p1_eps_set")
        sq_ready = sem("p1_sq_ready")
        sq_used = sem("p1_sq_used")
        ln_done = sem("p1_ln_done")
        rs_ready = sem("p1_rs_ready")
        xhi_ready = sem("p1_xhi_ready")
        xlo_ready = sem("p1_xlo_ready")
        whi_ready = sem("p1_whi_ready")
        wlo_ready = sem("p1_wlo_ready")
        summed = sem("p1_summed")
        evicted = sem("p1_evicted")
        stored = [sem(f"p1_stored{s}") for s in range(2)]
        hsq_ready = sem("p1_hsq_ready")
        hmean_ready = sem("p1_hmean_ready")
        hln_done = sem("p1_hln_done")
        hrs_ready = sem("p1_hrs_ready")
        qn_ready = sem("p1_qn_ready")
        sw_ready = sem("p1_sw_ready")
        cos_ready = sem("p1_cos_ready")
        sin_ready = sem("p1_sin_ready")
        sum_ready = sem("p1_sum_ready")
        hi_ready = sem("p1_hi_ready")
        lo_ready = sem("p1_lo_ready")
        roped_out = [sem(f"p1_roped_out{s}") for s in range(2)]
        dve_turn = sem("p1_dve_turn")
        par_in = sem("s_par_in")
        cc_in = sem("s_cc_in")
        b_in = sem("s_b_in")
        step_ready = sem("s_step_ready")
        angle_ready = sem("s_angle_ready")
        polar_ready = sem("s_polar_ready")
        d_done = sem("s_d_done")
        g_done = sem("s_g_done")

        QK_PAIRS = QK_T // 2
        PAIRS_ = GA_T // 2
        NQK = NBLK * QK_T
        cols = lambda b: slice(b * BLK, (b + 1) * BLK)

        def all_pairs(eng, pair):
            pair(0, False, True)
            with eng.Fori(1, QK_PAIRS) as i:
                pair(i, True, True)
            pair(QK_PAIRS, True, False)
            with eng.Fori(QK_PAIRS + 1, PAIRS_) as i:
                pair(i, False, False)

        def is_first(i):
            return isinstance(i, int) and i == 0

        def has(i, r, behind, own):
            return own if r >= 0 else behind

        with nc.Block() as block:

            @block.sync
            def _(sp):
                def load_w(m, s):
                    sp.dma_start(w_raw[s][:], w_in[m]).then_inc(w_in_s[s], 16)

                sp.dma_start(g[:], gain).then_inc(const_in, 16)
                for j in range(4):
                    sp.dma_start(x[0][:, 2 * j:2 * j + 2], x_t[0][:, 2 * j:2 * j + 2]).then_inc(x_in[j], 16)
                    if j == 0:
                        sp.dma_start(ones[:], ones_d).then_inc(const_in, 16)
                load_w(0, 0)
                load_w(1, 1)
                for dst, src in ((lam, lam_d), (lstep, step_d), (sign, sign_d), (sh.dd, d_d), (sh.ident, ident_d)):
                    sp.dma_start(dst[:], src).then_inc(par_in, 16)
                sp.dma_start(x[1][:], x_t[1]).then_inc(x_in[4], 16)
                sp.dma_start(hmean[:], head_mean_d).then_inc(rope_in, 16)
                sp.dma_start(head_gain[:], qk_gain).then_inc(rope_in, 16)
                sp.wait_ge(xlo_ready, KD)
                sp.dma_start(x[2][:], x_t[2]).then_inc(x_in[5], 16)
                sp.wait_ge(xlo_ready, 2 * KD)
                sp.dma_start(table, tables_d).then_inc(rope_in, 16)
                sp.wait_ge(xlo_ready, 3 * KD)
                sp.dma_start(sh.cc, c_d).then_inc(cc_in, 16)

                def pair(i, behind, own):
                    for s in range(2):
                        sp.wait_ge(wlo_ready, 2 * i + (s + 1))
                        load_w(2 * i + s + 2, s)
                        if behind:
                            for b in range(NBLK):
                                r = 3 * s + b - 6
                                sp.wait_ge(lo_ready, 6 * i + (r + 1))
                                for l, part in enumerate((r_hi, r_lo)):
                                    dst = roped[l].rearrange("(t h) d n -> t (h d) n", h=2)
                                    sp.dma_start(dst[2 * i - 2 + s][:, cols(b)],
                                                 f32(part[:, r % 2])).then_inc(roped_out[r % 2], 16)
                    if behind and not own:
                        sp.wait_ge(lo_ready, NQK)
                        sp.dma_start(bb_in, b_d).then_inc(b_in, 16)
                    for s in range(2) if not own else ():
                        sp.wait_ge(evicted, 6 * i + (6 + 3 * s + 3))
                        sp.dma_start(proj[2 * i + s], stage[s][:]).then_inc(stored[s], 16)

                all_pairs(sp, pair)
                for s in range(2):
                    sp.wait_ge(roped_out[s], 16 * NQK)
                    sp.wait_ge(stored[s], 16 * (PAIRS_ - QK_PAIRS))
                sp.wait_ge(b_in, 16)
                sp.wait_ge(cc_in, 16)

            @block.scalar
            def _(act):
                act.preload_act_table_set(LN_EXP)
                act.wait_ge(const_in, 32)
                act.wait_ge(eps_set, 2)

                def high(s, count):
                    act.wait_ge(w_in_s[s], count)
                    act.activation(w_hi[s][:], w_raw[s][:], ACT.Copy).then_inc(whi_ready, 1)

                for b in range(NBLK):
                    for k in range(KD):
                        if b:
                            act.wait_ge(x_in[3 + b], 16)
                        else:
                            act.wait_ge(x_in[k // 2], 16)
                        act.activation(x_hi[:, b, k], x[b][:, k], ACT.Identity,
                                       scale=g[:, k:k + 1]).then_inc(xhi_ready, 1)
                        act.wait_ge(sq_used, b * KD + k + 1)
                        act.activation(sq[:, k % 2], x[b][:, k], ACT.Square).then_inc(sq_ready, 1)
                    if b < 2:
                        high(b, 16)
                    act.wait_ge(sq_used, 2 + (b + 1) * KD)
                    act.activation(rs[:, cols(b)], mean[:, MEAN_BANK[b]], ACT.Ln,
                                   bias=eps[:, 0:1]).then_inc(ln_done, 1)
                    act.wait_ge(ln_done, b + 1)
                    act.activation(rs[:, cols(b)], rs[:, cols(b)],
                                   ACT.Exp, scale=-0.5).then_inc(rs_ready, 1)

                def pair(i, behind, own):
                    first = is_first(i)
                    for r in range(6):
                        if has(i, r, behind, own):
                            act.wait_ge(evicted, 6 * i + (6 + r + 1))
                            if not first or r >= 2:
                                act.wait_ge(hmean_ready, 6 * i + (r - 1))
                            act.activation(sq[:, r % 2], stage[r // 3][:, cols(r % 3)],
                                           ACT.Square).then_inc(hsq_ready, 1)
                        k = r - 1
                        if has(i, k, behind, own):
                            act.wait_ge(hmean_ready, 6 * i + (k + 1))
                            if not first or k >= 2:
                                act.wait_ge(qn_ready, 6 * i + (k - 1))
                            act.activation(head_rs[:, k % 2], mean[:, k % 2], ACT.Ln,
                                           bias=eps[:, 0:1]).then_inc(hln_done, 1)
                            act.wait_ge(hln_done, 6 * i + (k + 1))
                            act.activation(head_rs[:, k % 2], head_rs[:, k % 2], ACT.Exp,
                                           scale=-0.5).then_inc(hrs_ready, 1)
                        k = r - 2
                        if has(i, k, behind, own):
                            act.wait_ge(sum_ready, 6 * i + (k + 1))
                            if not first or k >= 2:
                                act.wait_ge(roped_out[k % 2], 96 * i + 32 * (k // 2))
                            act.activation(r_hi[:, k % 2], qn[:, k % 2], ACT.Copy).then_inc(hi_ready, 1)
                        if r % 3 == 2:
                            s = r // 3
                            act.wait_ge(summed, 6 * i + (3 * s + 3))
                            high(s, 16 * i + 32)
                    if first:
                        act.wait_ge(par_in, 16 * 5)
                        act.activation(lstep[:], lstep[:], ACT.Exp).then_inc(step_ready, 1)
                    if behind and not own:
                        act.wait_ge(angle_ready, 1)
                        act.activation(mag[:], z[:, 0], ACT.Exp).then_inc(polar_ready, 1)
                        act.activation(sh.ratio[:], z[:, 0], ACT.Exp, scale=float(CHUNK)).then_inc(polar_ready, 1)
                        act.activation(unit[:, 0, 1], ang[:, 0], ACT.Sin).then_inc(polar_ready, 1)
                        act.activation(unit[:, 0, 0], ang[:, 1], ACT.Sin, scale=-1.0,
                                       bias=half_pi[:, 0:1]).then_inc(polar_ready, 1)

                all_pairs(act, pair)

            @block.gpsimd
            def _(pool):
                pool.wait_ge(rope_in, 48)
                with pool.Fori(0, QK_PAIRS) as i:
                    for r in range(6):
                        pool.wait_ge(sw_ready, 6 * i + (r + 1))
                        pool.tensor_tensor(sw[:, r % 2], sw[:, r % 2], table[:, 1, cols(r % 3)],
                                           ALU.mult).then_inc(sin_ready, 1)

                n_link = [0]

                def link(ins):
                    n_link[0] += 1
                    ins.then_inc(g_done, 1)
                    pool.wait_ge(g_done, n_link[0])

                def tt(out, a, b, op):
                    link(pool.tensor_tensor(out, a, b, op))

                def cmul(out, a, b, t):
                    tt(t[0], a[0], b[0], ALU.mult)
                    tt(t[1], a[1], b[1], ALU.mult)
                    tt(t[2], a[0], b[1], ALU.mult)
                    tt(t[3], a[1], b[0], ALU.mult)
                    tt(out[0], t[0], t[1], ALU.subtract)
                    tt(out[1], t[2], t[3], ALU.add)

                T4 = [tmp[:, i] for i in range(4)]
                both = lambda t: (t[:, 0], t[:, 1])
                turn, p_lag = sh.turn, sh.p_lag
                one, lb = (pw[:, 0, 0], pw[:, 0, 1]), (pw[:, 1, 0], pw[:, 1, 1])
                link(pool.memset(one[0], 1.0))
                link(pool.memset(one[1], 0.0))
                pool.wait_ge(polar_ready, 4)
                for i in range(2):
                    tt(lb[i], unit[:, 0, i], mag[:], ALU.mult)
                for n in (1, 2, 4):
                    for j in range(n):
                        cmul(both(pw[:, n + 1 + j]), both(pw[:, 1 + j]), both(pw[:, n]), T4)
                for i in range(3):
                    cmul(both(unit[:, i + 1]), both(unit[:, i]), both(unit[:, i]), T4)
                pool.wait_ge(cc_in, 16)
                link(pool.tensor_copy(turn[:, 0, 0], unit[:, 3, 0]))
                tt(turn[:, 0, 1], unit[:, 3, 1], sign[:, 0:1].broadcast_to([P, G]), ALU.mult)
                for j in range(6):
                    cmul(both(turn[:, j + 1]), both(turn[:, j]), both(turn[:, j]), T4)
                tt(T4[0], lb[0], one[0], ALU.subtract)
                tt(T4[1], T4[0], lam[:, 0], ALU.mult)
                tt(T4[2], lb[1], lam[:, 1], ALU.mult)
                tt(fac[:, 0], T4[1], T4[2], ALU.add)
                tt(T4[1], lb[1], lam[:, 0], ALU.mult)
                tt(T4[2], T4[0], lam[:, 1], ALU.mult)
                tt(fac[:, 1], T4[1], T4[2], ALU.subtract)
                for i in range(2):
                    tt(fac[:, i], fac[:, i], lam_sq[:], ALU.mult)
                e8 = unit[:, 3]
                tt(T4[0], lb[0], e8[:, 0], ALU.mult)
                tt(T4[1], lb[1], e8[:, 1], ALU.mult)
                tt(wf[:, 0], T4[0], T4[1], ALU.add)
                tt(T4[0], lb[1], e8[:, 0], ALU.mult)
                tt(T4[1], lb[0], e8[:, 1], ALU.mult)
                tt(wf[:, 1], T4[0], T4[1], ALU.subtract)
                for l in range(8):
                    link(pool.tensor_copy(p_lag[0:64, l], pw[0:64, l]))
                    link(pool.tensor_copy(p_lag[64:128, l], pw[64:128, 7 - l]))
                wide_of = lambda t: tuple(t[:, i].unsqueeze(2).broadcast_to([P, G, GC]) for i in range(2))
                f2, w2 = wide_of(fac), wide_of(wf)
                pool.wait_ge(b_in, 16)
                for out, a, f in ((sh.bbar, bb_in, f2), (sh.bw, sh.bbar, w2)):
                    for i, (x_, y_, op) in enumerate(((0, 1, ALU.subtract), (1, 0, ALU.add))):
                        tt(tb[0], a[:, 0], f[x_], ALU.mult)
                        tt(tb[1], a[:, 1], f[y_], ALU.mult)
                        tt(out[:, i], tb[0], tb[1], op)

            @block.vector
            def _(dve):
                dve.memset(eps[:], EPS).then_inc(eps_set, 1)
                dve.memset(half_pi[:], math.pi / 2).then_inc(eps_set, 1)
                dve.sem_inc(evicted, 6)

                def low(s, count):
                    dve.wait_ge(whi_ready, count)
                    dve.tensor_tensor(w_lo[s][:], w_raw[s][:], f32(w_hi[s][:]),
                                      ALU.subtract).then_inc(wlo_ready, 1)

                dve.wait_ge(const_in, 32)
                for b in range(NBLK):
                    for k in range(KD):
                        dve.wait_ge(xhi_ready, b * KD + k + 1)
                        dve.wait_ge(sq_ready, b * KD + k + 1)
                        dve.scalar_tensor_tensor(x_lo[:, b, k], x[b][:, k], g[:, k:k + 1],
                                                 f32(x_hi[:, b, k]), ALU.mult,
                                                 ALU.subtract).then_inc(xlo_ready, 1)
                    if b < 2:
                        low(b, b + 1)
                dve.wait_ge(rope_in, 48)

                def rope(i, r, kind):
                    n, s, tok = 6 * i, r % 2, cols(r % 3)
                    early = is_first(i) and r < 2
                    dve.wait_ge(hrs_ready, n + (r + 1))
                    if not early:
                        dve.wait_ge(lo_ready, n + (r - 1))
                    dve.scalar_tensor_tensor(qn[:, s], stage[r % 6 // 3][:, tok], head_gain[:, kind:kind + 1],
                                             head_rs[:, s], ALU.mult, ALU.mult).then_inc(qn_ready, 1)
                    dve.wait_ge(qn_ready, n + (r + 1))
                    alone(dve, dve_turn)
                    dve.stream_shuffle(sw[:, s], qn[:, s], SWAP).then_inc(sw_ready, 1)
                    dve.wait_ge(sw_ready, n + (r + 1))
                    dve.tensor_tensor(qn[:, s], qn[:, s], table[:, 0, tok], ALU.mult).then_inc(cos_ready, 1)
                    dve.wait_ge(cos_ready, n + (r + 1))
                    dve.wait_ge(sin_ready, n + (r + 1))
                    dve.tensor_tensor(qn[:, s], qn[:, s], sw[:, s], ALU.add).then_inc(sum_ready, 1)
                    dve.wait_ge(hi_ready, n + (r + 1))
                    dve.tensor_tensor(r_lo[:, s], qn[:, s], f32(r_hi[:, s]), ALU.subtract).then_inc(lo_ready, 1)

                def pair(i, behind, own, kinds=(0, 0)):
                    first = is_first(i)
                    for r in range(6):
                        s, b = divmod(r, NBLK)
                        dve.wait_ge(summed, 6 * i + (r + 1))
                        if b == 0 and not own and not (isinstance(i, int) and i == QK_PAIRS):
                            dve.wait_ge(stored[s], 16 * i - 16 * QK_PAIRS)
                        if first:
                            dve.wait_ge(rs_ready, min(r + 1, NBLK))
                        dve.tensor_tensor(stage[s][:, cols(b)], acc[:, r], rs[:, cols(b)],
                                          ALU.mult).then_inc(evicted, 1)
                        if has(i, r - 2, behind, own):
                            rope(i, r - 2, kinds[int(r >= 2)])
                        if b == 2:
                            low(s, 2 * i + (s + 3))

                def angles():
                    n_link = [0]

                    def link(ins):
                        n_link[0] += 1
                        ins.then_inc(d_done, 1)
                        dve.wait_ge(d_done, n_link[0])

                    T = [tmp[:, i] for i in range(4)]
                    dve.wait_ge(step_ready, 1)
                    for i in range(2):
                        link(dve.tensor_tensor(z[:, i], lam[:, i], lstep[:], ALU.mult))
                    link(dve.tensor_scalar(T[0], z[:, 1], 1 / TWO_PI, ROUND, ALU.mult, ALU.add))
                    link(dve.tensor_scalar(T[0], T[0], -ROUND, None, ALU.add))
                    link(dve.scalar_tensor_tensor(ang[:, 0], T[0], -C1, z[:, 1], ALU.mult, ALU.add))
                    link(dve.scalar_tensor_tensor(ang[:, 0], T[0], -C2, ang[:, 0], ALU.mult, ALU.add))
                    link(dve.scalar_tensor_tensor(ang[:, 0], T[0], -C3, ang[:, 0], ALU.mult, ALU.add))
                    link(dve.tensor_scalar(ang[:, 0], ang[:, 0], 3.1415925, -3.1415925, ALU.min, ALU.max))
                    link(dve.scalar_tensor_tensor(ang[:, 1], ang[:, 0], -1.0, ang[:, 0], ALU.mult, ALU.max))
                    link(dve.tensor_tensor(T[1], lam[:, 0], lam[:, 0], ALU.mult))
                    link(dve.tensor_tensor(T[2], lam[:, 1], lam[:, 1], ALU.mult))
                    link(dve.tensor_tensor(T[3], T[1], T[2], ALU.add))
                    dve.reciprocal(lam_sq[:], T[3]).then_inc(angle_ready, 1)

                pair(0, False, True)
                angles()
                with dve.Fori(1, K_T // 2) as i:
                    pair(i, True, True)
                pair(K_T // 2, True, True, (0, 1))
                pair(QK_PAIRS, True, False, (1, 1))
                with dve.Fori(QK_PAIRS + 1, PAIRS_) as i:
                    pair(i, False, False)

            @block.tensor
            def _(pe):
                pe.sem_inc(sq_used, 2)
                pe.wait_ge(const_in, 32)

                def head_mean(i, k):
                    pe.wait_ge(hsq_ready, 6 * i + (k + 1))
                    if is_first(i) and k < 2:
                        pe.wait_ge(rs_ready, (1, 3)[k])
                    else:
                        pe.wait_ge(hln_done, 6 * i + (k - 1))
                    pe.matmul(mean[:, k % 2], hmean[:], sq[:, k % 2], start=True,
                              stop=True).then_inc(hmean_ready, 1)

                def pair(i, behind, own):
                    first = is_first(i)
                    for r in range(6):
                        s, b = divmod(r, NBLK)
                        if first and r < NBLK:
                            if b == 2:
                                pe.wait_ge(ln_done, 2)
                            for k in range(KD):
                                pe.wait_ge(sq_ready, b * KD + k + 1)
                                pe.matmul(mean[:, MEAN_BANK[b]], ones[:], sq[:, k % 2], start=(k == 0),
                                          stop=(k == KD - 1)).then_inc(sq_used, 1)
                            pe.wait_ge(xlo_ready, KD * (b + 1))
                        if b == 0:
                            pe.wait_ge(whi_ready, 2 * i + (s + 1))
                            pe.wait_ge(wlo_ready, 2 * i + (s + 1))
                        pe.wait_ge(evicted, 6 * i + (r + 1))
                        for k in range(KD):
                            mm = three_products(pe, acc[:, r], w_hi[s][:, k], w_lo[s][:, k],
                                                x_hi[:, b, k], x_lo[:, b, k], k == 0, k == KD - 1)
                        mm.then_inc(summed, 1)
                        if first and r == 2:
                            pe.wait_ge(rope_in, 48)
                            head_mean(0, 0)
                            head_mean(0, 1)
                        elif not (first and r < 2) and has(i, r - 1, behind, own):
                            head_mean(i, r - 1)

                all_pairs(pe, pair)


def gates_and_states(nc, sh, w_in, proj, mix):
    with ExitStack() as ctx:
        sb = lambda name, shape, dt=F32: ctx.enter_context(nc.sbuf_tensor(name, shape, dt))
        sem = lambda name: ctx.enter_context(nc.semaphore(name))
        N = BATCH * NCH
        w_raw, w_hi, w_lo, stage = sh.w_raw, sh.w_hi, sh.w_lo, sh.stage[0]
        out_w = sb("s_outw", [P, 2, BATCH, 8, GC])
        in_t = sb("s_int", [P, 2, BATCH, 8, GC])
        in_w = sb("s_inw", [P, 2, BATCH, P])
        resp = sb("s_resp", [GC, BATCH, 15, GC])
        rot = sb("s_rot", [P, 2, BATCH, NCH])
        decay = sb("s_decay", [P, BATCH, NCH])
        gs = [sb(f"s_gs{i}", [P, N + 2]) for i in range(2)]
        bbar_b = sb("s_bbar_b", [P, 2, BATCH, GC])
        turn_b = sb("s_turn_b", [P, 7, 2, BATCH])
        ratio_b = sb("s_ratio_b", [P, BATCH])
        p_lag = sb("s_plag_b", [P, 8, 2, BATCH])
        diag = sb("s_diag", [GC, BATCH, GC])
        groups = lambda ap: ap.rearrange("p (g k) -> p g k", g=BATCH)
        u = groups(sh.stage[1][:, 0:N])
        y = groups(sh.stage[1][:, N:2 * N])
        scratch = sh.slot[1]
        gin = [scratch[:, i * N:(i + 1) * N] for i in range(2)]
        gt = [scratch[:, (2 + i) * N:(3 + i) * N] for i in range(2)]
        wide = [t[:, 0:BATCH * 8 * GC].rearrange("p (g l c) -> p g l c", g=BATCH, l=8) for t in gt]
        at = 4 * N
        local = scratch[:, at:at + BATCH * P].rearrange("p (g c) -> p g c", g=BATCH)
        rt = [groups(scratch[:, at + BATCH * (P + i * 64):at + BATCH * (P + (i + 1) * 64)]) for i in range(2)]
        ps = ctx.enter_context(nc.psum_tensor("s_ps", [P, 8, BLK], F32))
        S_BANK, Y_BANK, G_BANK = 0, 4, 6

        u_in = sem("s_u_in")
        local_in = sem("s_local_in")
        y_out = sem("s_y_out")
        d_done = sem("s_d2_done")
        g_done = sem("s_g2_done")
        par_ready = sem("s_par_ready")
        in_ready = sem("s_in_ready")
        out_ready = sem("s_out_ready")
        t_done = sem("s_t_done")
        t_read = sem("s_t_read")
        s_done = sem("s_s_done")
        r_done = sem("s_r_done")
        resp_ready = sem("s_resp_ready")
        rot_ready = sem("s_rot_ready")
        h_ready = sem("s_h_ready")
        y_done = sem("s_y_done")
        y_ready = sem("s_y_ready")
        pool_turn, pe_turn = sem("s_pool_turn"), sem("s_pe_turn")
        w_in_s = [sem(f"g_w_in{s}") for s in range(2)]
        whi_ready = sem("g_whi_ready")
        wlo_ready = sem("g_wlo_ready")
        summed = sem("g_summed")
        evicted = sem("g_evicted")
        scaled = sem("g_scaled")
        stored = [sem(f"g_stored{c}") for c in range(NBLK)]

        BATCHES = GROUPS // BATCH
        GB = 2 * NBLK
        cols = lambda c: slice(c * BLK, (c + 1) * BLK)
        D_LINKS, G_LINKS = 40, 49

        def all_batches(eng, batch):
            with eng.Fori(0, BATCHES - 1) as b:
                batch(b, True)
            batch(BATCHES - 1, False)

        with nc.Block() as block:

            @block.sync
            def _(sp):
                seqs = ((0, 0, CH_A), (LEN_A, CH_A, CH_B))
                by_channel = lambda t: t.rearrange("t p n -> (t p) n").rearrange("(g c) n -> c g n", c=GC)
                u_src, y_dst = by_channel(proj[U_T:U_T + 4]), by_channel(mix[8:12])

                def load_u(b):
                    for t in range(CHUNK):
                        for pos, k0, n in seqs:
                            sp.dma_start(u[t * GC:(t + 1) * GC, :, k0:k0 + n],
                                         u_src[:, bass.ds(b * BATCH, BATCH), pos + t * n:pos + (t + 1) * n]
                                         ).then_inc(u_in, 16)

                sp.sem_inc(y_out, 16)
                for c in range(NBLK):
                    sp.sem_inc(stored[c], 16)
                load_u(0)

                def batch(b, more):
                    def store_gate(r):
                        sp.wait_ge(scaled, GB * b + (r + 1))
                        sp.dma_start(proj[2 * b + (GA_T + r // NBLK)][:, cols(r % NBLK)],
                                     stage[:, cols(r % NBLK)]).then_inc(stored[r % NBLK], 16)

                    if more:
                        for s in range(2):
                            sp.wait_ge(wlo_ready, 2 * b + (s + 1))
                            sp.dma_start(w_raw[s][:], w_in[2 * b + (GA_T + 2 + s)]).then_inc(w_in_s[s], 16)
                    store_gate(0)
                    store_gate(1)
                    sp.wait_ge(resp_ready, b + 1)
                    for s in range(CHUNK):
                        sp.dma_start(local[s * GC:(s + 1) * GC],
                                     resp[:, :, 7 - s:15 - s].rearrange("p g l c -> p g (l c)")
                                     ).then_inc(local_in, 16)
                    for r in (2, 3, 4):
                        store_gate(r)
                    if more:
                        sp.wait_ge(y_done, b + 2)
                        load_u(b + 1)
                    sp.wait_ge(y_ready, b + 2)
                    for t in range(CHUNK):
                        for pos, k0, n in seqs:
                            sp.dma_start(y_dst[:, bass.ds(b * BATCH, BATCH), pos + t * n:pos + (t + 1) * n],
                                         y[t * GC:(t + 1) * GC, :, k0:k0 + n]).then_inc(y_out, 16)
                    store_gate(5)

                all_batches(sp, batch)
                sp.wait_ge(y_out, 16 * 2 * CHUNK * BATCHES + 16)
                for c in range(NBLK):
                    sp.wait_ge(stored[c], 16 * 2 * BATCHES + 16)

            @block.scalar
            def _(act):
                act.preload_act_table(ACT.Gelu_apprx_tanh)
                act.sem_inc(whi_ready, 2)
                act.sem_inc(evicted, 2)
                act.sem_inc(y_ready, 1)

                def batch(b, more):
                    def evict(r):
                        act.wait_ge(summed, GB * b + (r + 1))
                        act.wait_ge(stored[r % NBLK], 32 * b + 16 * (r // NBLK) + 16)
                        act.activation(stage[:, cols(r % NBLK)], ps[:, G_BANK + r % 2],
                                       ACT.Copy).then_inc(evicted, 1)

                    def high(s):
                        act.wait_ge(w_in_s[s], 16 * b + 16)
                        act.activation(w_hi[s][:], w_raw[s][:], ACT.Copy).then_inc(whi_ready, 1)

                    evict(0)
                    for i in range(2):
                        act.wait_ge(t_done, 2 * b + (i + 1))
                        act.activation(in_w[:, i], ps[:, S_BANK + i].rearrange("p (g c) -> p g c", g=BATCH),
                                       ACT.Copy).then_inc(t_read, 1)
                    evict(1)
                    evict(2)
                    if more:
                        high(0)
                    evict(3)
                    evict(4)
                    act.wait_ge(y_done, b + 2)
                    act.wait_ge(y_out, 16 * 2 * CHUNK * b + 16)
                    act.activation(y.rearrange("p (b g) k -> p b g k", b=2),
                                   ps[:, Y_BANK:Y_BANK + 2, 0:2 * NCH].rearrange("p b (g k) -> p b g k", g=2),
                                   ACT.Gelu_apprx_tanh).then_inc(y_ready, 1)
                    evict(5)
                    if more:
                        high(1)

                all_batches(act, batch)

            @block.gpsimd
            def _(pool):
                pool.sem_inc(wlo_ready, 2)

                def rotations(b):
                    n_link = [0]

                    def link(ins):
                        n_link[0] += 1
                        ins.then_inc(g_done, 1)
                        pool.wait_ge(g_done, G_LINKS * b + n_link[0])

                    pool.wait_ge(par_ready, b + 1)
                    alone(pool, pool_turn)
                    re, im = rot[:, 0, :, CH_A:], rot[:, 1, :, CH_A:]
                    link(pool.memset(re[:, :, 0:1], 1.0))
                    alone(pool, pool_turn)
                    link(pool.memset(im[:, :, 0:1], 0.0))
                    for j in range(7):
                        n = 1 << j
                        t_re, t_im = (turn_b[:, j, x].unsqueeze(2).broadcast_to([P, BATCH, n]) for x in range(2))
                        a, c = rt[0][:, :, 0:n], rt[1][:, :, 0:n]
                        link(pool.tensor_tensor(a, re[:, :, 0:n], t_re, ALU.mult))
                        link(pool.tensor_tensor(c, im[:, :, 0:n], t_im, ALU.mult))
                        link(pool.tensor_tensor(re[:, :, n:2 * n], a, c, ALU.subtract))
                        link(pool.tensor_tensor(a, re[:, :, 0:n], t_im, ALU.mult))
                        link(pool.tensor_tensor(c, im[:, :, 0:n], t_re, ALU.mult))
                        link(pool.tensor_tensor(im[:, :, n:2 * n], a, c, ALU.add))
                    alone(pool, pool_turn)
                    link(pool.tensor_copy(rot[:, :, :, 0:CH_A], rot[:, :, :, CH_A:2 * CH_A]))
                    alone(pool, pool_turn)
                    link(pool.tensor_copy(decay[:], ratio_b[:].unsqueeze(2).broadcast_to([P, BATCH, NCH])))
                    first = decay[0:64, :, 0:2 * CH_A].rearrange("p g (s k) -> p g s k", s=2)[:, :, :, 0:1]
                    alone(pool, pool_turn)
                    link(pool.memset(first, 0.0))
                    alone(pool, pool_turn)
                    link(pool.memset(decay[64:128, :, CH_A - 1:CH_A], 0.0))
                    alone(pool, pool_turn)
                    link(pool.memset(decay[64:128, :, NCH - 1:NCH], 0.0))
                    pool.sem_inc(rot_ready, 1)
                    assert n_link[0] == G_LINKS, n_link

                def batch(b, more):
                    def scale(r):
                        pool.wait_ge(evicted, GB * b + (r + 3))
                        pool.tensor_tensor(stage[:, cols(r % NBLK)], stage[:, cols(r % NBLK)],
                                           sh.rs[:, cols(r % NBLK)], ALU.mult).then_inc(scaled, 1)

                    def low(s):
                        pool.wait_ge(whi_ready, 2 * b + (s + 3))
                        pool.tensor_tensor(w_lo[s][:], w_raw[s][:], f32(w_hi[s][:]),
                                           ALU.subtract).then_inc(wlo_ready, 1)

                    for r in range(3):
                        scale(r)
                    if more:
                        low(0)
                    scale(3)
                    scale(4)
                    if more:
                        rotations(b + 1)
                    scale(5)
                    if more:
                        low(1)

                rotations(0)
                all_batches(pool, batch)

            @block.vector
            def _(dve):
                def batch(b):
                    n_link = [0]

                    def link(ins):
                        n_link[0] += 1
                        ins.then_inc(d_done, 1)
                        dve.wait_ge(d_done, D_LINKS * b + n_link[0])

                    def tt(out, a, c, op):
                        link(dve.tensor_tensor(out, a, c, op))

                    gsl = bass.ds(b * BATCH, BATCH)
                    link(dve.tensor_copy(bbar_b[:], sh.bbar[:, :, gsl]))
                    link(dve.tensor_copy(ratio_b[:], sh.ratio[:, gsl]))
                    link(dve.tensor_copy(p_lag[:], sh.p_lag[:, :, :, gsl]))
                    tt(diag[:], sh.ident[0:GC, 0:GC].unsqueeze(1).broadcast_to([GC, BATCH, GC]),
                       sh.dd[:, gsl].unsqueeze(2).broadcast_to([GC, BATCH, GC]), ALU.mult)
                    dve.tensor_copy(turn_b[:], sh.turn[:, :, :, gsl]).then_inc(par_ready, 1)

                    full = [P, BATCH, 8, GC]
                    power = lambda t, i: t[:, :, i].rearrange("p l g -> p g l").unsqueeze(3).broadcast_to(full)
                    chan = lambda t, x: t[:, x, gsl].unsqueeze(2).broadcast_to(full)
                    p_in = p_lag[:, ::-1]
                    tt(wide[0], power(p_in, 0), chan(sh.bw, 0), ALU.mult)
                    tt(wide[1], power(p_in, 1), chan(sh.bw, 1), ALU.mult)
                    tt(in_t[:, 0], wide[0], wide[1], ALU.subtract)
                    tt(wide[0], power(p_in, 0), chan(sh.bw, 1), ALU.mult)
                    tt(wide[1], power(p_in, 1), chan(sh.bw, 0), ALU.mult)
                    dve.tensor_tensor(in_t[:, 1], wide[0], wide[1], ALU.add).then_inc(in_ready, 1)
                    dve.wait_ge(in_ready, b + 1)
                    dve.wait_ge(y_done, b + 1)
                    tt(wide[0], power(p_lag, 0), chan(sh.cc, 0), ALU.mult)
                    tt(wide[1], power(p_lag, 1), chan(sh.cc, 1), ALU.mult)
                    tt(out_w[:, 0], wide[0], wide[1], ALU.subtract)
                    tt(wide[0], power(p_lag, 0), chan(sh.cc, 1), ALU.mult)
                    tt(wide[1], power(p_lag, 1), chan(sh.cc, 0), ALU.mult)
                    dve.scalar_tensor_tensor(out_w[:, 1], wide[0], -1.0, wide[1], ALU.mult,
                                             ALU.subtract).then_inc(out_ready, 1)
                    dve.wait_ge(out_ready, b + 1)

                    s_re, s_im = ps[:, S_BANK:S_BANK + BATCH, 0:NCH], ps[:, S_BANK:S_BANK + BATCH, NCH:2 * NCH]
                    e_re, e_im = rot[:, 0], rot[:, 1]
                    dve.wait_ge(rot_ready, b + 1)
                    dve.wait_ge(s_done, b + 1)
                    tt(groups(gin[0]), s_re, e_re, ALU.mult)
                    tt(groups(gt[0]), s_im, e_im, ALU.mult)
                    tt(gin[0], gin[0], gt[0], ALU.add)
                    tt(groups(gin[1]), s_im, e_re, ALU.mult)
                    tt(groups(gt[1]), s_re, e_im, ALU.mult)
                    tt(gin[1], gin[1], gt[1], ALU.subtract)

                    view = lambda bank: ps[0:GC, bank].rearrange("p (g l c) -> p g l c", g=BATCH, l=8)
                    fwd, bwd = view(Y_BANK), view(Y_BANK + 1)
                    dve.wait_ge(r_done, b + 1)
                    link(dve.tensor_copy(resp[:, :, 7:15], fwd))
                    link(dve.tensor_copy(resp[:, :, 0:7], bwd[:, :, 0:7]))
                    tt(resp[:, :, 7], bwd[:, :, 7], resp[:, :, 7], ALU.add)
                    dve.tensor_tensor(resp[:, :, 7], resp[:, :, 7], diag[:], ALU.add).then_inc(resp_ready, 1)

                    dec = decay[:].rearrange("p g k -> p (g k)")
                    for i in range(2):
                        link(dve.tensor_tensor_scan(gs[i][0:64, 2:N + 2], dec[0:64], gin[i][0:64],
                                                    0.0, ALU.mult, ALU.add))
                        link(dve.tensor_tensor_scan(gs[i][64:128, 0:N][:, ::-1], dec[64:128][:, ::-1],
                                                    gin[i][64:128][:, ::-1], 0.0, ALU.mult, ALU.add))
                        ent = groups(gs[i][:, 1:N + 1])
                        for rows, k0 in ((slice(0, 64), 0), (slice(0, 64), CH_A),
                                         (slice(64, 128), CH_A - 1), (slice(64, 128), NCH - 1)):
                            link(dve.memset(ent[rows, :, k0:k0 + 1], 0.0))
                    e0, e1 = groups(gs[0][:, 1:N + 1]), groups(gs[1][:, 1:N + 1])
                    tt(groups(gt[0]), e0, e_re, ALU.mult)
                    tt(groups(gt[1]), e1, e_im, ALU.mult)
                    tt(gin[0], gt[0], gt[1], ALU.subtract)
                    tt(groups(gt[0]), e0, e_im, ALU.mult)
                    tt(groups(gt[1]), e1, e_re, ALU.mult)
                    dve.tensor_tensor(gin[1], gt[0], gt[1], ALU.add).then_inc(h_ready, 1)
                    dve.wait_ge(h_ready, b + 1)
                    assert n_link[0] == D_LINKS, n_link

                with dve.Fori(0, BATCHES) as b:
                    batch(b)

            @block.tensor
            def _(pe):
                pe.sem_inc(y_done, 1)
                flat = lambda t: t.rearrange("p l c -> p (l c)")

                def gate(b, r):
                    s, c = divmod(r, NBLK)
                    if c == 0:
                        pe.wait_ge(whi_ready, 2 * b + (s + 1))
                        pe.wait_ge(wlo_ready, 2 * b + (s + 1))
                    pe.wait_ge(evicted, GB * b + (r + 1))
                    for k in range(KD):
                        mm = three_products(pe, ps[:, G_BANK + r % 2], w_hi[s][:, k], w_lo[s][:, k],
                                            sh.x_hi[:, c, k], sh.x_lo[:, c, k], k == 0, k == KD - 1)
                    mm.then_inc(summed, 1)

                with pe.Fori(0, BATCHES) as b:
                    gate(b, 0)
                    pe.wait_ge(in_ready, b + 1)
                    for x in range(2):
                        for j in range(BATCH):
                            mm = pe.transpose(ps[:, S_BANK + x, j * P:(j + 1) * P], flat(in_t[:, x, j]), sh.ident[:])
                        mm.then_inc(t_done, 1)
                    gate(b, 1)
                    pe.wait_ge(t_read, 2 * b + 2)
                    pe.wait_ge(u_in, 16 * 2 * CHUNK * b + 16 * 2 * CHUNK)
                    for j in range(BATCH):
                        for x in range(2):
                            mm = pe.matmul(ps[:, S_BANK + j, x * NCH:(x + 1) * NCH], in_w[:, x, j], u[:, j],
                                           start=True, stop=True)
                    mm.then_inc(s_done, 1)
                    pe.wait_ge(out_ready, b + 1)
                    pe.wait_ge(y_ready, b + 1)
                    alone(pe, pe_turn)
                    for d, rows in enumerate((slice(0, 64), slice(64, 128))):
                        for j in range(BATCH):
                            for x in range(2):
                                mm = pe.matmul(ps[0:GC, Y_BANK + d, j * P:(j + 1) * P], bbar_b[rows, x, j],
                                               flat(out_w[rows, x, j]), start=(x == 0), stop=(x == 1))
                    mm.then_inc(r_done, 1)
                    for r in (2, 3, 4):
                        gate(b, r)
                    pe.wait_ge(local_in, 16 * CHUNK * b + 16 * CHUNK)
                    pe.wait_ge(h_ready, b + 1)
                    for j in range(BATCH):
                        out = ps[:, Y_BANK + j // 2, (j % 2) * NCH:(j % 2 + 1) * NCH]
                        pe.matmul(out, local[:, j], u[:, j], start=True, stop=False)
                        pe.matmul(out, flat(out_w[:, 0, j]), groups(gin[0])[:, j], start=False, stop=False)
                        mm = pe.matmul(out, flat(out_w[:, 1, j]), groups(gin[1])[:, j], start=False, stop=True)
                    mm.then_inc(y_done, 1)
                    gate(b, 5)


QKP = 4
LAG = 3


def attention(nc, roped, proj, ident_d, mix):
    with ExitStack() as ctx:
        sb = lambda name, shape, dt=F32: ctx.enter_context(nc.sbuf_tensor(name, shape, dt))
        sem = lambda name: ctx.enter_context(nc.semaphore(name))
        k1 = sb("a_k1", [P, NKV, TOK], F32R)
        k2 = sb("a_k2", [P, NKV, TOK], F32R)
        KT = TOK // P
        v1 = sb("a_v1", [P, KT, NKV, P], F32R)
        v2 = sb("a_v2", [P, KT, NKV, P], F32R)
        v_raw = sb("a_vraw", [P, 2, TOK])
        ident = sb("a_ident", [P, P])
        q1 = [sb(f"a_q1{s}", [P, BLK], F32R) for s in range(NKV)]
        q2 = [sb(f"a_q2{s}", [P, BLK], F32R) for s in range(NKV)]
        nmax = [sb(f"a_nmax{s}", [P, BLK // P], F32R) for s in range(NKV)]
        p32 = [sb(f"a_p32{s}", [P, BLK]) for s in range(QKP)]
        p_hi = [sb(f"a_phi{s}", [P, BLK], F32R) for s in range(QKP)]
        p_lo = [sb(f"a_plo{s}", [P, BLK], F32R) for s in range(QKP)]
        den = [sb(f"a_den{s}", [HEAD, BLK]) for s in range(2)]
        o = [sb(f"a_o{s}", [HEAD, BLK]) for s in range(2)]
        ps = ctx.enter_context(nc.psum_tensor("a_ps", [P, 8, BLK], F32))
        ST_BANK, O_BANK, MX_BANK = 0, 2, 4

        k_in = [sem(f"a_k_in{s}") for s in range(2)]
        v_in = sem("a_v_in")
        ones_set = sem("a_ones_set")
        q_in = [sem(f"a_q_in{s}") for s in range(NKV)]
        nmax_in = [sem(f"a_nmax_in{s}") for s in range(NKV)]
        stored = [sem(f"a_stored{s}") for s in range(2)]
        v_turned = sem("a_v_turned")
        v1_ready = sem("a_v1_ready")
        v2_ready = sem("a_v2_ready")
        max_mm = sem("a_max_mm")
        max_found = sem("a_max_found")
        scored = sem("a_scored")
        exp_done = sem("a_exp_done")
        phi_done = sem("a_phi_done")
        plo_done = sem("a_plo_done")
        pv_done = sem("a_pv_done")
        ln_done = sem("a_ln_done")
        rden_done = sem("a_rden_done")
        normed = sem("a_normed")

        class Seq:
            def __init__(self, u0, s0, n, iters, kt0, blk0):
                self.u0, self.s0, self.n, self.iters, self.kt0, self.blk0 = u0, s0, n, iters, kt0, blk0
        A = Seq(0, 0, LEN_A // P, 4, 0, 0)
        B = Seq(16, 16 * A.n, LEN_B // P, 8, LEN_A // P, 1)
        SEQS = (A, B)
        STEPS = B.s0 + 32 * B.n

        def for_iterations(eng, sq, body):
            body(0, False)
            with eng.Fori(1, sq.iters - 1) as it:
                body(it, False)
            body(sq.iters - 1, True)

        def looks_ahead(last, kv):
            return not (last and kv >= 2)

        with nc.Block() as block:

            @block.sync
            def _(sp):
                def load_k(n, tok):
                    for l, dst, rows in ((0, k1, 0), (0, k1, HEAD), (1, k2, 0)):
                        sp.dma_start(f32(dst[rows:rows + HEAD, :, tok]),
                                     roped[l, NQ:NQ + NKV, :, tok].rearrange("h d n -> d h n")
                                     ).then_inc(k_in[n], 16)

                sp.dma_start(ident[:], ident_d).then_inc(v_in, 16)
                sp.dma_start(v_raw[:], proj[V_T:V_T + 2].rearrange("t p n -> p t n")).then_inc(v_in, 16)

                def load_q(kv, head, blk):
                    for l, dst, rows in ((0, q1, 0), (1, q1, HEAD), (0, q2, 0)):
                        sp.dma_start(f32(dst[kv][rows:rows + HEAD]),
                                     roped[l, head][:, bass.ds(blk * BLK, BLK)]).then_inc(q_in[kv], 16)

                def place_max(sq, it, kv):
                    u = sq.u0 + it * 4 + kv
                    s = kv
                    for j in range(BLK // P):
                        sp.wait_ge(max_found, 4 * u + (3 + j))
                        sp.dma_start(f32(q2[s][HEAD:HEAD + 1, j * P:(j + 1) * P]),
                                     f32(nmax[s][:, j:j + 1])).then_inc(nmax_in[s], 16)

                def store(u, kv, head, blk):
                    sp.wait_ge(normed, u + 3)
                    sp.dma_start(mix[head][:, bass.ds(blk * BLK, BLK)], o[kv % 2][:]).then_inc(stored[kv % 2], 16)

                load_k(0, slice(0, LEN_A))
                for kv in range(NKV):
                    load_q(kv, 4 * kv, 0)
                load_k(1, slice(LEN_A, TOK))
                for sq in SEQS:
                    for kv in range(2):
                        place_max(sq, 0, kv)
                    n_blk = sq.iters // 4
                    for bi in range(n_blk):
                        blk = sq.blk0 + bi

                        def iteration(g, first_g, last_g):
                            it = g + 4 * bi
                            last = last_g and bi == n_blk - 1
                            for kv in range(NKV):
                                u = sq.u0 + it * 4 + kv
                                if looks_ahead(last, kv):
                                    place_max(sq, it if kv < 2 else it + 1, (kv + 2) % 4)
                                sp.wait_ge(scored, sq.s0 + sq.n * (it * 4 + kv + 1))
                                if not last_g:
                                    load_q(kv, g + (4 * kv + 1), blk)
                                elif blk + 1 < NBLK:
                                    load_q(kv, 4 * kv, blk + 1)
                                if kv:
                                    store(u - 1, kv - 1, g + 4 * (kv - 1), blk)
                                elif not first_g:
                                    store(u - 1, NKV - 1, g + (4 * (NKV - 1) - 1), blk)
                                elif bi:
                                    store(u - 1, NKV - 1, NQ - 1, blk - 1)

                        iteration(0, True, False)
                        with sp.Fori(1, 3) as g:
                            iteration(g, False, False)
                        iteration(3, False, True)
                    store(sq.u0 + 4 * sq.iters - 1, NKV - 1, NQ - 1, sq.blk0 + n_blk - 1)
                for s in range(2):
                    sp.wait_ge(stored[s], 16 * 24)

            @block.gpsimd
            def _(pool):
                pool.sem_inc(plo_done, QKP)
                with pool.Fori(0, STEPS // QKP) as i:
                    for s in range(QKP):
                        pool.wait_ge(phi_done, QKP * i + (s + 1))
                        pool.wait_ge(pv_done, QKP * i + (s + 1))
                        pool.tensor_tensor(p_lo[s][:], p32[s][:], f32(p_hi[s][:]),
                                           ALU.subtract).then_inc(plo_done, 1)

            @block.scalar
            def _(act):
                act.preload_act_table_set(LN_EXP)
                act.sem_inc(exp_done, 2)
                act.wait_ge(ones_set, 1)
                for i in range(6):
                    t, c = divmod(i, 3)
                    act.wait_ge(v_turned, i + 1)
                    act.activation(v1[:, 4 * c:4 * c + 4, 2 * t:2 * t + 2, 0:HEAD],
                                   ps[:, i].rearrange("p (c h d) -> p c h d", c=4, h=2),
                                   ACT.Copy).then_inc(v1_ready, 1)

                def normalise(u, s):
                    act.wait_ge(normed, u + 1)
                    act.activation(den[s][:], ps[HEAD:P, O_BANK + s], ACT.Ln).then_inc(ln_done, 1)
                    act.wait_ge(ln_done, u + 1)
                    act.activation(den[s][:], den[s][:], ACT.Exp, scale=-1.0).then_inc(rden_done, 1)

                for sq in SEQS:
                    def iteration(it, last):
                        for kv in range(NKV):
                            for kt in range(sq.n):
                                step = it * (4 * sq.n) + (sq.s0 + kv * sq.n + kt)
                                act.wait_ge(scored, step + 1)
                                act.wait_ge(plo_done, step + 1)
                                act.activation(p32[kt % QKP][:], ps[:, ST_BANK + kt % 2], ACT.Exp,
                                               scale=HEAD ** -0.5).then_inc(exp_done, 1)
                                if kt == LAG and not (isinstance(it, int) and it == 0 and kv == 0):
                                    act.wait_ge(pv_done, step + (1 + QKP - LAG))
                                    normalise(it * 4 + (sq.u0 + kv - 1), (kv + 1) % 2)
                    for_iterations(act, sq, iteration)
                    act.wait_ge(pv_done, sq.s0 + 4 * sq.iters * sq.n + QKP)
                    normalise(sq.u0 + 4 * sq.iters - 1, 1)

            @block.vector
            def _(dve):
                dve.sem_inc(max_found, 2)
                dve.sem_inc(normed, 2)
                dve.memset(f32(v1[:, :, :, HEAD:P]), 1.0).then_inc(ones_set, 1)
                dve.memset(f32(v2[:, :, :, HEAD:P]), 0.0)
                dve.memset(f32(k2[HEAD:HEAD + 1]), 1.0).then_inc(ones_set, 1)
                for i in range(6):
                    t, c = divmod(i, 3)
                    dve.wait_ge(v1_ready, i + 1)
                    dve.tensor_tensor(v2[:, 4 * c:4 * c + 4, 2 * t:2 * t + 2, 0:HEAD],
                                      ps[:, i].rearrange("p (c h d) -> p c h d", c=4, h=2),
                                      f32(v1[:, 4 * c:4 * c + 4, 2 * t:2 * t + 2, 0:HEAD]),
                                      ALU.subtract).then_inc(v2_ready, 1)

                def find_max(sq, u, s, j):
                    dve.wait_ge(max_mm, 4 * u + (j + 1))
                    if sq is A:
                        src = ps[:, MX_BANK + j]
                    else:
                        src = ps[:, MX_BANK + 2 * (j % 2):MX_BANK + 2 * (j % 2) + 2]
                    dve.tensor_reduce(nmax[s][:, j:j + 1], src, AX.X if sq is A else AX.XY, ALU.max,
                                      negate=True).then_inc(max_found, 1)

                def scale_out(u, s):
                    dve.wait_ge(rden_done, u + 1)
                    half = (u - s) * 8
                    dve.wait_ge(stored[s], half)
                    dve.tensor_tensor(o[s][:], ps[0:HEAD, O_BANK + s], den[s][:],
                                      ALU.mult).then_inc(normed, 1)

                for sq in SEQS:
                    for kv in range(2):
                        for j in range(4):
                            find_max(sq, sq.u0 + kv, kv, j)

                    def iteration(it, last):
                        for kv in range(NKV):
                            for kt in range(sq.n):
                                step = it * (4 * sq.n) + (sq.s0 + kv * sq.n + kt)
                                dve.wait_ge(exp_done, step + 3)
                                dve.wait_ge(pv_done, step + 1)
                                dve.tensor_copy(p_hi[kt % QKP][:], p32[kt % QKP][:]).then_inc(phi_done, 1)
                                if kt == LAG and not (isinstance(it, int) and it == 0 and kv == 0):
                                    scale_out(it * 4 + (sq.u0 + kv - 1), (kv + 1) % 2)
                                if looks_ahead(last, kv):
                                    per = sq.n // 4
                                    if kt % per == per - 1:
                                        find_max(sq, it * 4 + (sq.u0 + kv + 2), (kv + 2) % 4, kt // per)
                    for_iterations(dve, sq, iteration)
                    scale_out(sq.u0 + 4 * sq.iters - 1, 1)

            @block.tensor
            def _(pe):
                pe.sem_inc(pv_done, QKP)
                pe.wait_ge(v_in, 32)
                for i in range(6):
                    t, c = divmod(i, 3)
                    for j in range(4):
                        kt = 4 * c + j
                        mm = pe.transpose(ps[:, i, j * P:(j + 1) * P], v_raw[:, t, kt * P:(kt + 1) * P],
                                          ident[:])
                    mm.then_inc(v_turned, 1)
                pe.wait_ge(ones_set, 2)
                pe.wait_ge(v2_ready, 6)

                def max_part(sq, u, s, kt):
                    per = sq.n // 4
                    j, half = divmod(kt, per)
                    if half == 0:
                        pe.wait_ge(max_found, 4 * u + (j + 1))
                    bank = MX_BANK + (j if sq is A else 2 * (j % 2) + half)
                    key0 = (sq.kt0 + 4 * half) * P
                    mm = pe.matmul(ps[:, bank], q1[s][0:HEAD, j * P:(j + 1) * P],
                                   k1[0:HEAD, s, key0:key0 + BLK], start=True, stop=True)
                    if half == per - 1:
                        mm.then_inc(max_mm, 1)

                def output(sq, unit, s, kt, step):
                    pe.wait_ge(plo_done, step + 1 + QKP)
                    if kt == 0:
                        pe.wait_ge(normed, unit + 1)
                    out, tile = ps[:, O_BANK + s % 2], sq.kt0 + kt
                    first, last = kt == 0, kt == sq.n - 1
                    pe.matmul(out, v1[:, tile, s], p_hi[kt % QKP][:], start=first, stop=False)
                    pe.matmul(out, v2[:, tile, s], p_hi[kt % QKP][:], start=False, stop=False)
                    pe.matmul(out, v1[:, tile, s], p_lo[kt % QKP][:], start=False,
                              stop=last).then_inc(pv_done, 1)

                for n, sq in enumerate(SEQS):
                    pe.wait_ge(k_in[n], 48)
                    for kv in range(2):
                        pe.wait_ge(q_in[kv], 48 * (sq.u0 // 4 + 1))
                        for kt in range(sq.n):
                            max_part(sq, sq.u0 + kv, kv, kt)

                    def iteration(it, last):
                        for kv in range(NKV):
                            unit = it * 4 + (sq.u0 + kv)
                            ahead, s_ahead = unit + 2, (kv + 2) % 4
                            n_of = lambda k: it + (sq.u0 // 4 + 1 + (1 if k >= NKV else 0))
                            pe.wait_ge(nmax_in[kv], n_of(kv) * 64)
                            pe.wait_ge(q_in[kv], n_of(kv) * 48)
                            if looks_ahead(last, kv):
                                pe.wait_ge(q_in[s_ahead], n_of(kv + 2) * 48)
                            for kt in range(sq.n):
                                step = it * (4 * sq.n) + (sq.s0 + kv * sq.n + kt)
                                tile = sq.kt0 + kt
                                pe.wait_ge(exp_done, step + 1)
                                out = ps[:, ST_BANK + kt % 2]
                                keys = slice(tile * P, (tile + 1) * P)
                                pe.matmul(out, k1[:, kv, keys], q1[kv][:], start=True, stop=False)
                                pe.matmul(out, k2[0:HEAD + 1, kv, keys], q2[kv][0:HEAD + 1], start=False,
                                          stop=True).then_inc(scored, 1)
                                if looks_ahead(last, kv):
                                    max_part(sq, ahead, s_ahead, kt)
                                if kt >= LAG:
                                    output(sq, unit, kv, kt - LAG, step - LAG)
                                elif not (isinstance(it, int) and it == 0 and kv == 0):
                                    output(sq, unit - 1, (kv + 3) % 4, kt - LAG + sq.n, step - LAG)
                    for_iterations(pe, sq, iteration)
                    for kt in range(sq.n - LAG, sq.n):
                        output(sq, sq.u0 + 4 * sq.iters - 1, 3, kt, sq.s0 + (4 * sq.iters - 1) * sq.n + kt)


TAIL_T = 2 * KD + KD + 2 * (D_FF // P)
QUART = 8
MLP_ORDER = [("f1", 0), ("f1", 1), ("f2", 0), ("f1", 2), ("f2", 1), ("f1", 3), ("f2", 2), ("f2", 3)]


def tail(nc, mix, proj, x_t, w_tail, gain, ones_d, y_t):
    with ExitStack() as ctx:
        sb = lambda name, shape, dt=F32: ctx.enter_context(nc.sbuf_tensor(name, shape, dt))
        sem = lambda name: ctx.enter_context(nc.semaphore(name))
        h_hi = sb("t_hhi", [P, KD, BLK], F32R)
        h_lo = sb("t_hlo", [P, KD, BLK], F32R)
        y_hi = sb("t_yhi", [P, 4, BLK], F32R)
        y_lo = sb("t_ylo", [P, 4, BLK], F32R)
        a_hi = [sb(f"t_ahi{s}", [P, QUART, BLK], F32R) for s in range(2)]
        a_lo = [sb(f"t_alo{s}", [P, QUART, BLK], F32R) for s in range(2)]
        x1 = sb("t_x1", [P, KD, BLK])
        w_raw = [sb(f"t_wraw{s}", [P, KD, P]) for s in range(2)]
        w_hi = [sb(f"t_whi{s}", [P, KD, P], F32R) for s in range(2)]
        w_lo = [sb(f"t_wlo{s}", [P, KD, P], F32R) for s in range(2)]
        g_raw = [sb(f"t_graw{s}", [P, 2, BLK]) for s in range(2)]
        sg = [sb(f"t_sg{s}", [P, 2, BLK]) for s in range(2)]
        sgb = [sb(f"t_sgb{s}", [P, BLK]) for s in range(2)]
        ta = [sb(f"t_ta{s}", [P, BLK]) for s in range(2)]
        tb = [sb(f"t_tb{s}", [P, BLK]) for s in range(2)]
        tc = [sb(f"t_tc{s}", [P, BLK]) for s in range(2)]
        rs = sb("t_rs", [P, BLK])
        gn = sb("t_gain", [P, KD])
        eps = sb("t_eps", [P, 1])
        ones = sb("t_ones", [P, P])
        ps = ctx.enter_context(nc.psum_tensor("t_ps", [P, 8, BLK], F32))
        A_BANK, G_BANK, O_BANK, F1_BANK, F2_BANK, MEAN = 0, 2, 6, 0, 2, 4

        const_in = sem("t_const_in")
        eps_set = sem("t_eps_set")
        act_turn = sem("t_act_turn")
        w_in_s = [sem(f"t_w_in{s}") for s in range(2)]
        mix_in = [sem(f"t_mix_in{s}") for s in range(2)]
        g_in = [sem(f"t_g_in{s}") for s in range(2)]
        x1_in = sem("t_x1_in")
        y_out = sem("t_y_out")
        mixhi_ready = sem("t_mixhi_ready")
        mixlo_ready = sem("t_mixlo_ready")
        whi_ready = sem("t_whi_ready")
        wlo_ready = sem("t_wlo_ready")
        summed = sem("t_summed")
        sg_ready = sem("t_sg_ready")
        sgb_ready = sem("t_sgb_ready")
        merge_step = sem("t_merge_step")
        merged32 = sem("t_merged32")
        mhi_ready = sem("t_mhi_ready")
        mlo_ready = sem("t_mlo_ready")
        x1_ready = sem("t_x1_ready")
        hhi_ready = sem("t_hhi_ready")
        hlo_ready = sem("t_hlo_ready")
        sq_ready = sem("t_sq_ready")
        sq_used = sem("t_sq_used")
        ln_done = sem("t_ln_done")
        rs_ready = sem("t_rs_ready")
        relu_ready = sem("t_relu_ready")
        t_ready = sem("t_t_ready")
        tsq_ready = sem("t_tsq_ready")
        ahi_ready = sem("t_ahi_ready")
        alo_ready = sem("t_alo_ready")
        f2_added = sem("t_f2_added")

        S1, S2 = 0, 2 * KD
        MLP = S2 + KD
        SECT = [(kind, q, MLP + QUART * n) for n, (kind, q) in enumerate(MLP_ORDER)]
        PAIRS = QUART // 2
        N_MIX = 6
        PREFETCH = {("f2", 2): 0, ("f2", 3): PAIRS}
        H_FREE = MLP + QUART * (MLP_ORDER.index(("f1", 3)) + 1)

        def all_blocks(eng, one_block):
            with eng.Fori(0, NBLK - 1) as b:
                one_block(b, True)
            one_block(NBLK - 1, False)
        gates = proj[GA_T:GS_T + KD].rearrange("(t m) p n -> m p t n", t=2)

        with nc.Block() as block:

            @block.sync
            def _(sp):
                def load_w(j, s):
                    sp.dma_start(w_raw[s][:], w_tail[j]).then_inc(w_in_s[s], 16)

                def next_w(b, j, s):
                    sp.wait_ge(wlo_ready, b * TAIL_T + j + 3)
                    load_w(j + 2, s)

                sp.sem_inc(y_out, 16)
                sp.dma_start(gn[:], gain).then_inc(const_in, 16)
                sp.dma_start(ones[:], ones_d).then_inc(const_in, 16)
                load_w(0, 0)
                load_w(1, 1)

                def mix_chunk(b, c):
                    s, blk = c % 2, bass.ds(b * BLK, BLK)
                    if c < 2:
                        sp.wait_ge(sg_ready, b * KD + 1)
                    else:
                        sp.wait_ge(mixlo_ready, b * N_MIX + c - 1)
                    if c < N_MIX:
                        sp.dma_start(g_raw[s][:], mix[2 * c:2 * c + 2, :, blk].rearrange(
                            "k p n -> p k n")).then_inc(mix_in[s], 16)
                    else:
                        sp.dma_start(g_raw[s][:], gates[s][:, :, blk]).then_inc(g_in[s], 16)

                for c in range(N_MIX + 2):
                    mix_chunk(0, c)

                def one_block(b, more_blocks):
                    blk = bass.ds(b * BLK, BLK)
                    sp.wait_ge(y_out, b * KD * 16 + 16)
                    sp.dma_start(x1[:], x_t[b]).then_inc(x1_in, 16)

                    def merge_pair(i, more):
                        for s in range(2):
                            m = 2 * i + s
                            next_w(b, S1 + 2 * m, 0)
                            next_w(b, S1 + 2 * m + 1, 1)
                            if more:
                                sp.wait_ge(sg_ready, b * KD + m + 2)
                                sp.dma_start(g_raw[s][:], gates[m + 2][:, :, blk]).then_inc(g_in[s], 16)

                    with sp.Fori(0, KD // 2 - 1) as i:
                        merge_pair(i, True)
                    merge_pair(KD // 2 - 1, False)
                    with sp.Fori(0, (TAIL_T - S2 - 2 * QUART) // 2) as i:
                        for s in range(2):
                            next_w(b, 2 * i + (S2 + s), s)

                    def f2_pair(q, i, c=None):
                        for s in range(2):
                            next_w(b, 2 * i + (TAIL_T - QUART * (4 - q) + s), s)
                            if q == 3:
                                sp.wait_ge(f2_added, b * (4 * KD) + 2 * i + (3 * KD + s + 3))
                                sp.dma_start(y_t[b][:, 2 * i + s], x1[:, 2 * i + s]).then_inc(y_out, 16)
                        if c is not None:
                            mix_chunk(b + 1, c)

                    if more_blocks:
                        mix_chunk(b + 1, 0)
                        for n in range(2 * PAIRS):
                            f2_pair(2 + n // PAIRS, n % PAIRS, n + 1 if n + 1 < N_MIX + 2 else None)
                    else:
                        for q in (2, 3):
                            with sp.Fori(0, PAIRS) as i:
                                f2_pair(q, i)

                all_blocks(sp, one_block)
                sp.wait_ge(y_out, NBLK * KD * 16 + 16)
                for s in range(2):
                    sp.wait_ge(w_in_s[s], 16 * (NBLK * TAIL_T // 2 + 1))

            @block.gpsimd
            def _(pool):
                pool.sem_inc(wlo_ready, 2)
                with pool.Fori(0, NBLK * TAIL_T // 2 + 1) as i:
                    for s in range(2):
                        pool.wait_ge(whi_ready, 2 * i + (s + 1))
                        pool.wait_ge(w_in_s[s], 16 * i + 16)
                        pool.tensor_tensor(w_lo[s][:], w_raw[s][:], f32(w_hi[s][:]),
                                           ALU.subtract).then_inc(wlo_ready, 1)

            @block.scalar
            def _(act):
                act.preload_act_table(ACT.Sigmoid)
                act.sem_inc(relu_ready, 2)
                for sem_ in (sg_ready, mhi_ready, ahi_ready):
                    act.sem_inc(sem_, 1)

                def w_high(b, j, s):
                    act.wait_ge(w_in_s[s], b * (8 * TAIL_T) + (j - s) * 8 + 16)
                    act.wait_ge(summed, b * TAIL_T + j + 1)
                    act.activation(w_hi[s][:], w_raw[s][:], ACT.Copy).then_inc(whi_ready, 1)

                w_high(0, 0, 0)
                w_high(0, 1, 1)
                act.wait_ge(const_in, 32)
                act.wait_ge(eps_set, 1)

                def mix_high(b, c):
                    act.wait_ge(mix_in[c % 2], b * 48 + (c // 2 + 1) * 16)
                    dst = h_hi[:, 2 * c:2 * c + 2] if c < 4 else y_hi[:, 2 * c - 8:2 * c - 6]
                    act.activation(dst, g_raw[c % 2][:], ACT.Copy).then_inc(mixhi_ready, 1)

                for c in range(N_MIX):
                    mix_high(0, c)

                def one_block(b, more_blocks):
                    act.preload_act_table(ACT.Sigmoid)
                    with act.Fori(0, KD // 2) as i:
                        for s in range(2):
                            m = 2 * i + s
                            act.wait_ge(g_in[s], b * (8 * KD) + 16 * i + 16)
                            act.wait_ge(merged32, m + (b * KD + 1))
                            act.activation(sg[s][:], g_raw[s][:], ACT.Sigmoid).then_inc(sg_ready, 1)
                            w_high(b, 4 * i + (2 * s + 2), 0)
                            act.wait_ge(summed, b * TAIL_T + 4 * i + (2 * s + 4))
                            act.activation(sgb[s][:], ps[:, G_BANK + 2 * s + 1],
                                           ACT.Sigmoid).then_inc(sgb_ready, 1)
                            w_high(b, 4 * i + (2 * s + 3), 1)
                            act.wait_ge(merged32, b * KD + m + 2)
                            alone(act, act_turn)
                            act.activation(a_hi[0][:, m], tc[s][:], ACT.Copy).then_inc(mhi_ready, 1)
                    act.preload_act_table_set(LN_EXP)
                    with act.Fori(0, KD // 2) as i:
                        for s in range(2):
                            m = 2 * i + s
                            w_high(b, 2 * i + (S2 + 2 + s), s)
                            act.wait_ge(x1_ready, b * KD + m + 3)
                            alone(act, act_turn)
                            act.activation(h_hi[:, m], x1[:, m], ACT.Identity,
                                           scale=gn[:, bass.ds(m, 1)]).then_inc(hhi_ready, 1)
                            act.wait_ge(sq_used, b * KD + m + 1)
                            alone(act, act_turn)
                            act.activation(sgb[s][:], x1[:, m], ACT.Square).then_inc(sq_ready, 1)

                    for kind, q, j0 in SECT:
                        def pair(i, first=False):
                            for s in range(2):
                                j = 2 * i + (j0 + s)
                                f = 2 * i + (QUART * q + s)
                                if kind == "f1":
                                    act.wait_ge(summed, b * TAIL_T + j + 3)
                                    act.wait_ge(tsq_ready, b * (4 * QUART) + f + 1)
                                    act.activation(ta[s][:], ps[:, F1_BANK + s],
                                                   ACT.Relu).then_inc(relu_ready, 1)
                                w_high(b, j + 2, s)
                                if kind == "f1":
                                    if first and s == 0:
                                        act.wait_ge(sq_used, b * KD + KD + 2)
                                        act.activation(rs[:], ps[:, MEAN], ACT.Ln,
                                                       bias=eps[:, 0:1]).then_inc(ln_done, 1)
                                        act.wait_ge(ln_done, b + 1)
                                        act.activation(rs[:], rs[:], ACT.Exp,
                                                       scale=-0.5).then_inc(rs_ready, 1)
                                    act.wait_ge(t_ready, b * (4 * QUART) + f + 1)
                                    alone(act, act_turn)
                                    act.activation(a_hi[q % 2][:, 2 * i + s], tb[s][:],
                                                   ACT.Square).then_inc(ahi_ready, 1)
                        if (kind, q) == ("f1", 0):
                            pair(0, True)
                            with act.Fori(1, PAIRS) as i:
                                pair(i)
                        elif more_blocks and (kind, q) in PREFETCH:
                            for i in range(PAIRS):
                                pair(i)
                                c = PREFETCH[kind, q] + i
                                if c < N_MIX:
                                    act.wait_ge(summed, b * TAIL_T + H_FREE + 2)
                                    mix_high(b + 1, c)
                        else:
                            with act.Fori(0, PAIRS) as i:
                                pair(i)

                all_blocks(act, one_block)

            @block.vector
            def _(dve):
                dve.memset(eps[:], EPS).then_inc(eps_set, 1)
                for s_ in (x1_ready, alo_ready, f2_added):
                    dve.sem_inc(s_, 2)
                dve.sem_inc(merge_step, 6)
                for s_ in (merged32, mlo_ready, tsq_ready):
                    dve.sem_inc(s_, 1)
                dve.wait_ge(const_in, 32)

                def mix_low(b, c):
                    dst, hi = ((h_lo[:, 2 * c:2 * c + 2], h_hi[:, 2 * c:2 * c + 2]) if c < 4 else
                               (y_lo[:, 2 * c - 8:2 * c - 6], y_hi[:, 2 * c - 8:2 * c - 6]))
                    dve.wait_ge(mixhi_ready, b * N_MIX + c + 1)
                    dve.tensor_tensor(dst, g_raw[c % 2][:], f32(hi), ALU.subtract).then_inc(mixlo_ready, 1)

                for c in range(N_MIX):
                    mix_low(0, c)

                def one_block(b, more_blocks):
                    with dve.Fori(0, KD // 2) as i:
                        for s in range(2):
                            mm = b * KD + 2 * i + s
                            dve.wait_ge(sg_ready, mm + 2)
                            dve.wait_ge(summed, b * TAIL_T + 4 * i + (2 * s + 3))
                            dve.wait_ge(mhi_ready, mm + 1)
                            dve.wait_ge(mlo_ready, mm + 1)
                            dve.tensor_tensor(ta[s][:], ps[:, A_BANK + s], sg[s][:, 0],
                                              ALU.mult).then_inc(merge_step, 1)
                            dve.wait_ge(sgb_ready, mm + 1)
                            dve.tensor_tensor(tb[s][:], ps[:, G_BANK + 2 * s], sgb[s][:],
                                              ALU.mult).then_inc(merge_step, 1)
                            dve.wait_ge(merge_step, mm * 3 + 8)
                            dve.tensor_tensor(tb[s][:], tb[s][:], sg[s][:, 1], ALU.mult).then_inc(merge_step, 1)
                            dve.wait_ge(merge_step, mm * 3 + 9)
                            dve.tensor_tensor(tc[s][:], ta[s][:], tb[s][:], ALU.add).then_inc(merged32, 1)
                            dve.wait_ge(mhi_ready, mm + 2)
                            dve.tensor_tensor(a_lo[0][:, 2 * i + s], tc[s][:], f32(a_hi[0][:, 2 * i + s]),
                                              ALU.subtract).then_inc(mlo_ready, 1)
                    with dve.Fori(0, KD // 2) as i:
                        for s in range(2):
                            m = 2 * i + s
                            dve.wait_ge(x1_in, b * 16 + 16)
                            dve.wait_ge(summed, b * TAIL_T + 2 * i + (S2 + s + 3))
                            dve.tensor_tensor(x1[:, m], ps[:, O_BANK + s], x1[:, m],
                                              ALU.add).then_inc(x1_ready, 1)
                            dve.wait_ge(hhi_ready, b * KD + m + 1)
                            dve.scalar_tensor_tensor(h_lo[:, m], x1[:, m], gn[:, bass.ds(m, 1)],
                                                     f32(h_hi[:, m]), ALU.mult,
                                                     ALU.subtract).then_inc(hlo_ready, 1)
                    for kind, q, j0 in SECT:
                        def pair(i):
                            for s in range(2):
                                n = 2 * i + s
                                f = b * (4 * QUART) + 2 * i + (QUART * q + s)
                                if kind == "f1":
                                    if (q, s) == (0, 0):
                                        dve.wait_ge(rs_ready, b + 1)
                                    dve.wait_ge(relu_ready, f + 3)
                                    dve.wait_ge(ahi_ready, f + 1)
                                    dve.tensor_tensor(tb[s][:], ta[s][:], rs[:], ALU.mult).then_inc(t_ready, 1)
                                    dve.wait_ge(t_ready, f + 1)
                                    dve.wait_ge(alo_ready, f + 2)
                                    dve.tensor_tensor(tc[s][:], tb[s][:], tb[s][:],
                                                      ALU.mult).then_inc(tsq_ready, 1)
                                    dve.wait_ge(tsq_ready, f + 2)
                                    dve.wait_ge(ahi_ready, f + 2)
                                    dve.tensor_tensor(a_lo[q % 2][:, n], tc[s][:], f32(a_hi[q % 2][:, n]),
                                                      ALU.subtract).then_inc(alo_ready, 1)
                                else:
                                    dve.wait_ge(summed, b * TAIL_T + 2 * i + (j0 + s + 3))
                                    if q:
                                        dve.wait_ge(f2_added, f - 5)
                                    dve.tensor_tensor(x1[:, n], ps[:, F2_BANK + s], x1[:, n],
                                                      ALU.add).then_inc(f2_added, 1)
                        if more_blocks and (kind, q) in PREFETCH:
                            for i in range(PAIRS):
                                pair(i)
                                if PREFETCH[kind, q] + i < N_MIX:
                                    mix_low(b + 1, PREFETCH[kind, q] + i)
                        else:
                            with dve.Fori(0, PAIRS) as i:
                                pair(i)

                all_blocks(dve, one_block)

            @block.tensor
            def _(pe):
                pe.sem_inc(summed, 2)
                pe.sem_inc(sq_used, 2)
                pe.wait_ge(const_in, 32)

                def weights(b, j):
                    pe.wait_ge(whi_ready, b * TAIL_T + j + 1)
                    pe.wait_ge(wlo_ready, b * TAIL_T + j + 3)

                def product(bank, s, x_hi, x_lo, k0=0, n=KD, each=None, done=True):
                    for k in range(n):
                        if each:
                            each(k)
                        mm = three_products(pe, ps[:, bank], w_hi[s][:, k0 + k], w_lo[s][:, k0 + k],
                                            x_hi[:, k], x_lo[:, k], k == 0, k == n - 1)
                    if done:
                        mm.then_inc(summed, 1)

                def add_square(b, k, s):
                    pe.wait_ge(sq_ready, b * KD + k + 1)
                    pe.matmul(ps[:, MEAN], ones[:], sgb[s][:], start=isinstance(k, int) and k == 0,
                              stop=isinstance(k, int) and k == KD - 1, skip_group_check=True).then_inc(sq_used, 1)

                def one_block(b, more_blocks):
                    with pe.Fori(0, KD // 2) as i:
                        for s in range(2):
                            pe.wait_ge(mixlo_ready, b * N_MIX + N_MIX)
                            pe.wait_ge(f2_added, b * (4 * KD) + 2)
                            m = b * KD + 2 * i + s
                            pe.wait_ge(merge_step, m * 3 + 2)
                            weights(b, 4 * i + 2 * s)
                            product(A_BANK + s, 0, h_hi, h_lo)
                            weights(b, 4 * i + (2 * s + 1))
                            product(G_BANK + 2 * s, 1, y_hi, y_lo, 0, 4, done=False)
                            product(G_BANK + 2 * s + 1, 1, y_hi, y_lo, 4, 4)

                    def out_pair(i):
                        for s in range(2):
                            weights(b, 2 * i + (S2 + s))
                            pe.wait_ge(x1_ready, b * KD + 2 * i + (s + 1))
                            product(O_BANK + s, s, a_hi[0], a_lo[0], each=(
                                lambda k: pe.wait_ge(mlo_ready, b * KD + k + 2))
                                if (i, s) == (0, 0) else None)
                            if i and s == 0:
                                add_square(b, 2 * i - 2, 0)
                                add_square(b, 2 * i - 1, 1)

                    for i in range(KD // 2):
                        out_pair(i)

                    for kind, q, j0 in SECT:
                        def pair(i, first=False):
                            for s in range(2):
                                n = b * (4 * QUART) + 2 * i + (QUART * q + s)
                                weights(b, 2 * i + (j0 + s))
                                if kind == "f1":
                                    pe.wait_ge(relu_ready, n + 1)
                                    product(F1_BANK + s, s, h_hi, h_lo, each=(
                                        lambda k: pe.wait_ge(hlo_ready, b * KD + k + 1))
                                        if first and s == 0 else None)
                                    if first and s == 0 and q == 0:
                                        add_square(b, KD - 2, 0)
                                        add_square(b, KD - 1, 1)
                                else:
                                    pe.wait_ge(f2_added, n + 1)
                                    product(F2_BANK + s, s, a_hi[q % 2], a_lo[q % 2], each=(
                                        lambda k: pe.wait_ge(alo_ready, b * (4 * QUART) + QUART * q + k + 3))
                                        if first and s == 0 else None)
                        pair(0, True)
                        with pe.Fori(1, PAIRS) as i:
                            pair(i)

                all_blocks(pe, one_block)


def encoder_layer(nc, ap, y_t):
    scratch = lambda name, shape: nc.dram_tensor(name, shape, F32).ap()
    proj = scratch("proj_scratch", [PROJ_T, P, TOK])
    roped = scratch("roped_scratch", [2, NQ + NKV, HEAD, TOK])
    mix = scratch("mix_scratch", [12, P, TOK])
    with ExitStack() as ctx:
        sh = Shared(nc, ctx)
        project(nc, sh, ap["x_t"], ap["w_in_t"], ap["norm_mix_t"], ap["model_mean"], ap["qk_gain"],
                ap["head_mean"], ap["rope"], ap["lam"], ap["log_step"], ap["ssm_b"], ap["ssm_c"],
                ap["ssm_d_t"], ap["direction"], ap["identity"], proj, roped)
        gates_and_states(nc, sh, ap["w_in_t"], proj, mix)
    attention(nc, roped, proj, ap["identity"],
              mix[0:8].rearrange("t p n -> (t p) n").rearrange("(h d) n -> h d n", d=HEAD))
    tail(nc, mix, proj, ap["x_t"], ap["w_tail_t"], ap["norm_mlp_t"], ap["model_mean"], y_t)



def tiles(w):
    k, m = w.shape
    return w.reshape(k // P, P, m // P, P).transpose(2, 1, 0, 3)


def tail_stream(w_attn, w_glu_a, w_glu_b, w_out, w_ff1, w_ff2):
    attn, f1 = tiles(w_attn), tiles(w_ff1)
    glu = np.concatenate([tiles(w_glu_a), tiles(w_glu_b)], 2)
    f2 = tiles(w_ff2).reshape(KD, P, D_FF // P // QUART, QUART, P).transpose(2, 0, 1, 3, 4)
    parts = [np.stack([attn, glu], 1).reshape(2 * KD, P, KD, P), tiles(w_out)]
    parts += [f1[QUART * q:QUART * (q + 1)] if kind == "f1" else f2[q] for kind, q in MLP_ORDER]
    return np.ascontiguousarray(np.concatenate(parts + [attn[:1], glu[:1]], 0))


def token_order(length):
    return np.arange(length).reshape(length // CHUNK, CHUNK).T.reshape(-1)


def rope_tables():
    axis = HEAD // 2
    inv = (ROPE_THETA ** (-np.arange(0, axis, 2, dtype=np.float32) / np.float32(axis))).astype(np.float32)
    out = []
    for length in (LEN_A, LEN_B):
        t = token_order(length)
        ang = np.concatenate([(t // GRID_W)[None, :].astype(np.float32) * inv[:, None],
                              (t % GRID_W)[None, :].astype(np.float32) * inv[:, None]], 0)
        cos, sin = np.repeat(np.cos(ang), 2, 0), np.repeat(np.sin(ang), 2, 0)
        sin[0::2] *= -1
        out.append(np.tile(np.stack([cos, sin], 1), (2, 1, 1)))
    return np.ascontiguousarray(np.concatenate(out, 2).astype(np.float32))


def layouts(v):
    lay = np.ascontiguousarray
    g = lambda name: np.asarray(v[name])[0]
    x = np.concatenate([g("x_prompt")[token_order(LEN_A)], g("x_sample")[token_order(LEN_B)]], 0)
    eye = np.eye(P, dtype=np.float32)
    two = lambda a, b: np.stack([g(a), g(b)])
    return {
        "x_t": lay(x.reshape(NBLK, BLK, KD, P).transpose(0, 3, 2, 1)),
        "w_in_t": lay(tiles(g("w_in"))),
        "norm_mix_t": lay(g("norm_mix").reshape(KD, P).T),
        "norm_mlp_t": lay(g("norm_mlp").reshape(KD, P).T),
        "qk_gain": lay(np.tile(np.stack([g("q_norm"), g("k_norm")], 1), (2, 1))),
        "w_tail_t": tail_stream(g("w_attn_proj"), g("w_glu_a"), g("w_glu_b"), g("w_out"),
                                g("w_ff1"), g("w_ff2")),
        "lam": lay(two("ssm_lambda_re", "ssm_lambda_im").transpose(1, 3, 0, 2).reshape(P, 2, GROUPS)),
        "log_step": lay(np.repeat(g("ssm_log_step"), STATE, axis=0)),
        "ssm_b": lay(two("ssm_b_re", "ssm_b_im").transpose(1, 3, 0, 2, 4).reshape(P, 2, GROUPS, GC)),
        "ssm_c": lay(two("ssm_c_re", "ssm_c_im").transpose(1, 4, 0, 2, 3).reshape(P, 2, GROUPS, GC)),
        "ssm_d_t": lay(g("ssm_d").reshape(GROUPS, GC).T),
        "model_mean": np.full((P, P), 1.0 / D_MODEL, np.float32),
        "head_mean": lay(np.kron(np.eye(2), np.full((HEAD, HEAD), 1.0 / HEAD)).astype(np.float32)),
        "rope": rope_tables(),
        "direction": lay(np.repeat(np.array([1.0, -1.0], np.float32), STATE)[:, None]),
        "identity": eye,
    }


def kernel(**inputs):
    import concourse.bacc as bacc
    from concourse.bass_utils import run_bass_kernel_spmd

    arrays = layouts(inputs)
    nc = bacc.Bacc("TRN2", target_bir_lowering=False, num_devices=1)
    ap = {n: nc.dram_tensor(n, a.shape, F32, kind="ExternalInput").ap() for n, a in arrays.items()}
    y_t = nc.dram_tensor("y_t", (NBLK, P, KD, BLK), F32, kind="ExternalOutput").ap()
    encoder_layer(nc, ap, y_t)
    result = run_bass_kernel_spmd(nc, [arrays], core_ids=[0])
    y = np.asarray(result.results[0]["y_t"]).transpose(0, 3, 2, 1).reshape(TOK, D_MODEL)
    out = []
    for start, length in ((0, LEN_A), (LEN_A, LEN_B)):
        part = y[start:start + length].reshape(CHUNK, length // CHUNK, D_MODEL).transpose(1, 0, 2)
        out.append(np.ascontiguousarray(part.reshape(1, length, D_MODEL)))
    return tuple(out)
```

```python
import math
from contextlib import ExitStack

import numpy as np

import concourse.bass as bass
from concourse import mybir

ALU = mybir.AluOpType
ACT = mybir.ActivationFunctionType
AX = mybir.AxisListType
F32 = mybir.dt.float32
F32R = mybir.dt.float32r

P = 128
D_MODEL = 1024
D_FF = 4096
HEAD = 64
NQ, NKV = 16, 4
LEN_A, LEN_B = 512, 1024
TOK = LEN_A + LEN_B
BLK = 512
NBLK = TOK // BLK
KD = D_MODEL // P
EPS = 1e-6
GRID_W = 64
ROPE_THETA = 10000.0
CHUNK = 8
GROUPS, GC, STATE = 32, 16, 64
LN_EXP = "natural_log_exp_and_others"

Q_T, K_T, V_T, U_T, GA_T, GS_T = 0, 8, 10, 12, 16, 24
PROJ_T = 32


def f32(ap):
    return ap.bitcast(F32)


def alone(eng, turn):
    eng.sem_inc(turn, 1)


def three_products(pe, out, whi, wlo, xhi, xlo, start, stop):
    pe.matmul(out, whi, xhi, start=start, stop=False)
    pe.matmul(out, whi, xlo, start=False, stop=False)
    return pe.matmul(out, wlo, xhi, start=False, stop=stop)


SWAP = [i ^ 1 for i in range(32)]
QK_T = V_T


CH_A, CH_B = LEN_A // CHUNK, LEN_B // CHUNK
NCH = CH_A + CH_B
BATCH = 4
TWO_PI = 2 * math.pi
C1 = 6.28125
C2 = float((np.float32(TWO_PI - C1).view(np.uint32) & np.uint32(0xfffff000)).view(np.float32))
C3 = TWO_PI - C1 - C2
ROUND = 1.5 * 2.0 ** 23


class Stores:

    def __init__(self, nc, ctx):
        sem = lambda name: ctx.enter_context(nc.semaphore(name))
        self.u_v = [sem(f"stored_u_v{s}") for s in range(2)]
        self.gates = [sem(f"stored_gates{c}") for c in range(NBLK)]
        self.y = sem("stored_y")
        self.attention = [sem(f"stored_attention{s}") for s in range(2)]
        self.stage = [ctx.enter_context(nc.sbuf_tensor(f"stage{s}", [P, TOK], F32)) for s in range(2)]
        self.o = [ctx.enter_context(nc.sbuf_tensor(f"a_o{s}", [HEAD, BLK], F32)) for s in range(2)]


class Shared:

    def __init__(self, nc, ctx):
        sb = lambda name, shape, dt=F32: ctx.enter_context(nc.sbuf_tensor(name, shape, dt))
        self.x_hi = sb("x_hi", [P, NBLK, KD, BLK], F32R)
        self.x_lo = sb("x_lo", [P, NBLK, KD, BLK], F32R)
        self.rs = sb("x_rs", [P, TOK])
        self.w_raw = [sb(f"w_raw{s}", [P, KD, P]) for s in range(2)]
        self.w_hi = [sb(f"w_hi{s}", [P, KD, P], F32R) for s in range(2)]
        self.w_lo = [sb(f"w_lo{s}", [P, KD, P], F32R) for s in range(2)]
        self.slot = [sb(f"slot{s}", [P, KD * BLK]) for s in range(2)]
        self.ident = sb("s_ident", [P, P])
        self.dd = sb("s_d", [GC, GROUPS])
        self.ratio = sb("s_ratio", [P, GROUPS])
        G, at = GROUPS, 0
        parts = {}
        for name, size in (("cc", 2 * G * GC), ("bbar", 2 * G * GC), ("bw", 2 * G * GC), ("turn", 14 * G),
                           ("p_lag", 16 * G)):
            parts[name] = self.slot[0][:, at:at + size]
            at += size
        assert at <= KD * BLK
        self.cc, self.bbar, self.bw = (parts[n].rearrange("p (x g c) -> p x g c", x=2, g=G)
                                       for n in ("cc", "bbar", "bw"))
        self.turn = parts["turn"].rearrange("p (j x g) -> p j x g", j=7, x=2)
        self.p_lag = parts["p_lag"].rearrange("p (l x g) -> p l x g", l=8, x=2)


def project(nc, st, sh, x_t, w_in, gain, ones_d, qk_gain, head_mean_d, tables_d, lam_d, step_d, b_d, c_d, d_d,
            sign_d, ident_d, proj, roped):
    with ExitStack() as ctx:
        sb = lambda name, shape, dt=F32: ctx.enter_context(nc.sbuf_tensor(name, shape, dt))
        sem = lambda name: ctx.enter_context(nc.semaphore(name))
        x_hi, x_lo, rs, w_raw, w_hi, w_lo, stage = sh.x_hi, sh.x_lo, sh.rs, sh.w_raw, sh.w_hi, sh.w_lo, st.stage
        x = [sh.slot[b % 2][:].rearrange("p (k n) -> p k n", k=KD) for b in range(NBLK)]
        sq = sb("p1_sq", [P, 2, BLK])
        g = sb("p1_gain", [P, KD])
        eps = sb("p1_eps", [P, 1])
        ones = sb("p1_ones", [P, P])
        table = sh.slot[1][:, 0:2 * TOK].rearrange("p (x n) -> p x n", x=2)
        head_gain = sb("p1_head_gain", [P, 2])
        hmean = sb("p1_hmean", [P, P])
        head_rs, qn, sw = (sb(f"p1_{n}", [P, 2, BLK]) for n in ("head_rs", "qn", "sw"))
        r_hi, r_lo = (sb(f"p1_{n}", [P, 2, BLK], F32R) for n in ("r_hi", "r_lo"))
        sq_sum, pool_sum, pool_tmp = head_rs, sw, qn[:, 0]
        G = GROUPS
        lam = sb("s_lam", [P, 2, G])
        lstep = sb("s_lstep", [P, G])
        sign = sb("s_sign", [P, 1])
        half_pi = sb("s_half_pi", [P, 1])
        z = sb("s_z", [P, 2, G])
        lam_sq = sb("s_lam_sq", [P, G])
        tmp = sb("s_tmp", [P, 4, G])
        ang = sb("s_ang", [P, 2, G])
        mag = sb("s_mag", [P, G])
        unit = sb("s_unit", [P, 4, 2, G])
        pw = sb("s_pw", [P, 9, 2, G])
        fac = sb("s_fac", [P, 2, G])
        wf = sb("s_wf", [P, 2, G])
        bb_in = qn[:].rearrange("p s (g c) -> p s g c", g=G)
        tb = [sw[:, i].rearrange("p (g c) -> p g c", g=G) for i in range(2)]
        acc = ctx.enter_context(nc.psum_tensor("p1_acc", [P, 6, BLK], F32))
        mean = ctx.enter_context(nc.psum_tensor("p1_mean", [P, 2, BLK], F32))
        MEAN_BANK = (0, 1, 1)

        gain_in, ones_in = sem("p1_gain_in"), sem("p1_ones_in")
        rope_in = sem("p1_rope_in")
        x_in = [[sem(f"p1_x_in{b}_{j}") for j in range(4)] for b in range(NBLK)]
        w_in_s = [sem(f"p1_w_in{s}") for s in range(2)]
        eps_set = sem("p1_eps_set")
        act_sq = sem("p1_act_sq")
        act_added = sem("p1_act_added")
        pool_sq = sem("p1_pool_sq")
        x_mean = sem("p1_x_mean")
        ln_done = sem("p1_ln_done")
        rs_ready = sem("p1_rs_ready")
        xhi_ready = sem("p1_xhi_ready")
        xlo_ready = sem("p1_xlo_ready")
        whi_ready = sem("p1_whi_ready")
        wlo_ready = sem("p1_wlo_ready")
        summed = sem("p1_summed")
        evicted = sem("p1_evicted")
        stored = st.u_v
        hsq_ready = sem("p1_hsq_ready")
        hmean_ready = sem("p1_hmean_ready")
        hln_done = sem("p1_hln_done")
        hrs_ready = sem("p1_hrs_ready")
        qn_ready = sem("p1_qn_ready")
        sw_ready = sem("p1_sw_ready")
        cos_ready = sem("p1_cos_ready")
        sin_ready = sem("p1_sin_ready")
        sum_ready = sem("p1_sum_ready")
        hi_ready = sem("p1_hi_ready")
        lo_ready = sem("p1_lo_ready")
        roped_out = [sem(f"p1_roped_out{s}") for s in range(2)]
        dve_turn = sem("p1_dve_turn")
        par_in = sem("s_par_in")
        cc_in = sem("s_cc_in")
        b_in = sem("s_b_in")
        step_ready = sem("s_step_ready")
        angle_ready = sem("s_angle_ready")
        polar_ready = sem("s_polar_ready")
        d_done = sem("s_d_done")
        g_done = sem("s_g_done")

        QK_PAIRS = QK_T // 2
        PAIRS_ = GA_T // 2
        NQK = NBLK * QK_T
        cols = lambda b: slice(b * BLK, (b + 1) * BLK)

        def all_pairs(eng, pair):
            pair(0, False, True)
            with eng.Fori(1, QK_PAIRS) as i:
                pair(i, True, True)
            pair(QK_PAIRS, True, False)
            with eng.Fori(QK_PAIRS + 1, PAIRS_ - 1) as i:
                pair(i, False, False)
            pair(PAIRS_ - 1, False, False)

        def is_first(i):
            return isinstance(i, int) and i == 0

        MEAN_LAG = 5
        ACT_SQ = 5
        ACT_ADDS = ACT_SQ - 1
        POOL_STEPS = 2 * (KD - ACT_SQ) - 1

        def x_read(b, k):
            return (b * KD + k, b * ACT_SQ + min(k, ACT_SQ),
                    b * POOL_STEPS + max(0, 2 * (k - ACT_SQ) - (2 if k > ACT_SQ + 1 else 1) + 1))

        def has(i, r, behind, own):
            return own if r >= 0 else behind

        with nc.Block() as block:

            @block.sync
            def _(sp):
                def load_w(m, s):
                    sp.dma_start(w_raw[s][:], w_in[m]).then_inc(w_in_s[s], 16)

                load_w(0, 0)
                sp.dma_start(g[:], gain).then_inc(gain_in, 16)

                def load_x(b, j):
                    sp.dma_start(x[b][:, 2 * j:2 * j + 2], x_t[b][:, 2 * j:2 * j + 2]).then_inc(x_in[b][j], 16)

                def wait_read(b, k):
                    for sem_, count in zip((xlo_ready, act_sq, pool_sq), x_read(b, k)):
                        if count:
                            sp.wait_ge(sem_, count)

                for j in range(4):
                    load_x(0, j)
                for j in range(4):
                    load_x(1, j)
                load_w(1, 1)
                sp.dma_start(ones[:], ones_d).then_inc(ones_in, 16)
                for dst, src in ((lam, lam_d), (lstep, step_d), (sign, sign_d), (sh.dd, d_d), (sh.ident, ident_d)):
                    sp.dma_start(dst[:], src).then_inc(par_in, 16)
                sp.dma_start(hmean[:], head_mean_d).then_inc(rope_in, 16)
                sp.dma_start(head_gain[:], qk_gain).then_inc(rope_in, 16)
                for j in range(4):
                    wait_read(0, 2 * j + 2)
                    load_x(2, j)
                wait_read(1, KD)
                sp.dma_start(table, tables_d).then_inc(rope_in, 16)
                wait_read(2, KD)
                sp.dma_start(sh.cc, c_d).then_inc(cc_in, 16)

                def pair(i, behind, own):
                    for s in range(2):
                        sp.wait_ge(wlo_ready, 2 * i + (s + 1))
                        load_w(2 * i + s + 2, s)
                        if behind:
                            for b in range(NBLK):
                                r = 3 * s + b - 6
                                sp.wait_ge(lo_ready, 6 * i + (r + 1))
                                for l, part in enumerate((r_hi, r_lo)):
                                    sp.dma_start(roped[bass.ds(4 * i + (2 * s - 4), 2), l, :, cols(b)],
                                                 f32(part[:, r % 2])).then_inc(roped_out[r % 2], 16)
                    if behind and not own:
                        sp.wait_ge(lo_ready, NQK)
                        sp.dma_start(bb_in, b_d).then_inc(b_in, 16)
                    for s in range(2) if not own else ():
                        sp.wait_ge(evicted, 6 * i + (6 + 3 * s + 3))
                        sp.dma_start(proj[2 * i + s], stage[s][:]).then_inc(stored[s], 16)

                all_pairs(sp, pair)
                for s in range(2):
                    sp.wait_ge(roped_out[s], 16 * NQK)
                sp.wait_ge(b_in, 16)
                sp.wait_ge(cc_in, 16)

            @block.scalar
            def _(act):
                act.preload_act_table_set(LN_EXP)
                act.sem_inc(hln_done, 1)
                act.wait_ge(gain_in, 16)
                act.wait_ge(eps_set, 2)

                def high(s, count):
                    act.wait_ge(w_in_s[s], count)
                    act.activation(w_hi[s][:], w_raw[s][:], ACT.Copy).then_inc(whi_ready, 1)

                def split(b, k):
                    act.wait_ge(x_in[b][k // 2], 16)
                    act.activation(x_hi[:, b, k], x[b][:, k], ACT.Identity,
                                   scale=g[:, k:k + 1]).then_inc(xhi_ready, 1)

                def square(b, k):
                    if k == 0:
                        if b == 2:
                            act.wait_ge(x_mean, 1)
                        act.activation(sq_sum[:, b % 2], x[b][:, k], ACT.Square).then_inc(act_sq, 1)
                        return
                    if b or k > 2:
                        act.wait_ge(act_added, b * ACT_ADDS + k - 2)
                    act.activation(sq[:, k % 2], x[b][:, k], ACT.Square).then_inc(act_sq, 1)

                high(0, 16)
                for b in range(NBLK):
                    for k in range(KD):
                        split(b, k)
                        if b == 0 and k < ACT_SQ:
                            square(b, k)
                        if b == 1 and k == 1:
                            high(b, 16)
                    if b == 1:
                        for k in range(ACT_SQ):
                            square(b, k)
                for k in range(ACT_SQ):
                    square(2, k)
                act.wait_ge(summed, 3)
                high(0, 32)
                for b in range(NBLK):
                    act.wait_ge(x_mean, b + 1)
                    act.activation(rs[:, cols(b)], mean[:, MEAN_BANK[b]], ACT.Ln,
                                   bias=eps[:, 0:1]).then_inc(ln_done, 1)
                    act.wait_ge(ln_done, b + 1)
                    act.activation(rs[:, cols(b)], rs[:, cols(b)],
                                   ACT.Exp, scale=-0.5).then_inc(rs_ready, 1)

                def pair(i, behind, own):
                    first, last = is_first(i), isinstance(i, int) and i == PAIRS_ - 1
                    if behind and not own:
                        act.wait_ge(angle_ready, 1)
                        act.activation(mag[:], z[:, 0], ACT.Exp).then_inc(polar_ready, 1)
                        act.activation(sh.ratio[:], z[:, 0], ACT.Exp, scale=float(CHUNK)).then_inc(polar_ready, 1)
                        act.activation(unit[:, 0, 1], ang[:, 0], ACT.Sin).then_inc(polar_ready, 1)
                        act.activation(unit[:, 0, 0], ang[:, 1], ACT.Sin, scale=-1.0,
                                       bias=half_pi[:, 0:1]).then_inc(polar_ready, 1)
                    for r in range(6):
                        if has(i, r, behind, own):
                            act.wait_ge(evicted, 6 * i + (6 + r + 1))
                            if not first or r >= 2:
                                act.wait_ge(hmean_ready, 6 * i + (r - 1))
                            act.activation(sq[:, r % 2], stage[r // 3][:, cols(r % 3)],
                                           ACT.Square).then_inc(hsq_ready, 1)
                        k = r - 1
                        if has(i, k, behind, own):
                            act.wait_ge(hmean_ready, 6 * i + (k + 1))
                            if not first or k >= 2:
                                act.wait_ge(qn_ready, 6 * i + (k - 1))
                            act.activation(head_rs[:, k % 2], mean[:, k % 2], ACT.Ln,
                                           bias=eps[:, 0:1]).then_inc(hln_done, 1)
                            act.wait_ge(hln_done, 6 * i + (k + 2))
                            act.activation(head_rs[:, k % 2], head_rs[:, k % 2], ACT.Exp,
                                           scale=-0.5).then_inc(hrs_ready, 1)
                        k = r - 2
                        if has(i, k, behind, own):
                            act.wait_ge(sum_ready, 6 * i + (k + 1))
                            if not first or k >= 2:
                                act.wait_ge(roped_out[k % 2], 96 * i + 32 * (k // 2))
                            act.activation(r_hi[:, k % 2], qn[:, k % 2], ACT.Copy).then_inc(hi_ready, 1)
                        if r == 2:
                            act.wait_ge(summed, 6 * i + 6)
                            high(1, 16 * i + 32)
                        if r == 5 and not last:
                            act.wait_ge(summed, 6 * i + 9)
                            high(0, 16 * i + 48)
                    if first:
                        act.wait_ge(par_in, 16 * 5)
                        act.activation(lstep[:], lstep[:], ACT.Exp).then_inc(step_ready, 1)

                all_pairs(act, pair)

            @block.gpsimd
            def _(pool):
                steps = 0
                for b in range(NBLK):
                    total = pool_sum[:, b % 2]
                    if b == 2:
                        pool.wait_ge(x_mean, 1)
                    for k in range(ACT_SQ, KD):
                        pool.wait_ge(x_in[b][k // 2], 16)
                        first = k == ACT_SQ
                        pool.tensor_tensor(total if first else pool_tmp, x[b][:, k], x[b][:, k],
                                           ALU.mult).then_inc(pool_sq, 1)
                        steps += 1
                        pool.wait_ge(pool_sq, steps)
                        if not first:
                            pool.tensor_tensor(total, total, pool_tmp, ALU.add).then_inc(pool_sq, 1)
                            steps += 1
                            pool.wait_ge(pool_sq, steps)
                pool.wait_ge(rope_in, 48)
                with pool.Fori(0, QK_PAIRS) as i:
                    for r in range(6):
                        pool.wait_ge(sw_ready, 6 * i + (r + 1))
                        pool.tensor_tensor(sw[:, r % 2], sw[:, r % 2], table[:, 1, cols(r % 3)],
                                           ALU.mult).then_inc(sin_ready, 1)

                n_link = [0]

                def link(ins):
                    n_link[0] += 1
                    ins.then_inc(g_done, 1)
                    pool.wait_ge(g_done, n_link[0])

                def tt(out, a, b, op):
                    link(pool.tensor_tensor(out, a, b, op))

                def cmul(out, a, b, t):
                    tt(t[0], a[0], b[0], ALU.mult)
                    tt(t[1], a[1], b[1], ALU.mult)
                    tt(t[2], a[0], b[1], ALU.mult)
                    tt(t[3], a[1], b[0], ALU.mult)
                    tt(out[0], t[0], t[1], ALU.subtract)
                    tt(out[1], t[2], t[3], ALU.add)

                T4 = [tmp[:, i] for i in range(4)]
                both = lambda t: (t[:, 0], t[:, 1])
                turn, p_lag = sh.turn, sh.p_lag
                one, lb = (pw[:, 0, 0], pw[:, 0, 1]), (pw[:, 1, 0], pw[:, 1, 1])
                link(pool.memset(one[0], 1.0))
                link(pool.memset(one[1], 0.0))
                pool.wait_ge(polar_ready, 4)
                for i in range(2):
                    tt(lb[i], unit[:, 0, i], mag[:], ALU.mult)
                for n in (1, 2, 4):
                    for j in range(n):
                        cmul(both(pw[:, n + 1 + j]), both(pw[:, 1 + j]), both(pw[:, n]), T4)
                for i in range(3):
                    cmul(both(unit[:, i + 1]), both(unit[:, i]), both(unit[:, i]), T4)
                pool.wait_ge(cc_in, 16)
                link(pool.tensor_copy(turn[:, 0, 0], unit[:, 3, 0]))
                tt(turn[:, 0, 1], unit[:, 3, 1], sign[:, 0:1].broadcast_to([P, G]), ALU.mult)
                for j in range(6):
                    cmul(both(turn[:, j + 1]), both(turn[:, j]), both(turn[:, j]), T4)
                tt(T4[0], lb[0], one[0], ALU.subtract)
                tt(T4[1], T4[0], lam[:, 0], ALU.mult)
                tt(T4[2], lb[1], lam[:, 1], ALU.mult)
                tt(fac[:, 0], T4[1], T4[2], ALU.add)
                tt(T4[1], lb[1], lam[:, 0], ALU.mult)
                tt(T4[2], T4[0], lam[:, 1], ALU.mult)
                tt(fac[:, 1], T4[1], T4[2], ALU.subtract)
                for i in range(2):
                    tt(fac[:, i], fac[:, i], lam_sq[:], ALU.mult)
                e8 = unit[:, 3]
                tt(T4[0], lb[0], e8[:, 0], ALU.mult)
                tt(T4[1], lb[1], e8[:, 1], ALU.mult)
                tt(wf[:, 0], T4[0], T4[1], ALU.add)
                tt(T4[0], lb[1], e8[:, 0], ALU.mult)
                tt(T4[1], lb[0], e8[:, 1], ALU.mult)
                tt(wf[:, 1], T4[0], T4[1], ALU.subtract)
                for l in range(8):
                    link(pool.tensor_copy(p_lag[0:64, l], pw[0:64, l]))
                    link(pool.tensor_copy(p_lag[64:128, l], pw[64:128, 7 - l]))
                wide_of = lambda t: tuple(t[:, i].unsqueeze(2).broadcast_to([P, G, GC]) for i in range(2))
                f2, w2 = wide_of(fac), wide_of(wf)
                pool.wait_ge(b_in, 16)
                for out, a, f in ((sh.bbar, bb_in, f2), (sh.bw, sh.bbar, w2)):
                    for i, (x_, y_, op) in enumerate(((0, 1, ALU.subtract), (1, 0, ALU.add))):
                        tt(tb[0], a[:, 0], f[x_], ALU.mult)
                        tt(tb[1], a[:, 1], f[y_], ALU.mult)
                        tt(out[:, i], tb[0], tb[1], op)

            @block.vector
            def _(dve):
                dve.memset(eps[:], EPS).then_inc(eps_set, 1)
                dve.memset(half_pi[:], math.pi / 2).then_inc(eps_set, 1)
                dve.sem_inc(evicted, 6)

                def low(s, count):
                    dve.wait_ge(whi_ready, count)
                    dve.tensor_tensor(w_lo[s][:], w_raw[s][:], f32(w_hi[s][:]),
                                      ALU.subtract).then_inc(wlo_ready, 1)

                dve.wait_ge(gain_in, 16)

                def split(b, k):
                    dve.wait_ge(xhi_ready, b * KD + k + 1)
                    dve.scalar_tensor_tensor(x_lo[:, b, k], x[b][:, k], g[:, k:k + 1],
                                             f32(x_hi[:, b, k]), ALU.mult,
                                             ALU.subtract).then_inc(xlo_ready, 1)

                def add_square(b, k):
                    dve.wait_ge(act_sq, b * ACT_SQ + k + 1)
                    if b or k > 1:
                        dve.wait_ge(act_added, b * ACT_ADDS + k - 1)
                    dve.tensor_tensor(sq_sum[:, b % 2], sq_sum[:, b % 2], sq[:, k % 2],
                                      ALU.add).then_inc(act_added, 1)

                low(0, 1)
                for b in range(NBLK):
                    for k in range(KD):
                        split(b, k)
                        if b == 0 and 1 <= k < ACT_SQ:
                            add_square(b, k)
                        if b == 1 and k == 1:
                            low(b, b + 1)
                    if b == 1:
                        for k in range(1, ACT_SQ):
                            add_square(b, k)
                for k in range(1, ACT_SQ):
                    add_square(2, k)
                dve.wait_ge(rope_in, 48)

                def rope(i, r, kind):
                    n, s, tok = 6 * i, r % 2, cols(r % 3)
                    early = is_first(i) and r < 2
                    dve.wait_ge(hrs_ready, n + (r + 1))
                    if not early:
                        dve.wait_ge(lo_ready, n + (r - 1))
                    dve.scalar_tensor_tensor(qn[:, s], stage[r % 6 // 3][:, tok], head_gain[:, kind:kind + 1],
                                             head_rs[:, s], ALU.mult, ALU.mult).then_inc(qn_ready, 1)
                    dve.wait_ge(qn_ready, n + (r + 1))
                    alone(dve, dve_turn)
                    dve.stream_shuffle(sw[:, s], qn[:, s], SWAP).then_inc(sw_ready, 1)
                    dve.wait_ge(sw_ready, n + (r + 1))
                    dve.tensor_tensor(qn[:, s], qn[:, s], table[:, 0, tok], ALU.mult).then_inc(cos_ready, 1)
                    dve.wait_ge(cos_ready, n + (r + 1))
                    dve.wait_ge(sin_ready, n + (r + 1))
                    dve.tensor_tensor(qn[:, s], qn[:, s], sw[:, s], ALU.add).then_inc(sum_ready, 1)
                    dve.wait_ge(hi_ready, n + (r + 1))
                    dve.tensor_tensor(r_lo[:, s], qn[:, s], f32(r_hi[:, s]), ALU.subtract).then_inc(lo_ready, 1)

                def pair(i, behind, own, kinds=(0, 0)):
                    first = is_first(i)
                    for r in range(6):
                        s, b = divmod(r, NBLK)
                        dve.wait_ge(summed, 6 * i + (r + 1))
                        if b == 0 and not own and not (isinstance(i, int) and i == QK_PAIRS):
                            dve.wait_ge(stored[s], 16 * i - 16 * QK_PAIRS)
                        if first:
                            dve.wait_ge(rs_ready, min(r + 1, NBLK))
                        dve.tensor_tensor(stage[s][:, cols(b)], acc[:, r], rs[:, cols(b)],
                                          ALU.mult).then_inc(evicted, 1)
                        if has(i, r - 2, behind, own):
                            rope(i, r - 2, kinds[int(r >= 2)])
                        if b == 0:
                            low(s, 2 * i + (s + 3))

                def angles():
                    n_link = [0]

                    def link(ins):
                        n_link[0] += 1
                        ins.then_inc(d_done, 1)
                        dve.wait_ge(d_done, n_link[0])

                    T = [tmp[:, i] for i in range(4)]
                    dve.wait_ge(step_ready, 1)
                    for i in range(2):
                        link(dve.tensor_tensor(z[:, i], lam[:, i], lstep[:], ALU.mult))
                    link(dve.tensor_scalar(T[0], z[:, 1], 1 / TWO_PI, ROUND, ALU.mult, ALU.add))
                    link(dve.tensor_scalar(T[0], T[0], -ROUND, None, ALU.add))
                    link(dve.scalar_tensor_tensor(ang[:, 0], T[0], -C1, z[:, 1], ALU.mult, ALU.add))
                    link(dve.scalar_tensor_tensor(ang[:, 0], T[0], -C2, ang[:, 0], ALU.mult, ALU.add))
                    link(dve.scalar_tensor_tensor(ang[:, 0], T[0], -C3, ang[:, 0], ALU.mult, ALU.add))
                    link(dve.tensor_scalar(ang[:, 0], ang[:, 0], 3.1415925, -3.1415925, ALU.min, ALU.max))
                    link(dve.scalar_tensor_tensor(ang[:, 1], ang[:, 0], -1.0, ang[:, 0], ALU.mult, ALU.max))
                    link(dve.tensor_tensor(T[1], lam[:, 0], lam[:, 0], ALU.mult))
                    link(dve.tensor_tensor(T[2], lam[:, 1], lam[:, 1], ALU.mult))
                    link(dve.tensor_tensor(T[3], T[1], T[2], ALU.add))
                    dve.reciprocal(lam_sq[:], T[3]).then_inc(angle_ready, 1)

                pair(0, False, True)
                angles()
                with dve.Fori(1, K_T // 2) as i:
                    pair(i, True, True)
                pair(K_T // 2, True, True, (0, 1))
                pair(QK_PAIRS, True, False, (1, 1))
                with dve.Fori(QK_PAIRS + 1, PAIRS_) as i:
                    pair(i, False, False)

            @block.tensor
            def _(pe):
                def x_means(b):
                    if b == 0:
                        pe.wait_ge(ones_in, 16)
                    if b == 2:
                        pe.wait_ge(ln_done, 2)
                    pe.wait_ge(act_added, ACT_ADDS * (b + 1))
                    pe.wait_ge(pool_sq, POOL_STEPS * (b + 1))
                    pe.matmul(mean[:, MEAN_BANK[b]], ones[:], sq_sum[:, b % 2], start=True, stop=False)
                    pe.matmul(mean[:, MEAN_BANK[b]], ones[:], pool_sum[:, b % 2], start=False,
                              stop=True).then_inc(x_mean, 1)

                def head_mean(i, k):
                    pe.wait_ge(hsq_ready, 6 * i + (k + 1))
                    if is_first(i):
                        pe.wait_ge(rs_ready, NBLK)
                    else:
                        pe.wait_ge(hln_done, 6 * i + k)
                    pe.matmul(mean[:, k % 2], hmean[:], sq[:, k % 2], start=True,
                              stop=True).then_inc(hmean_ready, 1)

                def pair(i, behind, own):
                    first = is_first(i)
                    for r in range(6):
                        s, b = divmod(r, NBLK)
                        if b == 0:
                            pe.wait_ge(whi_ready, 2 * i + (s + 1))
                            pe.wait_ge(wlo_ready, 2 * i + (s + 1))
                        pe.wait_ge(evicted, 6 * i + (r + 1))
                        for k in range(KD):
                            if first and s == 0:
                                pe.wait_ge(xlo_ready, KD * b + k + 1)
                            mm = three_products(pe, acc[:, r], w_hi[s][:, k], w_lo[s][:, k],
                                                x_hi[:, b, k], x_lo[:, b, k], k == 0, k == KD - 1)
                        mm.then_inc(summed, 1)
                        if first and r in (1, 2, 4):
                            x_means((1, 2, 4).index(r))
                        if has(i, r - MEAN_LAG, behind, own):
                            if first:
                                pe.wait_ge(rope_in, 48)
                            head_mean(i, r - MEAN_LAG)

                all_pairs(pe, pair)


def gates_and_states(nc, st, sh, w_in, proj, mix):
    with ExitStack() as ctx:
        sb = lambda name, shape, dt=F32: ctx.enter_context(nc.sbuf_tensor(name, shape, dt))
        sem = lambda name: ctx.enter_context(nc.semaphore(name))
        N = BATCH * NCH
        w_raw, w_hi, w_lo, stage = sh.w_raw, sh.w_hi, sh.w_lo, st.stage[0]
        out_w = sb("s_outw", [P, 2, BATCH, 8, GC])
        in_t = sb("s_int", [P, 2, BATCH, 8, GC])
        in_w = sb("s_inw", [P, 2, BATCH, P])
        resp = sb("s_resp", [GC, BATCH, 15, GC])
        rot = sb("s_rot", [P, 2, BATCH, NCH])
        decay = sb("s_decay", [P, BATCH, NCH])
        gs = [sb(f"s_gs{i}", [P, N + 2]) for i in range(2)]
        bbar_b = sb("s_bbar_b", [P, 2, BATCH, GC])
        turn_b = sb("s_turn_b", [P, 7, 2, BATCH])
        ratio_b = sb("s_ratio_b", [P, BATCH])
        p_lag = sb("s_plag_b", [P, 8, 2, BATCH])
        diag = sb("s_diag", [GC, BATCH, GC])
        groups = lambda ap: ap.rearrange("p (g k) -> p g k", g=BATCH)
        u = groups(st.stage[1][:, 0:N])
        y = groups(st.stage[1][:, N:2 * N])
        scratch = sh.slot[1]
        gin = [scratch[:, i * N:(i + 1) * N] for i in range(2)]
        gt = [scratch[:, (2 + i) * N:(3 + i) * N] for i in range(2)]
        wide = [t[:, 0:BATCH * 8 * GC].rearrange("p (g l c) -> p g l c", g=BATCH, l=8) for t in gt]
        at = 4 * N
        local = scratch[:, at:at + BATCH * P].rearrange("p (g c) -> p g c", g=BATCH)
        rt = [groups(scratch[:, at + BATCH * (P + i * 64):at + BATCH * (P + (i + 1) * 64)]) for i in range(2)]
        ps = ctx.enter_context(nc.psum_tensor("s_ps", [P, 8, BLK], F32))
        S_BANK, Y_BANK, G_BANK = 0, 4, 6

        u_in = sem("s_u_in")
        local_in = sem("s_local_in")
        y_out = st.y
        d_done = sem("s_d2_done")
        g_done = sem("s_g2_done")
        par_ready = sem("s_par_ready")
        in_ready = sem("s_in_ready")
        out_ready = sem("s_out_ready")
        t_done = sem("s_t_done")
        t_read = sem("s_t_read")
        s_done = sem("s_s_done")
        r_done = sem("s_r_done")
        resp_ready = sem("s_resp_ready")
        rot_ready = sem("s_rot_ready")
        decay_ready = sem("s_decay_ready")
        h_ready = sem("s_h_ready")
        y_done = sem("s_y_done")
        y_ready = sem("s_y_ready")
        pool_turn, pe_turn = sem("s_pool_turn"), sem("s_pe_turn")
        w_in_s = [sem(f"g_w_in{s}") for s in range(2)]
        whi_ready = sem("g_whi_ready")
        wlo_ready = sem("g_wlo_ready")
        summed = sem("g_summed")
        evicted = sem("g_evicted")
        scaled = sem("g_scaled")
        stored = st.gates

        BATCHES = GROUPS // BATCH
        GB = 2 * NBLK
        cols = lambda c: slice(c * BLK, (c + 1) * BLK)
        D_LINKS, G_LINKS = 40, 49

        def all_batches(eng, batch):
            with eng.Fori(0, BATCHES - 1) as b:
                batch(b, True)
            batch(BATCHES - 1, False)

        with nc.Block() as block:

            @block.sync
            def _(sp):
                seqs = ((0, 0, CH_A), (LEN_A, CH_A, CH_B))
                by_channel = lambda t: t.rearrange("t p n -> (t p) n").rearrange("(g c) n -> c g n", c=GC)
                u_src, y_dst = by_channel(proj[U_T:U_T + 4]), by_channel(mix[8:12])

                def load_u(b):
                    for t in range(CHUNK):
                        for pos, k0, n in seqs:
                            sp.dma_start(u[t * GC:(t + 1) * GC, :, k0:k0 + n],
                                         u_src[:, bass.ds(b * BATCH, BATCH), pos + t * n:pos + (t + 1) * n]
                                         ).then_inc(u_in, 16)

                sp.sem_inc(y_out, 16)
                for c in range(NBLK):
                    sp.sem_inc(stored[c], 16)
                for s in range(2):
                    sp.wait_ge(st.u_v[s], 16 * (GA_T - QK_T) // 2)
                load_u(0)

                def batch(b, more):
                    def store_gate(r):
                        sp.wait_ge(scaled, GB * b + (r + 1))
                        sp.dma_start(proj[2 * b + (GA_T + r // NBLK)][:, cols(r % NBLK)],
                                     stage[:, cols(r % NBLK)]).then_inc(stored[r % NBLK], 16)

                    if more:
                        for s in range(2):
                            sp.wait_ge(wlo_ready, 2 * b + (s + 1))
                            sp.dma_start(w_raw[s][:], w_in[2 * b + (GA_T + 2 + s)]).then_inc(w_in_s[s], 16)
                    store_gate(0)
                    store_gate(1)
                    sp.wait_ge(resp_ready, b + 1)
                    for s in range(CHUNK):
                        sp.dma_start(local[s * GC:(s + 1) * GC],
                                     resp[:, :, 7 - s:15 - s].rearrange("p g l c -> p g (l c)")
                                     ).then_inc(local_in, 16)
                    for r in (2, 3, 4):
                        store_gate(r)
                    if more:
                        sp.wait_ge(y_done, b + 2)
                        load_u(b + 1)
                    sp.wait_ge(y_ready, b + 2)
                    for t in range(CHUNK):
                        for pos, k0, n in seqs:
                            sp.dma_start(y_dst[:, bass.ds(b * BATCH, BATCH), pos + t * n:pos + (t + 1) * n],
                                         y[t * GC:(t + 1) * GC, :, k0:k0 + n]).then_inc(y_out, 16)
                    store_gate(5)

                all_batches(sp, batch)

            @block.scalar
            def _(act):
                act.preload_act_table(ACT.Gelu_apprx_tanh)
                act.sem_inc(whi_ready, 2)
                act.sem_inc(evicted, 2)
                for s in range(2):
                    act.wait_ge(st.u_v[s], 16 * (GA_T - QK_T) // 2)
                act.sem_inc(y_ready, 1)

                def batch(b, more):
                    def evict(r):
                        act.wait_ge(summed, GB * b + (r + 1))
                        act.wait_ge(stored[r % NBLK], 32 * b + 16 * (r // NBLK) + 16)
                        act.activation(stage[:, cols(r % NBLK)], ps[:, G_BANK + r % 2],
                                       ACT.Copy).then_inc(evicted, 1)

                    def high(s):
                        act.wait_ge(w_in_s[s], 16 * b + 16)
                        act.activation(w_hi[s][:], w_raw[s][:], ACT.Copy).then_inc(whi_ready, 1)

                    evict(0)
                    for i in range(2):
                        act.wait_ge(t_done, 2 * b + (i + 1))
                        act.activation(in_w[:, i], ps[:, S_BANK + i].rearrange("p (g c) -> p g c", g=BATCH),
                                       ACT.Copy).then_inc(t_read, 1)
                    evict(1)
                    evict(2)
                    if more:
                        high(0)
                    evict(3)
                    evict(4)
                    act.wait_ge(y_done, b + 2)
                    act.wait_ge(y_out, 16 * 2 * CHUNK * b + 16)
                    act.activation(y.rearrange("p (b g) k -> p b g k", b=2),
                                   ps[:, Y_BANK:Y_BANK + 2, 0:2 * NCH].rearrange("p b (g k) -> p b g k", g=2),
                                   ACT.Gelu_apprx_tanh).then_inc(y_ready, 1)
                    evict(5)
                    if more:
                        high(1)

                all_batches(act, batch)

            @block.gpsimd
            def _(pool):
                pool.sem_inc(wlo_ready, 2)

                def rotations(b):
                    n_link = [0]

                    def link(ins):
                        n_link[0] += 1
                        ins.then_inc(g_done, 1)
                        pool.wait_ge(g_done, G_LINKS * b + n_link[0])

                    pool.wait_ge(par_ready, b + 1)
                    alone(pool, pool_turn)
                    re, im = rot[:, 0, :, CH_A:], rot[:, 1, :, CH_A:]
                    link(pool.memset(re[:, :, 0:1], 1.0))
                    alone(pool, pool_turn)
                    link(pool.memset(im[:, :, 0:1], 0.0))
                    for j in range(7):
                        n = 1 << j
                        t_re, t_im = (turn_b[:, j, x].unsqueeze(2).broadcast_to([P, BATCH, n]) for x in range(2))
                        a, c = rt[0][:, :, 0:n], rt[1][:, :, 0:n]
                        link(pool.tensor_tensor(a, re[:, :, 0:n], t_re, ALU.mult))
                        link(pool.tensor_tensor(c, im[:, :, 0:n], t_im, ALU.mult))
                        link(pool.tensor_tensor(re[:, :, n:2 * n], a, c, ALU.subtract))
                        link(pool.tensor_tensor(a, re[:, :, 0:n], t_im, ALU.mult))
                        link(pool.tensor_tensor(c, im[:, :, 0:n], t_re, ALU.mult))
                        link(pool.tensor_tensor(im[:, :, n:2 * n], a, c, ALU.add))
                    alone(pool, pool_turn)
                    link(pool.tensor_copy(rot[:, :, :, 0:CH_A], rot[:, :, :, CH_A:2 * CH_A]))
                    pool.sem_inc(rot_ready, 1)
                    alone(pool, pool_turn)
                    link(pool.tensor_copy(decay[:], ratio_b[:].unsqueeze(2).broadcast_to([P, BATCH, NCH])))
                    first = decay[0:64, :, 0:2 * CH_A].rearrange("p g (s k) -> p g s k", s=2)[:, :, :, 0:1]
                    alone(pool, pool_turn)
                    link(pool.memset(first, 0.0))
                    alone(pool, pool_turn)
                    link(pool.memset(decay[64:128, :, CH_A - 1:CH_A], 0.0))
                    alone(pool, pool_turn)
                    link(pool.memset(decay[64:128, :, NCH - 1:NCH], 0.0))
                    pool.sem_inc(decay_ready, 1)
                    assert n_link[0] == G_LINKS, n_link

                def batch(b, more):
                    def scale(r):
                        pool.wait_ge(evicted, GB * b + (r + 3))
                        pool.tensor_tensor(stage[:, cols(r % NBLK)], stage[:, cols(r % NBLK)],
                                           sh.rs[:, cols(r % NBLK)], ALU.mult).then_inc(scaled, 1)

                    def low(s):
                        pool.wait_ge(whi_ready, 2 * b + (s + 3))
                        pool.tensor_tensor(w_lo[s][:], w_raw[s][:], f32(w_hi[s][:]),
                                           ALU.subtract).then_inc(wlo_ready, 1)

                    for r in range(3):
                        scale(r)
                    if more:
                        low(0)
                    scale(3)
                    scale(4)
                    if more:
                        rotations(b + 1)
                    scale(5)
                    if more:
                        low(1)

                rotations(0)
                all_batches(pool, batch)

            @block.vector
            def _(dve):
                def batch(b):
                    n_link = [0]

                    def link(ins):
                        n_link[0] += 1
                        ins.then_inc(d_done, 1)
                        dve.wait_ge(d_done, D_LINKS * b + n_link[0])

                    def tt(out, a, c, op):
                        link(dve.tensor_tensor(out, a, c, op))

                    gsl = bass.ds(b * BATCH, BATCH)
                    link(dve.tensor_copy(bbar_b[:], sh.bbar[:, :, gsl]))
                    link(dve.tensor_copy(ratio_b[:], sh.ratio[:, gsl]))
                    link(dve.tensor_copy(p_lag[:], sh.p_lag[:, :, :, gsl]))
                    tt(diag[:], sh.ident[0:GC, 0:GC].unsqueeze(1).broadcast_to([GC, BATCH, GC]),
                       sh.dd[:, gsl].unsqueeze(2).broadcast_to([GC, BATCH, GC]), ALU.mult)
                    dve.tensor_copy(turn_b[:], sh.turn[:, :, :, gsl]).then_inc(par_ready, 1)

                    full = [P, BATCH, 8, GC]
                    power = lambda t, i: t[:, :, i].rearrange("p l g -> p g l").unsqueeze(3).broadcast_to(full)
                    chan = lambda t, x: t[:, x, gsl].unsqueeze(2).broadcast_to(full)
                    p_in = p_lag[:, ::-1]
                    tt(wide[0], power(p_in, 0), chan(sh.bw, 0), ALU.mult)
                    tt(wide[1], power(p_in, 1), chan(sh.bw, 1), ALU.mult)
                    tt(in_t[:, 0], wide[0], wide[1], ALU.subtract)
                    tt(wide[0], power(p_in, 0), chan(sh.bw, 1), ALU.mult)
                    tt(wide[1], power(p_in, 1), chan(sh.bw, 0), ALU.mult)
                    dve.tensor_tensor(in_t[:, 1], wide[0], wide[1], ALU.add).then_inc(in_ready, 1)
                    dve.wait_ge(in_ready, b + 1)
                    dve.wait_ge(y_done, b + 1)
                    tt(wide[0], power(p_lag, 0), chan(sh.cc, 0), ALU.mult)
                    tt(wide[1], power(p_lag, 1), chan(sh.cc, 1), ALU.mult)
                    tt(out_w[:, 0], wide[0], wide[1], ALU.subtract)
                    tt(wide[0], power(p_lag, 0), chan(sh.cc, 1), ALU.mult)
                    tt(wide[1], power(p_lag, 1), chan(sh.cc, 0), ALU.mult)
                    dve.scalar_tensor_tensor(out_w[:, 1], wide[0], -1.0, wide[1], ALU.mult,
                                             ALU.subtract).then_inc(out_ready, 1)
                    dve.wait_ge(out_ready, b + 1)

                    s_re, s_im = ps[:, S_BANK:S_BANK + BATCH, 0:NCH], ps[:, S_BANK:S_BANK + BATCH, NCH:2 * NCH]
                    e_re, e_im = rot[:, 0], rot[:, 1]
                    dve.wait_ge(rot_ready, b + 1)
                    dve.wait_ge(s_done, b + 1)
                    tt(groups(gin[0]), s_re, e_re, ALU.mult)
                    tt(groups(gt[0]), s_im, e_im, ALU.mult)
                    tt(gin[0], gin[0], gt[0], ALU.add)
                    tt(groups(gin[1]), s_im, e_re, ALU.mult)
                    tt(groups(gt[1]), s_re, e_im, ALU.mult)
                    tt(gin[1], gin[1], gt[1], ALU.subtract)

                    view = lambda bank: ps[0:GC, bank].rearrange("p (g l c) -> p g l c", g=BATCH, l=8)
                    fwd, bwd = view(Y_BANK), view(Y_BANK + 1)
                    dve.wait_ge(r_done, b + 1)
                    link(dve.tensor_copy(resp[:, :, 7:15], fwd))
                    link(dve.tensor_copy(resp[:, :, 0:7], bwd[:, :, 0:7]))
                    tt(resp[:, :, 7], bwd[:, :, 7], resp[:, :, 7], ALU.add)
                    dve.tensor_tensor(resp[:, :, 7], resp[:, :, 7], diag[:], ALU.add).then_inc(resp_ready, 1)

                    dec = decay[:].rearrange("p g k -> p (g k)")
                    dve.wait_ge(decay_ready, b + 1)
                    for i in range(2):
                        link(dve.tensor_tensor_scan(gs[i][0:64, 2:N + 2], dec[0:64], gin[i][0:64],
                                                    0.0, ALU.mult, ALU.add))
                        link(dve.tensor_tensor_scan(gs[i][64:128, 0:N][:, ::-1], dec[64:128][:, ::-1],
                                                    gin[i][64:128][:, ::-1], 0.0, ALU.mult, ALU.add))
                        ent = groups(gs[i][:, 1:N + 1])
                        for rows, k0 in ((slice(0, 64), 0), (slice(0, 64), CH_A),
                                         (slice(64, 128), CH_A - 1), (slice(64, 128), NCH - 1)):
                            link(dve.memset(ent[rows, :, k0:k0 + 1], 0.0))
                    e0, e1 = groups(gs[0][:, 1:N + 1]), groups(gs[1][:, 1:N + 1])
                    tt(groups(gt[0]), e0, e_re, ALU.mult)
                    tt(groups(gt[1]), e1, e_im, ALU.mult)
                    tt(gin[0], gt[0], gt[1], ALU.subtract)
                    tt(groups(gt[0]), e0, e_im, ALU.mult)
                    tt(groups(gt[1]), e1, e_re, ALU.mult)
                    dve.tensor_tensor(gin[1], gt[0], gt[1], ALU.add).then_inc(h_ready, 1)
                    dve.wait_ge(h_ready, b + 1)
                    assert n_link[0] == D_LINKS, n_link

                with dve.Fori(0, BATCHES) as b:
                    batch(b)

            @block.tensor
            def _(pe):
                pe.sem_inc(y_done, 1)
                flat = lambda t: t.rearrange("p l c -> p (l c)")

                def gate(b, r):
                    s, c = divmod(r, NBLK)
                    if c == 0:
                        pe.wait_ge(whi_ready, 2 * b + (s + 1))
                        pe.wait_ge(wlo_ready, 2 * b + (s + 1))
                    pe.wait_ge(evicted, GB * b + (r + 1))
                    for k in range(KD):
                        mm = three_products(pe, ps[:, G_BANK + r % 2], w_hi[s][:, k], w_lo[s][:, k],
                                            sh.x_hi[:, c, k], sh.x_lo[:, c, k], k == 0, k == KD - 1)
                    mm.then_inc(summed, 1)

                with pe.Fori(0, BATCHES) as b:
                    gate(b, 0)
                    pe.wait_ge(in_ready, b + 1)
                    for x in range(2):
                        for j in range(BATCH):
                            mm = pe.transpose(ps[:, S_BANK + x, j * P:(j + 1) * P], flat(in_t[:, x, j]), sh.ident[:])
                        mm.then_inc(t_done, 1)
                    gate(b, 1)
                    pe.wait_ge(t_read, 2 * b + 2)
                    pe.wait_ge(u_in, 16 * 2 * CHUNK * b + 16 * 2 * CHUNK)
                    for j in range(BATCH):
                        for x in range(2):
                            mm = pe.matmul(ps[:, S_BANK + j, x * NCH:(x + 1) * NCH], in_w[:, x, j], u[:, j],
                                           start=True, stop=True)
                    mm.then_inc(s_done, 1)
                    pe.wait_ge(out_ready, b + 1)
                    pe.wait_ge(y_ready, b + 1)
                    alone(pe, pe_turn)
                    for d, rows in enumerate((slice(0, 64), slice(64, 128))):
                        for j in range(BATCH):
                            for x in range(2):
                                mm = pe.matmul(ps[0:GC, Y_BANK + d, j * P:(j + 1) * P], bbar_b[rows, x, j],
                                               flat(out_w[rows, x, j]), start=(x == 0), stop=(x == 1))
                    mm.then_inc(r_done, 1)
                    for r in (2, 3, 4):
                        gate(b, r)
                    pe.wait_ge(local_in, 16 * CHUNK * b + 16 * CHUNK)
                    pe.wait_ge(h_ready, b + 1)
                    for j in range(BATCH):
                        out = ps[:, Y_BANK + j // 2, (j % 2) * NCH:(j % 2 + 1) * NCH]
                        pe.matmul(out, local[:, j], u[:, j], start=True, stop=False)
                        pe.matmul(out, flat(out_w[:, 0, j]), groups(gin[0])[:, j], start=False, stop=False)
                        mm = pe.matmul(out, flat(out_w[:, 1, j]), groups(gin[1])[:, j], start=False, stop=True)
                    mm.then_inc(y_done, 1)
                    gate(b, 5)


QKP = 4
LAG = 3


def attention(nc, st, roped, proj, ident_d, mix):
    with ExitStack() as ctx:
        sb = lambda name, shape, dt=F32: ctx.enter_context(nc.sbuf_tensor(name, shape, dt))
        sem = lambda name: ctx.enter_context(nc.semaphore(name))
        k1 = sb("a_k1", [P, NKV, TOK], F32R)
        k2 = sb("a_k2", [P, NKV, TOK], F32R)
        KT = TOK // P
        v1 = sb("a_v1", [P, KT, NKV, P], F32R)
        v2 = sb("a_v2", [P, KT, NKV, P], F32R)
        v_raw = sb("a_vraw", [P, 2, TOK])
        ident = sb("a_ident", [P, P])
        q1 = [sb(f"a_q1{s}", [P, BLK], F32R) for s in range(NKV)]
        q2 = [sb(f"a_q2{s}", [P, BLK], F32R) for s in range(NKV)]
        nmax = [sb(f"a_nmax{s}", [P, BLK // P], F32R) for s in range(NKV)]
        p32 = [sb(f"a_p32{s}", [P, BLK]) for s in range(QKP)]
        p_hi = [sb(f"a_phi{s}", [P, BLK], F32R) for s in range(QKP)]
        p_lo = [sb(f"a_plo{s}", [P, BLK], F32R) for s in range(QKP)]
        den = [sb(f"a_den{s}", [HEAD, BLK]) for s in range(2)]
        o = st.o
        ps = ctx.enter_context(nc.psum_tensor("a_ps", [P, 8, BLK], F32))
        ST_BANK, O_BANK, MX_BANK = 0, 2, 4
        V_BANKS = 4

        k_first_in = [sem(f"a_k_first_in{s}") for s in range(2)]
        k_in = [sem(f"a_k_in{s}") for s in range(2)]
        v_in = sem("a_v_in")
        ones_set = sem("a_ones_set")
        q_in = [sem(f"a_q_in{s}") for s in range(NKV)]
        nmax_in = [sem(f"a_nmax_in{s}") for s in range(NKV)]
        stored = st.attention
        v_turned = sem("a_v_turned")
        v1_ready = sem("a_v1_ready")
        v2_ready = sem("a_v2_ready")
        max_mm = sem("a_max_mm")
        max_found = sem("a_max_found")
        scored = sem("a_scored")
        exp_done = sem("a_exp_done")
        phi_done = sem("a_phi_done")
        plo_done = sem("a_plo_done")
        pv_done = sem("a_pv_done")
        ln_done = sem("a_ln_done")
        rden_done = sem("a_rden_done")
        normed = sem("a_normed")

        class Seq:
            def __init__(self, u0, s0, n, iters, kt0, blk0):
                self.u0, self.s0, self.n, self.iters, self.kt0, self.blk0 = u0, s0, n, iters, kt0, blk0
        A = Seq(0, 0, LEN_A // P, 4, 0, 0)
        B = Seq(16, 16 * A.n, LEN_B // P, 8, LEN_A // P, 1)
        SEQS = (A, B)
        STEPS = B.s0 + 32 * B.n

        def for_iterations(eng, sq, body):
            body(0, False)
            with eng.Fori(1, sq.iters - 1) as it:
                body(it, False)
            body(sq.iters - 1, True)

        LN_STEP, RDEN_STEP, SCALE_STEP = LAG, LAG + 1, LAG + 2

        def due(sq, off, it, kv, kt):
            d, at = divmod(off, sq.n)
            if at != kt or (isinstance(it, int) and it == 0 and kv - 1 - d < 0):
                return None
            return 1 + d

        def left_over(sq, off):
            return range(off // sq.n, -1, -1)

        def next_seq(sq, last, kv):
            if not (last and kv >= 2):
                return sq
            return B if sq is A else None

        with nc.Block() as block:

            @block.sync
            def _(sp):
                def load_k(l, dst, rows, tok, done):
                    sp.dma_start(f32(dst[rows:rows + HEAD, :, tok]),
                                 roped[NQ:NQ + NKV, l, :, tok].rearrange("h d n -> d h n")).then_inc(done, 16)

                def load_q(kv, head, blk):
                    tok = bass.ds(blk * BLK, BLK)
                    both = roped.rearrange("h l d n -> h (l d) n")
                    sp.dma_start(f32(q1[kv][:]), both[head][:, tok]).then_inc(q_in[kv], 16)
                    sp.dma_start(f32(q2[kv][0:HEAD]), both[head][0:HEAD, tok]).then_inc(q_in[kv], 16)

                def place_max(sq, it, kv):
                    u = sq.u0 + it * 4 + kv
                    s = kv
                    for j in range(BLK // P):
                        sp.wait_ge(max_found, 4 * u + (3 + j))
                        sp.dma_start(f32(q2[s][HEAD:HEAD + 1, j * P:(j + 1) * P]),
                                     f32(nmax[s][:, j:j + 1])).then_inc(nmax_in[s], 16)

                def store(u, kv, head, blk):
                    sp.wait_ge(normed, u + 3)
                    sp.dma_start(mix[head][:, bass.ds(blk * BLK, BLK)], o[kv % 2][:]).then_inc(stored[kv % 2], 16)

                toks = (slice(0, LEN_A), slice(LEN_A, TOK))
                load_k(0, k1, 0, toks[0], k_first_in[0])
                load_q(0, 0, 0)
                load_q(1, 4, 0)
                sp.dma_start(ident[:], ident_d).then_inc(v_in, 16)
                sp.dma_start(v_raw[:], proj[V_T:V_T + 2].rearrange("t p n -> p t n")).then_inc(v_in, 16)
                load_k(0, k1, HEAD, toks[0], k_in[0])
                load_k(1, k2, 0, toks[0], k_in[0])
                for kv in range(2, NKV):
                    load_q(kv, 4 * kv, 0)
                for sq in SEQS:
                    if sq is A:
                        for kv in range(2):
                            place_max(sq, 0, kv)
                        load_k(0, k1, 0, toks[1], k_first_in[1])
                        load_k(0, k1, HEAD, toks[1], k_in[1])
                        load_k(1, k2, 0, toks[1], k_in[1])
                    n_blk = sq.iters // 4
                    for bi in range(n_blk):
                        blk = sq.blk0 + bi

                        def iteration(g, first_g, last_g):
                            it = g + 4 * bi
                            last = last_g and bi == n_blk - 1
                            for kv in range(NKV):
                                u = sq.u0 + it * 4 + kv
                                if next_seq(sq, last, kv):
                                    place_max(sq, it if kv < 2 else it + 1, (kv + 2) % 4)
                                sp.wait_ge(scored, sq.s0 + sq.n * (it * 4 + kv + 1))
                                if not last_g:
                                    load_q(kv, g + (4 * kv + 1), blk)
                                elif blk + 1 < NBLK:
                                    load_q(kv, 4 * kv, blk + 1)
                                if kv:
                                    store(u - 1, kv - 1, g + 4 * (kv - 1), blk)
                                elif not first_g:
                                    store(u - 1, NKV - 1, g + (4 * (NKV - 1) - 1), blk)
                                elif bi:
                                    store(u - 1, NKV - 1, NQ - 1, blk - 1)

                        iteration(0, True, False)
                        with sp.Fori(1, 3) as g:
                            iteration(g, False, False)
                        iteration(3, False, True)
                    store(sq.u0 + 4 * sq.iters - 1, NKV - 1, NQ - 1, sq.blk0 + n_blk - 1)
                sp.wait_ge(st.y, 16 * 2 * CHUNK * (GROUPS // BATCH) + 16)
                for c in range(NBLK):
                    sp.wait_ge(st.gates[c], 16 * (2 * KD) + 16)
                for s in range(2):
                    sp.wait_ge(stored[s], 16 * (NQ // 2))

            @block.gpsimd
            def _(pool):
                for n, (part, value) in enumerate(((v1[:, :, :, HEAD:P], 1.0), (v2[:, :, :, HEAD:P], 0.0),
                                                   (k2[HEAD:HEAD + 1], 1.0))):
                    pool.memset(f32(part), value).then_inc(ones_set, 1)
                    pool.wait_ge(ones_set, n + 1)
                pool.sem_inc(plo_done, QKP)
                with pool.Fori(0, STEPS // QKP) as i:
                    for s in range(QKP):
                        pool.wait_ge(phi_done, QKP * i + (s + 1))
                        pool.wait_ge(pv_done, QKP * i + (s + 1))
                        pool.tensor_tensor(p_lo[s][:], p32[s][:], f32(p_hi[s][:]),
                                           ALU.subtract).then_inc(plo_done, 1)

            @block.scalar
            def _(act):
                act.preload_act_table_set(LN_EXP)
                act.sem_inc(exp_done, 2)
                act.wait_ge(ones_set, 3)
                for i in range(6):
                    t, c = divmod(i, 3)
                    act.wait_ge(v_turned, i + 1)
                    act.activation(v1[:, 4 * c:4 * c + 4, 2 * t:2 * t + 2, 0:HEAD],
                                   ps[:, i % V_BANKS].rearrange("p (c h d) -> p c h d", c=4, h=2),
                                   ACT.Copy).then_inc(v1_ready, 1)

                def ln_sums(u, s):
                    act.wait_ge(normed, u + 1)
                    act.activation(den[s][:], ps[HEAD:P, O_BANK + s], ACT.Ln).then_inc(ln_done, 1)

                def exp_sums(u, s):
                    act.wait_ge(ln_done, u + 1)
                    act.activation(den[s][:], den[s][:], ACT.Exp, scale=-1.0).then_inc(rden_done, 1)

                for sq in SEQS:
                    def iteration(it, last):
                        for kv in range(NKV):
                            for kt in range(sq.n):
                                step = it * (4 * sq.n) + (sq.s0 + kv * sq.n + kt)
                                act.wait_ge(scored, step + 1)
                                act.wait_ge(plo_done, step + 1)
                                act.activation(p32[kt % QKP][:], ps[:, ST_BANK + kt % 2], ACT.Exp,
                                               scale=HEAD ** -0.5).then_inc(exp_done, 1)
                                d = due(sq, LN_STEP, it, kv, kt)
                                if d:
                                    act.wait_ge(pv_done, step + (1 + QKP - LAG))
                                    ln_sums(it * 4 + (sq.u0 + kv - d), (kv + d) % 2)
                                d = due(sq, RDEN_STEP, it, kv, kt)
                                if d:
                                    exp_sums(it * 4 + (sq.u0 + kv - d), (kv + d) % 2)
                    for_iterations(act, sq, iteration)
                    last_unit = sq.u0 + 4 * sq.iters - 1
                    for d in left_over(sq, RDEN_STEP):
                        if d in left_over(sq, LN_STEP):
                            act.wait_ge(pv_done, sq.s0 + 4 * sq.iters * sq.n + QKP)
                            ln_sums(last_unit - d, (1 + d) % 2)
                        exp_sums(last_unit - d, (1 + d) % 2)

            @block.vector
            def _(dve):
                dve.sem_inc(max_found, 2)
                dve.sem_inc(normed, 2)
                def find_max(sq, u, s, j):
                    dve.wait_ge(max_mm, 4 * u + (j + 1))
                    if sq is A:
                        src = ps[:, MX_BANK + j]
                    else:
                        src = ps[:, MX_BANK + 2 * (j % 2):MX_BANK + 2 * (j % 2) + 2]
                    dve.tensor_reduce(nmax[s][:, j:j + 1], src, AX.X if sq is A else AX.XY, ALU.max,
                                      negate=True).then_inc(max_found, 1)

                def scale_out(u, s):
                    dve.wait_ge(rden_done, u + 1)
                    half = (u - s) * 8
                    dve.wait_ge(stored[s], half)
                    dve.tensor_tensor(o[s][:], ps[0:HEAD, O_BANK + s], den[s][:],
                                      ALU.mult).then_inc(normed, 1)

                for sq in SEQS:
                    if sq is A:
                        for kv in range(2):
                            for j in range(4):
                                find_max(sq, sq.u0 + kv, kv, j)
                        for i in range(6):
                            t, c = divmod(i, 3)
                            dve.wait_ge(v1_ready, i + 1)
                            dve.tensor_tensor(v2[:, 4 * c:4 * c + 4, 2 * t:2 * t + 2, 0:HEAD],
                                              ps[:, i % V_BANKS].rearrange("p (c h d) -> p c h d", c=4, h=2),
                                              f32(v1[:, 4 * c:4 * c + 4, 2 * t:2 * t + 2, 0:HEAD]),
                                              ALU.subtract).then_inc(v2_ready, 1)

                    def iteration(it, last):
                        for kv in range(NKV):
                            for kt in range(sq.n):
                                step = it * (4 * sq.n) + (sq.s0 + kv * sq.n + kt)
                                dve.wait_ge(exp_done, step + 3)
                                dve.wait_ge(pv_done, step + 1)
                                dve.tensor_copy(p_hi[kt % QKP][:], p32[kt % QKP][:]).then_inc(phi_done, 1)
                                d = due(sq, SCALE_STEP, it, kv, kt)
                                if d:
                                    scale_out(it * 4 + (sq.u0 + kv - d), (kv + d) % 2)
                                ahead = next_seq(sq, last, kv)
                                if ahead:
                                    per = sq.n // 4
                                    if kt % per == per - 1:
                                        find_max(ahead, it * 4 + (sq.u0 + kv + 2), (kv + 2) % 4, kt // per)
                    for_iterations(dve, sq, iteration)
                    for d in left_over(sq, SCALE_STEP):
                        scale_out(sq.u0 + 4 * sq.iters - 1 - d, (1 + d) % 2)

            @block.tensor
            def _(pe):
                pe.sem_inc(pv_done, QKP)
                def max_part(sq, u, s, kt):
                    per = sq.n // 4
                    j, half = divmod(kt, per)
                    if half == 0:
                        pe.wait_ge(max_found, 4 * u + (j + 1))
                    bank = MX_BANK + (j if sq is A else 2 * (j % 2) + half)
                    key0 = (sq.kt0 + 4 * half) * P
                    mm = pe.matmul(ps[:, bank], q1[s][0:HEAD, j * P:(j + 1) * P],
                                   k1[0:HEAD, s, key0:key0 + BLK], start=True, stop=True)
                    if half == per - 1:
                        mm.then_inc(max_mm, 1)

                def output(sq, unit, s, kt, step):
                    pe.wait_ge(plo_done, step + 1 + QKP)
                    if kt == 0:
                        pe.wait_ge(normed, unit + 1)
                    out, tile = ps[:, O_BANK + s % 2], sq.kt0 + kt
                    first, last = kt == 0, kt == sq.n - 1
                    pe.matmul(out, v1[:, tile, s], p_hi[kt % QKP][:], start=first, stop=False)
                    pe.matmul(out, v2[:, tile, s], p_hi[kt % QKP][:], start=False, stop=False)
                    pe.matmul(out, v1[:, tile, s], p_lo[kt % QKP][:], start=False,
                              stop=last).then_inc(pv_done, 1)

                for n, sq in enumerate(SEQS):
                    if sq is A:
                        pe.wait_ge(k_first_in[n], 16)
                        for kv in range(2):
                            pe.wait_ge(q_in[kv], 32)
                            for kt in range(sq.n):
                                max_part(sq, kv, kv, kt)
                        pe.wait_ge(v_in, 32)
                        for i in range(6):
                            half, c = divmod(i, 3)
                            if i >= V_BANKS:
                                pe.wait_ge(v2_ready, i - V_BANKS + 1)
                            for j in range(4):
                                kt = 4 * c + j
                                mm = pe.transpose(ps[:, i % V_BANKS, j * P:(j + 1) * P],
                                                  v_raw[:, half, kt * P:(kt + 1) * P], ident[:])
                            mm.then_inc(v_turned, 1)
                        pe.wait_ge(ones_set, 3)
                        pe.wait_ge(v2_ready, 6)
                    pe.wait_ge(k_in[n], 32)

                    def iteration(it, last):
                        for kv in range(NKV):
                            unit = it * 4 + (sq.u0 + kv)
                            ahead, s_ahead = unit + 2, (kv + 2) % 4
                            sq_ahead = next_seq(sq, last, kv)
                            n_of = lambda k: it + (sq.u0 // 4 + 1 + (1 if k >= NKV else 0))
                            pe.wait_ge(nmax_in[kv], n_of(kv) * 64)
                            pe.wait_ge(q_in[kv], n_of(kv) * 32)
                            if sq_ahead is not sq and sq_ahead:
                                pe.wait_ge(k_first_in[1], 16)
                            if sq_ahead:
                                pe.wait_ge(q_in[s_ahead], n_of(kv + 2) * 32)
                            for kt in range(sq.n):
                                step = it * (4 * sq.n) + (sq.s0 + kv * sq.n + kt)
                                tile = sq.kt0 + kt
                                pe.wait_ge(exp_done, step + 1)
                                out = ps[:, ST_BANK + kt % 2]
                                keys = slice(tile * P, (tile + 1) * P)
                                pe.matmul(out, k1[:, kv, keys], q1[kv][:], start=True, stop=False)
                                pe.matmul(out, k2[0:HEAD + 1, kv, keys], q2[kv][0:HEAD + 1], start=False,
                                          stop=True).then_inc(scored, 1)
                                if sq_ahead:
                                    for part in range(sq_ahead.n // sq.n):
                                        max_part(sq_ahead, ahead, s_ahead, kt * (sq_ahead.n // sq.n) + part)
                                if kt >= LAG:
                                    output(sq, unit, kv, kt - LAG, step - LAG)
                                elif not (isinstance(it, int) and it == 0 and kv == 0):
                                    output(sq, unit - 1, (kv + 3) % 4, kt - LAG + sq.n, step - LAG)
                    for_iterations(pe, sq, iteration)
                    for kt in range(sq.n - LAG, sq.n):
                        output(sq, sq.u0 + 4 * sq.iters - 1, 3, kt, sq.s0 + (4 * sq.iters - 1) * sq.n + kt)


TAIL_T = 2 * KD + KD + 2 * (D_FF // P)
QUART = 8
MLP_ORDER = [("f1", 0), ("f1", 1), ("f2", 0), ("f1", 2), ("f2", 1), ("f1", 3), ("f2", 2), ("f2", 3)]


def tail(nc, st, mix, proj, x_t, w_tail, gain, ones_d, y_t):
    with ExitStack() as ctx:
        sb = lambda name, shape, dt=F32: ctx.enter_context(nc.sbuf_tensor(name, shape, dt))
        sem = lambda name: ctx.enter_context(nc.semaphore(name))
        h_hi = sb("t_hhi", [P, KD, BLK], F32R)
        h_lo = sb("t_hlo", [P, KD, BLK], F32R)
        y_hi = sb("t_yhi", [P, 4, BLK], F32R)
        y_lo = sb("t_ylo", [P, 4, BLK], F32R)
        a_hi = [sb(f"t_ahi{s}", [P, QUART, BLK], F32R) for s in range(2)]
        a_lo = [sb(f"t_alo{s}", [P, QUART, BLK], F32R) for s in range(2)]
        x1 = sb("t_x1", [P, KD, BLK])
        w_raw = [sb(f"t_wraw{s}", [P, KD, P]) for s in range(2)]
        w_hi = [sb(f"t_whi{s}", [P, KD, P], F32R) for s in range(2)]
        w_lo = [sb(f"t_wlo{s}", [P, KD, P], F32R) for s in range(2)]
        g_raw = [sb(f"t_graw{s}", [P, 2, BLK]) for s in range(2)]
        sg = [sb(f"t_sg{s}", [P, 2, BLK]) for s in range(2)]
        sgb = [sb(f"t_sgb{s}", [P, BLK]) for s in range(2)]
        ta = [sb(f"t_ta{s}", [P, BLK]) for s in range(2)]
        tb = [sb(f"t_tb{s}", [P, BLK]) for s in range(2)]
        tc = [sb(f"t_tc{s}", [P, BLK]) for s in range(2)]
        rs = sb("t_rs", [P, BLK])
        gn = sb("t_gain", [P, KD])
        eps = sb("t_eps", [P, 1])
        ones = sb("t_ones", [P, P])
        ps = ctx.enter_context(nc.psum_tensor("t_ps", [P, 8, BLK], F32))
        A_BANK, G_BANK, O_BANK, F1_BANK, F2_BANK, MEAN = 0, 2, 6, 0, 2, 4

        const_in = sem("t_const_in")
        eps_set = sem("t_eps_set")
        act_turn, sp_turn = sem("t_act_turn"), sem("t_sp_turn")
        w_in_s = [sem(f"t_w_in{s}") for s in range(2)]
        mix_in = [sem(f"t_mix_in{s}") for s in range(2)]
        g_in = [sem(f"t_g_in{s}") for s in range(2)]
        first_in = [sem(f"t_first_in{c}") for c in range(6)]
        x1_in = sem("t_x1_in")
        y_out = sem("t_y_out")
        mixhi_ready = sem("t_mixhi_ready")
        mixlo_ready = sem("t_mixlo_ready")
        whi_ready = sem("t_whi_ready")
        wlo_ready = sem("t_wlo_ready")
        summed = sem("t_summed")
        sg_ready = sem("t_sg_ready")
        sgb_ready = sem("t_sgb_ready")
        merge_step = sem("t_merge_step")
        merged32 = sem("t_merged32")
        mhi_ready = sem("t_mhi_ready")
        mlo_ready = sem("t_mlo_ready")
        x1_ready = sem("t_x1_ready")
        hhi_ready = sem("t_hhi_ready")
        hlo_ready = sem("t_hlo_ready")
        sq_ready = sem("t_sq_ready")
        sq_step = sem("t_sq_step")
        mean_done = sem("t_mean_done")
        ln_done = sem("t_ln_done")
        rs_ready = sem("t_rs_ready")
        relu_ready = sem("t_relu_ready")
        t_ready = sem("t_t_ready")
        tsq_ready = sem("t_tsq_ready")
        ahi_ready = sem("t_ahi_ready")
        alo_ready = sem("t_alo_ready")
        f2_added = sem("t_f2_added")

        S1, S2 = 0, 2 * KD
        MLP = S2 + KD
        SECT = [(kind, q, MLP + QUART * n) for n, (kind, q) in enumerate(MLP_ORDER)]
        PAIRS = QUART // 2
        N_MIX = 6

        def chunk(c):
            if c < 2:
                return 8 + 2 * c, y_hi[:, 2 * c:2 * c + 2], y_lo[:, 2 * c:2 * c + 2]
            return 2 * c - 4, h_hi[:, 2 * c - 4:2 * c - 2], h_lo[:, 2 * c - 4:2 * c - 2]

        def first_place(c):
            return g_raw[c][:] if c < 2 else x1[:, 2 * c - 4:2 * c - 2]

        PREFETCH = {("f2", 2): 0, ("f2", 3): PAIRS}
        H_FREE = MLP + QUART * (MLP_ORDER.index(("f1", 3)) + 1)

        def all_blocks(eng, one_block):
            with eng.Fori(0, NBLK - 1) as b:
                one_block(b, True)
            one_block(NBLK - 1, False)
        gates = proj[GA_T:GS_T + KD].rearrange("(t m) p n -> m p t n", t=2)

        with nc.Block() as block:

            @block.sync
            def _(sp):
                def load_w(j, s):
                    sp.dma_start(w_raw[s][:], w_tail[j]).then_inc(w_in_s[s], 16)

                def next_w(b, j, s):
                    sp.wait_ge(wlo_ready, b * TAIL_T + j + 3)
                    load_w(j + 2, s)

                sp.sem_inc(y_out, 16)
                load_w(0, 0)
                for c in range(N_MIX):
                    t0 = chunk(c)[0]
                    sp.dma_start(first_place(c), mix[t0:t0 + 2, :, 0:BLK].rearrange(
                        "k p n -> p k n")).then_inc(first_in[c], 16)
                    if c == 1:
                        load_w(1, 1)
                sp.dma_start(gn[:], gain).then_inc(const_in, 16)
                sp.dma_start(ones[:], ones_d).then_inc(const_in, 16)

                def mix_chunk(b, c):
                    s, blk = c % 2, bass.ds(b * BLK, BLK)
                    if c < 2:
                        sp.wait_ge(sg_ready, b * KD + 1)
                    else:
                        sp.wait_ge(mixlo_ready, b * N_MIX + c - 1)
                    alone(sp, sp_turn)
                    if c < N_MIX:
                        t0 = chunk(c)[0]
                        sp.dma_start(g_raw[s][:], mix[t0:t0 + 2, :, blk].rearrange(
                            "k p n -> p k n")).then_inc(mix_in[s], 16)
                    else:
                        sp.dma_start(g_raw[s][:], gates[s][:, :, blk]).then_inc(g_in[s], 16)

                for s in range(2):
                    sp.wait_ge(mixlo_ready, s + 1)
                    sp.dma_start(g_raw[s][:], gates[s][:, :, 0:BLK]).then_inc(g_in[s], 16)
                sp.wait_ge(mixlo_ready, N_MIX)

                def one_block(b, more_blocks):
                    blk = bass.ds(b * BLK, BLK)

                    def merge_pair(i, more):
                        for s in range(2):
                            m = 2 * i + s
                            next_w(b, S1 + 2 * m, 0)
                            next_w(b, S1 + 2 * m + 1, 1)
                            sp.wait_ge(y_out, b * KD * 16 + 16)
                            alone(sp, sp_turn)
                            sp.dma_start(x1[:, m], x_t[b][:, m]).then_inc(x1_in, 16)
                            if more:
                                sp.wait_ge(sg_ready, b * KD + m + 2)
                                alone(sp, sp_turn)
                                sp.dma_start(g_raw[s][:], gates[m + 2][:, :, blk]).then_inc(g_in[s], 16)

                    with sp.Fori(0, KD // 2 - 1) as i:
                        merge_pair(i, True)
                    merge_pair(KD // 2 - 1, False)
                    with sp.Fori(0, (TAIL_T - S2 - 2 * QUART) // 2) as i:
                        for s in range(2):
                            next_w(b, 2 * i + (S2 + s), s)

                    def f2_pair(q, i, c=None):
                        for s in range(2):
                            next_w(b, 2 * i + (TAIL_T - QUART * (4 - q) + s), s)
                            if q == 3:
                                sp.wait_ge(f2_added, b * (4 * KD) + 2 * i + (3 * KD + s + 3))
                                alone(sp, sp_turn)
                                sp.dma_start(y_t[b][:, 2 * i + s], x1[:, 2 * i + s]).then_inc(y_out, 16)
                        if c is not None:
                            mix_chunk(b + 1, c)

                    if more_blocks:
                        for s in range(2):
                            sp.wait_ge(st.attention[s], 16 * (NQ * NBLK // 2))
                        mix_chunk(b + 1, 0)
                        for n in range(2 * PAIRS):
                            f2_pair(2 + n // PAIRS, n % PAIRS, n + 1 if n + 1 < N_MIX + 2 else None)
                    else:
                        for q in (2, 3):
                            with sp.Fori(0, PAIRS) as i:
                                f2_pair(q, i)

                all_blocks(sp, one_block)
                sp.wait_ge(y_out, NBLK * KD * 16 + 16)
                for s in range(2):
                    sp.wait_ge(w_in_s[s], 16 * (NBLK * TAIL_T // 2 + 1))

            @block.gpsimd
            def _(pool):
                pool.sem_inc(wlo_ready, 2)
                with pool.Fori(0, NBLK * TAIL_T // 2 + 1) as i:
                    for s in range(2):
                        pool.wait_ge(whi_ready, 2 * i + (s + 1))
                        pool.wait_ge(w_in_s[s], 16 * i + 16)
                        pool.tensor_tensor(w_lo[s][:], w_raw[s][:], f32(w_hi[s][:]),
                                           ALU.subtract).then_inc(wlo_ready, 1)

            @block.scalar
            def _(act):
                act.preload_act_table(ACT.Sigmoid)
                act.sem_inc(relu_ready, 2)
                for sem_ in (sg_ready, mhi_ready, ahi_ready):
                    act.sem_inc(sem_, 1)

                def w_high(b, j, s):
                    act.wait_ge(w_in_s[s], b * (8 * TAIL_T) + (j - s) * 8 + 16)
                    act.wait_ge(summed, b * TAIL_T + j + 1)
                    act.activation(w_hi[s][:], w_raw[s][:], ACT.Copy).then_inc(whi_ready, 1)

                w_high(0, 0, 0)

                for c in range(N_MIX):
                    act.wait_ge(first_in[c], 16)
                    act.activation(chunk(c)[1], first_place(c), ACT.Copy).then_inc(mixhi_ready, 1)
                    if c == 1:
                        w_high(0, 1, 1)

                act.wait_ge(const_in, 32)
                act.wait_ge(eps_set, 1)

                def one_block(b, more_blocks):
                    act.preload_act_table(ACT.Sigmoid)
                    with act.Fori(0, KD // 2) as i:
                        for s in range(2):
                            m = 2 * i + s
                            act.wait_ge(g_in[s], b * (8 * KD) + 16 * i + 16)
                            act.wait_ge(merged32, m + (b * KD + 1))
                            act.activation(sg[s][:], g_raw[s][:], ACT.Sigmoid).then_inc(sg_ready, 1)
                            w_high(b, 4 * i + (2 * s + 2), 0)
                            act.wait_ge(summed, b * TAIL_T + 4 * i + (2 * s + 3))
                            act.activation(sgb[s][:], ps[:, G_BANK + 2 * s + 1],
                                           ACT.Sigmoid).then_inc(sgb_ready, 1)
                            w_high(b, 4 * i + (2 * s + 3), 1)
                            act.wait_ge(merged32, b * KD + m + 2)
                            alone(act, act_turn)
                            act.activation(a_hi[0][:, m], tc[s][:], ACT.Copy).then_inc(mhi_ready, 1)
                    act.preload_act_table_set(LN_EXP)
                    with act.Fori(0, KD // 2) as i:
                        for s in range(2):
                            m = 2 * i + s
                            w_high(b, 2 * i + (S2 + 2 + s), s)
                            act.wait_ge(x1_ready, b * KD + m + 3)
                            alone(act, act_turn)
                            act.activation(h_hi[:, m], x1[:, m], ACT.Identity,
                                           scale=gn[:, bass.ds(m, 1)]).then_inc(hhi_ready, 1)
                            act.wait_ge(sq_step, b * (KD + 1) + m + 2)
                            alone(act, act_turn)
                            act.activation(sgb[s][:], x1[:, m], ACT.Square).then_inc(sq_ready, 1)

                    for kind, q, j0 in SECT:
                        def pair(i, first=False):
                            for s in range(2):
                                j = 2 * i + (j0 + s)
                                f = 2 * i + (QUART * q + s)
                                if kind == "f1":
                                    act.wait_ge(summed, b * TAIL_T + j + 3)
                                    act.wait_ge(tsq_ready, b * (4 * QUART) + f + 1)
                                    act.activation(ta[s][:], ps[:, F1_BANK + s],
                                                   ACT.Relu).then_inc(relu_ready, 1)
                                w_high(b, j + 2, s)
                                if kind == "f1":
                                    if first and s == 0:
                                        act.wait_ge(mean_done, b + 1)
                                        act.activation(rs[:], ps[:, MEAN], ACT.Ln,
                                                       bias=eps[:, 0:1]).then_inc(ln_done, 1)
                                        act.wait_ge(ln_done, b + 1)
                                        act.activation(rs[:], rs[:], ACT.Exp,
                                                       scale=-0.5).then_inc(rs_ready, 1)
                                    act.wait_ge(t_ready, b * (4 * QUART) + f + 1)
                                    alone(act, act_turn)
                                    act.activation(a_hi[q % 2][:, 2 * i + s], tb[s][:],
                                                   ACT.Square).then_inc(ahi_ready, 1)
                        if (kind, q) == ("f1", 0):
                            pair(0, True)
                            with act.Fori(1, PAIRS) as i:
                                pair(i)
                        elif more_blocks and (kind, q) in PREFETCH:
                            for i in range(PAIRS):
                                pair(i)
                                c = PREFETCH[kind, q] + i
                                if c < N_MIX:
                                    act.wait_ge(summed, b * TAIL_T + H_FREE + 2)
                                    act.wait_ge(mix_in[c % 2], b * 48 + (c // 2 + 1) * 16)
                                    act.activation(chunk(c)[1], g_raw[c % 2][:], ACT.Copy).then_inc(mixhi_ready, 1)
                        else:
                            with act.Fori(0, PAIRS) as i:
                                pair(i)

                all_blocks(act, one_block)

            @block.vector
            def _(dve):
                dve.memset(eps[:], EPS).then_inc(eps_set, 1)
                for s_ in (x1_ready, alo_ready, f2_added, sq_step):
                    dve.sem_inc(s_, 2)
                dve.sem_inc(merge_step, 6)
                for s_ in (merged32, mlo_ready, tsq_ready):
                    dve.sem_inc(s_, 1)

                def mix_low(b, c, src):
                    _, hi, lo = chunk(c)
                    dve.wait_ge(mixhi_ready, b * N_MIX + c + 1)
                    dve.tensor_tensor(lo, src, f32(hi), ALU.subtract).then_inc(mixlo_ready, 1)

                for c in range(N_MIX):
                    mix_low(0, c, first_place(c))
                dve.wait_ge(const_in, 32)

                def one_block(b, more_blocks):
                    with dve.Fori(0, KD // 2) as i:
                        for s in range(2):
                            mm = b * KD + 2 * i + s
                            dve.wait_ge(mhi_ready, mm + 1)
                            dve.wait_ge(mlo_ready, mm + 1)
                            dve.wait_ge(sgb_ready, mm + 1)
                            dve.tensor_tensor(tb[s][:], ps[:, G_BANK + 2 * s], sgb[s][:],
                                              ALU.mult).then_inc(merge_step, 1)
                            dve.wait_ge(sg_ready, mm + 2)
                            dve.wait_ge(merge_step, mm * 3 + 7)
                            dve.tensor_tensor(tb[s][:], tb[s][:], sg[s][:, 1], ALU.mult).then_inc(merge_step, 1)
                            dve.wait_ge(summed, b * TAIL_T + 4 * i + (2 * s + 4))
                            dve.tensor_tensor(ta[s][:], ps[:, A_BANK + s], sg[s][:, 0],
                                              ALU.mult).then_inc(merge_step, 1)
                            dve.wait_ge(merge_step, mm * 3 + 9)
                            dve.tensor_tensor(tc[s][:], ta[s][:], tb[s][:], ALU.add).then_inc(merged32, 1)
                            dve.wait_ge(mhi_ready, mm + 2)
                            dve.tensor_tensor(a_lo[0][:, 2 * i + s], tc[s][:], f32(a_hi[0][:, 2 * i + s]),
                                              ALU.subtract).then_inc(mlo_ready, 1)
                    dve.memset(rs[:], 0.0).then_inc(sq_step, 1)
                    with dve.Fori(0, KD // 2) as i:
                        for s in range(2):
                            m = 2 * i + s
                            dve.wait_ge(x1_in, b * (16 * KD) + 16 * KD)
                            dve.wait_ge(summed, b * TAIL_T + 2 * i + (S2 + s + 3))
                            dve.tensor_tensor(x1[:, m], ps[:, O_BANK + s], x1[:, m],
                                              ALU.add).then_inc(x1_ready, 1)
                            dve.wait_ge(hhi_ready, b * KD + m + 1)
                            dve.scalar_tensor_tensor(h_lo[:, m], x1[:, m], gn[:, bass.ds(m, 1)],
                                                     f32(h_hi[:, m]), ALU.mult,
                                                     ALU.subtract).then_inc(hlo_ready, 1)
                            dve.wait_ge(sq_ready, b * KD + m + 1)
                            dve.wait_ge(sq_step, b * (KD + 1) + m + 3)
                            dve.tensor_tensor(rs[:], rs[:], sgb[s][:], ALU.add).then_inc(sq_step, 1)
                    for kind, q, j0 in SECT:
                        def pair(i):
                            for s in range(2):
                                n = 2 * i + s
                                f = b * (4 * QUART) + 2 * i + (QUART * q + s)
                                if kind == "f1":
                                    if (q, s) == (0, 0):
                                        dve.wait_ge(rs_ready, b + 1)
                                    dve.wait_ge(relu_ready, f + 3)
                                    dve.wait_ge(ahi_ready, f + 1)
                                    dve.tensor_tensor(tb[s][:], ta[s][:], rs[:], ALU.mult).then_inc(t_ready, 1)
                                    dve.wait_ge(t_ready, f + 1)
                                    dve.wait_ge(alo_ready, f + 2)
                                    dve.tensor_tensor(tc[s][:], tb[s][:], tb[s][:],
                                                      ALU.mult).then_inc(tsq_ready, 1)
                                    dve.wait_ge(tsq_ready, f + 2)
                                    dve.wait_ge(ahi_ready, f + 2)
                                    dve.tensor_tensor(a_lo[q % 2][:, n], tc[s][:], f32(a_hi[q % 2][:, n]),
                                                      ALU.subtract).then_inc(alo_ready, 1)
                                else:
                                    dve.wait_ge(summed, b * TAIL_T + 2 * i + (j0 + s + 3))
                                    if q:
                                        dve.wait_ge(f2_added, f - 5)
                                    dve.tensor_tensor(x1[:, n], ps[:, F2_BANK + s], x1[:, n],
                                                      ALU.add).then_inc(f2_added, 1)
                        if more_blocks and (kind, q) in PREFETCH:
                            for i in range(PAIRS):
                                pair(i)
                                if PREFETCH[kind, q] + i < N_MIX:
                                    c = PREFETCH[kind, q] + i
                                    mix_low(b + 1, c, g_raw[c % 2][:])
                        else:
                            with dve.Fori(0, PAIRS) as i:
                                pair(i)

                all_blocks(dve, one_block)

            @block.tensor
            def _(pe):
                pe.sem_inc(summed, 2)

                def weights(b, j):
                    pe.wait_ge(whi_ready, b * TAIL_T + j + 1)
                    pe.wait_ge(wlo_ready, b * TAIL_T + j + 3)

                def product(bank, s, x_hi, x_lo, k0=0, n=KD, each=None, done=True):
                    for k in range(n):
                        if each:
                            each(k)
                        mm = three_products(pe, ps[:, bank], w_hi[s][:, k0 + k], w_lo[s][:, k0 + k],
                                            x_hi[:, k], x_lo[:, k], k == 0, k == n - 1)
                    if done:
                        mm.then_inc(summed, 1)

                def mean_square(b):
                    pe.wait_ge(const_in, 32)
                    pe.wait_ge(sq_step, (b + 1) * (KD + 1) + 2)
                    pe.matmul(ps[:, MEAN], ones[:], rs[:], start=True, stop=True).then_inc(mean_done, 1)

                def one_block(b, more_blocks):
                    with pe.Fori(0, KD // 2) as i:
                        for s in range(2):
                            pe.wait_ge(mixlo_ready, b * N_MIX + 2)
                            pe.wait_ge(f2_added, b * (4 * KD) + 2)
                            m = b * KD + 2 * i + s
                            pe.wait_ge(merge_step, m * 3 + 3)
                            weights(b, 4 * i + 2 * s)
                            product(G_BANK + 2 * s, 0, y_hi, y_lo, 0, 4, done=False)
                            product(G_BANK + 2 * s + 1, 0, y_hi, y_lo, 4, 4)
                            pe.wait_ge(mixlo_ready, b * N_MIX + N_MIX)
                            weights(b, 4 * i + (2 * s + 1))
                            product(A_BANK + s, 1, h_hi, h_lo)

                    def out_pair(i, first=False):
                        for s in range(2):
                            weights(b, 2 * i + (S2 + s))
                            pe.wait_ge(x1_ready, b * KD + 2 * i + (s + 1))
                            product(O_BANK + s, s, a_hi[0], a_lo[0], each=(
                                lambda k: pe.wait_ge(mlo_ready, b * KD + k + 2))
                                if first and s == 0 else None)

                    out_pair(0, True)
                    with pe.Fori(1, KD // 2) as i:
                        out_pair(i)

                    for kind, q, j0 in SECT:
                        def pair(i, first=False):
                            for s in range(2):
                                n = b * (4 * QUART) + 2 * i + (QUART * q + s)
                                weights(b, 2 * i + (j0 + s))
                                if kind == "f1":
                                    pe.wait_ge(relu_ready, n + 1)
                                    product(F1_BANK + s, s, h_hi, h_lo, each=(
                                        lambda k: pe.wait_ge(hlo_ready, b * KD + k + 1))
                                        if first and s == 0 else None)
                                    if first and s == 0 and q == 0:
                                        mean_square(b)
                                else:
                                    pe.wait_ge(f2_added, n + 1)
                                    product(F2_BANK + s, s, a_hi[q % 2], a_lo[q % 2], each=(
                                        lambda k: pe.wait_ge(alo_ready, b * (4 * QUART) + QUART * q + k + 3))
                                        if first and s == 0 else None)
                        pair(0, True)
                        with pe.Fori(1, PAIRS) as i:
                            pair(i)

                all_blocks(pe, one_block)


def encoder_layer(nc, ap, y_t):
    scratch = lambda name, shape: nc.dram_tensor(name, shape, F32).ap()
    proj = scratch("proj_scratch", [PROJ_T, P, TOK])
    roped = scratch("roped_scratch", [NQ + NKV, 2, HEAD, TOK])
    mix = scratch("mix_scratch", [12, P, TOK])
    with ExitStack() as sems:
        st = Stores(nc, sems)
        with ExitStack() as ctx:
            sh = Shared(nc, ctx)
            project(nc, st, sh, ap["x_t"], ap["w_in_t"], ap["norm_mix_t"], ap["model_mean"], ap["qk_gain"],
                    ap["head_mean"], ap["rope"], ap["lam"], ap["log_step"], ap["ssm_b"], ap["ssm_c"],
                    ap["ssm_d_t"], ap["direction"], ap["identity"], proj, roped)
            gates_and_states(nc, st, sh, ap["w_in_t"], proj, mix)
        attention(nc, st, roped, proj, ap["identity"],
                  mix[0:8].rearrange("t p n -> (t p) n").rearrange("(h d) n -> h d n", d=HEAD))
        tail(nc, st, mix, proj, ap["x_t"], ap["w_tail_t"], ap["norm_mlp_t"], ap["model_mean"], y_t)



def tiles(w):
    k, m = w.shape
    return w.reshape(k // P, P, m // P, P).transpose(2, 1, 0, 3)


def tail_stream(w_attn, w_glu_a, w_glu_b, w_out, w_ff1, w_ff2):
    attn, f1 = tiles(w_attn), tiles(w_ff1)
    glu = np.concatenate([tiles(w_glu_a), tiles(w_glu_b)], 2)
    f2 = tiles(w_ff2).reshape(KD, P, D_FF // P // QUART, QUART, P).transpose(2, 0, 1, 3, 4)
    parts = [np.stack([glu, attn], 1).reshape(2 * KD, P, KD, P), tiles(w_out)]
    parts += [f1[QUART * q:QUART * (q + 1)] if kind == "f1" else f2[q] for kind, q in MLP_ORDER]
    return np.ascontiguousarray(np.concatenate(parts + [glu[:1], attn[:1]], 0))


def token_order(length):
    return np.arange(length).reshape(length // CHUNK, CHUNK).T.reshape(-1)


def rope_tables():
    axis = HEAD // 2
    inv = (ROPE_THETA ** (-np.arange(0, axis, 2, dtype=np.float32) / np.float32(axis))).astype(np.float32)
    out = []
    for length in (LEN_A, LEN_B):
        t = token_order(length)
        ang = np.concatenate([(t // GRID_W)[None, :].astype(np.float32) * inv[:, None],
                              (t % GRID_W)[None, :].astype(np.float32) * inv[:, None]], 0)
        cos, sin = np.repeat(np.cos(ang), 2, 0), np.repeat(np.sin(ang), 2, 0)
        sin[0::2] *= -1
        out.append(np.tile(np.stack([cos, sin], 1), (2, 1, 1)))
    return np.ascontiguousarray(np.concatenate(out, 2).astype(np.float32))


def layouts(v):
    lay = np.ascontiguousarray
    g = lambda name: np.asarray(v[name])[0]
    x = np.concatenate([g("x_prompt")[token_order(LEN_A)], g("x_sample")[token_order(LEN_B)]], 0)
    eye = np.eye(P, dtype=np.float32)
    two = lambda a, b: np.stack([g(a), g(b)])
    return {
        "x_t": lay(x.reshape(NBLK, BLK, KD, P).transpose(0, 3, 2, 1)),
        "w_in_t": lay(tiles(g("w_in"))),
        "norm_mix_t": lay(g("norm_mix").reshape(KD, P).T),
        "norm_mlp_t": lay(g("norm_mlp").reshape(KD, P).T),
        "qk_gain": lay(np.tile(np.stack([g("q_norm"), g("k_norm")], 1), (2, 1))),
        "w_tail_t": tail_stream(g("w_attn_proj"), g("w_glu_a"), g("w_glu_b"), g("w_out"),
                                g("w_ff1"), g("w_ff2")),
        "lam": lay(two("ssm_lambda_re", "ssm_lambda_im").transpose(1, 3, 0, 2).reshape(P, 2, GROUPS)),
        "log_step": lay(np.repeat(g("ssm_log_step"), STATE, axis=0)),
        "ssm_b": lay(two("ssm_b_re", "ssm_b_im").transpose(1, 3, 0, 2, 4).reshape(P, 2, GROUPS, GC)),
        "ssm_c": lay(two("ssm_c_re", "ssm_c_im").transpose(1, 4, 0, 2, 3).reshape(P, 2, GROUPS, GC)),
        "ssm_d_t": lay(g("ssm_d").reshape(GROUPS, GC).T),
        "model_mean": np.full((P, P), 1.0 / D_MODEL, np.float32),
        "head_mean": lay(np.kron(np.eye(2), np.full((HEAD, HEAD), 1.0 / HEAD)).astype(np.float32)),
        "rope": rope_tables(),
        "direction": lay(np.repeat(np.array([1.0, -1.0], np.float32), STATE)[:, None]),
        "identity": eye,
    }


def kernel(**inputs):
    import concourse.bacc as bacc
    from concourse.bass_utils import run_bass_kernel_spmd

    arrays = layouts(inputs)
    nc = bacc.Bacc("TRN2", target_bir_lowering=False, num_devices=1)
    ap = {n: nc.dram_tensor(n, a.shape, F32, kind="ExternalInput").ap() for n, a in arrays.items()}
    y_t = nc.dram_tensor("y_t", (NBLK, P, KD, BLK), F32, kind="ExternalOutput").ap()
    encoder_layer(nc, ap, y_t)
    result = run_bass_kernel_spmd(nc, [arrays], core_ids=[0])
    y = np.asarray(result.results[0]["y_t"]).transpose(0, 3, 2, 1).reshape(TOK, D_MODEL)
    out = []
    for start, length in ((0, LEN_A), (LEN_A, LEN_B)):
        part = y[start:start + length].reshape(CHUNK, length // CHUNK, D_MODEL).transpose(1, 0, 2)
        out.append(np.ascontiguousarray(part.reshape(1, length, D_MODEL)))
    return tuple(out)
```
